# Optimizing a Trainium2 kernel written in Bass

```python
import jax
import jax.numpy as jnp
from jax import lax
import numpy as np
import math
import jax, jax.numpy as jnp

D_MODEL = 1024
BATCH = 1
SEQ = 256
DEPTH = 1

HEAD_DIM = 64
N_HEADS = 4
BRANCH_W = N_HEADS * HEAD_DIM
N_BRANCH = 4
Q_BLOCK = 128
CMP_BLOCK = 32
SEL_BLOCK = 64
SEL_TOPK = 16
NSA_WINDOW = 512
SWA_WINDOW = 128
SWA_KV_HEADS = 2
RET_CHUNK = 128
RMS_EPS = 1e-6
LN_EPS = 1e-5
NEG_INF = -1e30
TINY = 1e-30
FORCED_SCORE = 1e4

IN_WIDTHS = (
    BRANCH_W, 6 * HEAD_DIM, 3 * N_HEADS, BRANCH_W,
    BRANCH_W, SWA_KV_HEADS * HEAD_DIM, SWA_KV_HEADS * HEAD_DIM, BRANCH_W,
    BRANCH_W, BRANCH_W, BRANCH_W, BRANCH_W,
    BRANCH_W, BRANCH_W, BRANCH_W, BRANCH_W,
)
IN_W = sum(IN_WIDTHS)
IN_OFFSETS = tuple(int(v) for v in np.cumsum(IN_WIDTHS)[:-1])


def alibi_slopes(n):
    return jnp.asarray(2.0 ** (-8.0 * (np.arange(n) + 1) / n), dtype=jnp.float32)

def rms_norm(x, g):
    xf = x.astype(jnp.float32)
    y = xf * lax.rsqrt(jnp.mean(xf * xf, axis=-1, keepdims=True) + RMS_EPS)
    return (y * g.astype(jnp.float32)).astype(x.dtype)

def masked_softmax(s, mask, sink=None):
    s = jnp.where(mask, s, NEG_INF)
    m = jnp.max(s, axis=-1, keepdims=True)
    if sink is not None:
        m = jnp.maximum(m, sink)
    e = jnp.where(mask, jnp.exp(s - m), 0.0)
    den = jnp.sum(e, axis=-1, keepdims=True)
    if sink is not None:
        den = den + jnp.exp(sink - m)
    return e / jnp.maximum(den, TINY)

def band_windows(k, n_prev):
    B, S = k.shape[:2]
    nblk = S // Q_BLOCK
    pad = [(0, 0), (n_prev * Q_BLOCK, 0)] + [(0, 0)] * (k.ndim - 2)
    kp = jnp.pad(k, pad).reshape(B, nblk + n_prev, Q_BLOCK, *k.shape[2:])
    return jnp.concatenate([kp[:, j:j + nblk] for j in range(n_prev + 1)], axis=2)

def banded_attention(q, k, v, window, slopes, sink=None):
    B, S, H, Dh = q.shape
    Hkv = k.shape[2]
    G = H // Hkv
    nblk = S // Q_BLOCK
    n_prev = -(-(window - 1) // Q_BLOCK)
    K = (n_prev + 1) * Q_BLOCK
    kw = band_windows(k, n_prev)
    vw = band_windows(v, n_prev)
    qb = q.reshape(B, nblk, Q_BLOCK, Hkv, G, Dh)
    s = jnp.einsum("bnqhgd,bnkhd->bnhgqk", qb, kw).astype(jnp.float32) * Dh ** -0.5
    rel = jnp.arange(Q_BLOCK)[:, None] + n_prev * Q_BLOCK - jnp.arange(K)[None, :]
    kpos = jnp.arange(nblk)[:, None] * Q_BLOCK - n_prev * Q_BLOCK + jnp.arange(K)[None, :]
    mask = ((rel >= 0) & (rel < window))[None] & (kpos >= 0)[:, None, :]
    s = s - slopes.reshape(Hkv, G, 1, 1) * rel.astype(jnp.float32)
    sk = None if sink is None else sink.astype(jnp.float32).reshape(1, 1, Hkv, G, 1, 1)
    p = masked_softmax(s, mask[None, :, None, None], sk)
    o = jnp.einsum("bnhgqk,bnkhd->bnqhgd", p.astype(v.dtype), vw)
    return o.reshape(B, S, H, Dh)

def nsa_attention(q, kv, gate_logits, pos_emb, w1, w2):
    B, S, H, Dh = q.shape
    k_cmp, v_cmp, k_sel, v_sel, k_win, v_win = jnp.split(kv, 6, axis=-1)
    slopes = alibi_slopes(H)
    scale = Dh ** -0.5
    t = jnp.arange(S)

    nc = S // CMP_BLOCK
    def compress(z, j):
        zb = z.reshape(B, nc, CMP_BLOCK, Dh) + pos_emb[j]
        return jax.nn.silu(zb.reshape(B, nc, CMP_BLOCK * Dh) @ w1[j]) @ w2[j]
    kc = compress(k_cmp, 0)
    vc = compress(v_cmp, 1)
    blk_end = jnp.arange(nc) * CMP_BLOCK + CMP_BLOCK - 1
    dist = t[:, None] - blk_end[None, :]
    s = jnp.einsum("bshd,bcd->bhsc", q, kc).astype(jnp.float32) * scale
    s = s - slopes[:, None, None] * dist.astype(jnp.float32)
    p_cmp = masked_softmax(s, dist >= 0)
    o_cmp = jnp.einsum("bhsc,bcd->bshd", p_cmp.astype(vc.dtype), vc)

    ns = S // SEL_BLOCK
    ratio = SEL_BLOCK // CMP_BLOCK
    imp = p_cmp.sum(axis=1).reshape(B, S, ns, ratio).sum(axis=-1)
    blk = jnp.arange(ns)[None, :]
    cur = (t // SEL_BLOCK)[:, None]
    future = blk * SEL_BLOCK > t[:, None]
    forced = (blk == 0) | (blk == cur) | (blk == cur - 1)
    imp = jnp.where(forced, FORCED_SCORE, jnp.where(future, -1.0, imp))
    topk = min(SEL_TOPK, ns)
    _, idx = lax.top_k(imp, topk)

    kb = k_sel.reshape(B, ns, SEL_BLOCK, Dh)
    vb = v_sel.reshape(B, ns, SEL_BLOCK, Dh)
    nq = S // Q_BLOCK
    qs = q.reshape(B, nq, Q_BLOCK, H, Dh).swapaxes(0, 1)
    ids = idx.reshape(B, nq, Q_BLOCK, topk).swapaxes(0, 1)
    qpos = t.reshape(nq, Q_BLOCK)
    bidx = jnp.arange(B)[:, None, None]
    n_keys = topk * SEL_BLOCK

    def sel_block(args):
        qi, ii, pi = args
        kg = kb[bidx, ii].reshape(B, Q_BLOCK, n_keys, Dh)
        vg = vb[bidx, ii].reshape(B, Q_BLOCK, n_keys, Dh)
        kpos = (ii[..., None] * SEL_BLOCK + jnp.arange(SEL_BLOCK)).reshape(B, Q_BLOCK, n_keys)
        d = pi[None, :, None] - kpos
        sc = jnp.einsum("bqhd,bqkd->bhqk", qi, kg).astype(jnp.float32) * scale
        sc = sc - slopes[:, None, None] * d[:, None].astype(jnp.float32)
        pr = masked_softmax(sc, (d >= 0)[:, None])
        return jnp.einsum("bhqk,bqkd->bqhd", pr.astype(vg.dtype), vg)

    o_sel = lax.map(sel_block, (qs, ids, qpos)).swapaxes(0, 1).reshape(B, S, H, Dh)

    o_win = banded_attention(q, k_win[:, :, None], v_win[:, :, None], NSA_WINDOW, slopes)

    g = jax.nn.sigmoid(gate_logits.astype(jnp.float32)).reshape(B, S, H, 3).astype(q.dtype)
    return g[..., 0:1] * o_cmp + g[..., 1:2] * o_sel + g[..., 2:3] * o_win

def stick_breaking_attention(q, k, v):
    B, S, H, Dh = q.shape
    nq = S // Q_BLOCK
    qs = q.reshape(B, nq, Q_BLOCK, H, Dh).swapaxes(0, 1)
    qpos = jnp.arange(S).reshape(nq, Q_BLOCK)
    kpos = jnp.arange(S)
    scale = Dh ** -0.5

    def one_block(args):
        qi, pi = args
        z = jnp.einsum("bqhd,bkhd->bhqk", qi, k).astype(jnp.float32) * scale
        mask = kpos[None, :] < pi[:, None]
        log_beta = jax.nn.log_sigmoid(z)
        log_1m = jnp.where(mask, jax.nn.log_sigmoid(-z), 0.0)
        suffix = lax.cumsum(log_1m, axis=3, reverse=True) - log_1m
        a = jnp.where(mask, jnp.exp(log_beta + suffix), 0.0)
        return jnp.einsum("bhqk,bkhd->bqhd", a.astype(v.dtype), v)

    return lax.map(one_block, (qs, qpos)).swapaxes(0, 1).reshape(B, S, H, Dh)

def retention(q, k, v):
    B, S, H, Dh = q.shape
    C = RET_CHUNK
    n = S // C
    log_g = jnp.log(1.0 - jnp.asarray(2.0 ** (-5.0 - np.arange(H)), dtype=jnp.float32))
    qc = (q.astype(jnp.float32) * Dh ** -0.5).reshape(B, n, C, H, Dh)
    kc = k.astype(jnp.float32).reshape(B, n, C, H, Dh)
    vc = v.astype(jnp.float32).reshape(B, n, C, H, Dh)
    i = jnp.arange(C)
    diff = (i[:, None] - i[None, :]).astype(jnp.float32)
    dmat = jnp.where(diff >= 0, jnp.exp(log_g[:, None, None] * jnp.maximum(diff, 0.0)), 0.0)
    s = jnp.einsum("bnihd,bnjhd->bnhij", qc, kc) * dmat
    intra = jnp.einsum("bnhij,bnjhd->bnihd", s, vc)
    zeta = jnp.exp(log_g[:, None] * (C - 1 - i)[None, :].astype(jnp.float32))
    u = jnp.einsum("bnjhd,bnjhe,hj->nbhde", kc, vc, zeta)
    g_chunk = jnp.exp(log_g * C)[None, :, None, None]

    def step(r, u_n):
        return r * g_chunk + u_n, r

    _, r_prev = lax.scan(step, jnp.zeros((B, H, Dh, Dh), jnp.float32), u)
    xi = jnp.exp(log_g[:, None] * (i + 1)[None, :].astype(jnp.float32))
    cross = jnp.einsum("bnihd,nbhde,hi->bnihe", qc, r_prev, xi)
    o = (intra + cross).reshape(B, S, H, Dh)
    mu = jnp.mean(o, axis=-1, keepdims=True)
    var = jnp.mean((o - mu) ** 2, axis=-1, keepdims=True)
    return ((o - mu) * lax.rsqrt(var + LN_EPS)).astype(q.dtype)

def hybrid_layer(x, c, w_ada, b_ada, norm_g, w_in, cmp_pos, cmp_w1, cmp_w2, sink, w_merge, w_br, w_out):
    B, S, _ = x.shape
    mod = (jax.nn.silu(c) @ w_ada + b_ada)[:, None, :]
    shift, scale, gate = jnp.split(mod, 3, axis=-1)
    h = rms_norm(x, norm_g) * (1.0 + scale) + shift
    (a_q, a_kv, a_g, a_z, b_q, b_k, b_v, b_z,
     c_q, c_k, c_v, c_z, d_q, d_k, d_v, d_z) = jnp.split(h @ w_in, IN_OFFSETS, axis=-1)

    def heads(z):
        return z.reshape(B, S, -1, HEAD_DIM)

    y_a = nsa_attention(heads(a_q), a_kv, a_g, cmp_pos, cmp_w1, cmp_w2)
    y_b = banded_attention(heads(b_q), heads(b_k), heads(b_v), SWA_WINDOW, alibi_slopes(N_HEADS), sink)
    y_c = stick_breaking_attention(heads(c_q), heads(c_k), heads(c_v))
    y_d = retention(heads(d_q), heads(d_k), heads(d_v))

    branches = ((y_a, a_z), (y_b, b_z), (y_c, c_z), (y_d, d_z))
    merged = None
    for i, (y, z) in enumerate(branches):
        yi = y.reshape(B, S, BRANCH_W) * jax.nn.silu(z)
        term = jax.nn.sigmoid(h @ w_merge[i]) * (yi @ w_br[i])
        merged = term if merged is None else merged + term
    return x + gate * (merged @ w_out)

def first_inputs(seed: int = 0) -> dict:
    key = jax.random.key(seed)
    ks = jax.random.split(key, 14)
    D = D_MODEL
    f32 = jnp.float32

    def nrm(k, shape, fan):
        return jax.random.normal(k, shape, f32) * fan ** -0.5

    return {
        "x": jax.random.normal(ks[0], (BATCH, SEQ, D), f32),
        "c": jax.random.normal(ks[1], (BATCH, D), f32),
        "w_ada": nrm(ks[2], (DEPTH, D, 3 * D), D) * 0.5,
        "b_ada": 0.02 * jax.random.normal(ks[3], (DEPTH, 3 * D), f32),
        "norm_g": 1.0 + 0.05 * jax.random.normal(ks[4], (DEPTH, D), f32),
        "w_in": nrm(ks[5], (DEPTH, D, IN_W), D),
        "cmp_pos": 0.1 * jax.random.normal(ks[6], (DEPTH, 2, CMP_BLOCK, HEAD_DIM), f32),
        "cmp_w1": nrm(ks[7], (DEPTH, 2, CMP_BLOCK * HEAD_DIM, HEAD_DIM), CMP_BLOCK * HEAD_DIM),
        "cmp_w2": nrm(ks[8], (DEPTH, 2, HEAD_DIM, HEAD_DIM), HEAD_DIM),
        "sink": 0.5 * jax.random.normal(ks[9], (DEPTH, N_HEADS), f32),
        "w_merge": nrm(ks[10], (DEPTH, N_BRANCH, D, D), D),
        "w_br": nrm(ks[11], (DEPTH, N_BRANCH, BRANCH_W, D), BRANCH_W),
        "w_out": nrm(ks[12], (DEPTH, D, D), D),
        "final_g": 1.0 + 0.05 * jax.random.normal(ks[13], (D,), f32),
    }

def first_block(x, c, w_ada, b_ada, norm_g, w_in, cmp_pos, cmp_w1, cmp_w2, sink, w_merge, w_br, w_out, final_g):
    for l in range(DEPTH):
        x = hybrid_layer(x, c, w_ada[l], b_ada[l], norm_g[l], w_in[l], cmp_pos[l], cmp_w1[l], cmp_w2[l],
                         sink[l], w_merge[l], w_br[l], w_out[l])
    return rms_norm(x, final_g)


DEPTH_2 = 2

N_A_LAYERS = DEPTH_2 // 2
N_B_LAYERS = DEPTH_2 - N_A_LAYERS
CONV_WIDTH = 31
DIFF_HEADS = 8
DIFF_HEAD_DIM = 64
DIFF_V_DIM = 2 * DIFF_HEAD_DIM
ROT_DIM = DIFF_HEAD_DIM // 4
ROPE_THETA = 500000.0
MEM_TOKENS = 256
MEM_HEADS = 4
MEM_HEAD_DIM = D_MODEL // MEM_HEADS
FFN_HIDDEN = -(-(8 * D_MODEL) // (3 * 256)) * 256
SUBLN_EPS = 1e-5


def rms_norm_2(x, g, eps=RMS_EPS):
    xf = x.astype(jnp.float32)
    y = xf * lax.rsqrt(jnp.mean(xf * xf, axis=-1, keepdims=True) + eps)
    return (y * g.astype(jnp.float32)).astype(x.dtype)

def layer_norm(x, g, b, eps=LN_EPS):
    xf = x.astype(jnp.float32)
    mu = jnp.mean(xf, axis=-1, keepdims=True)
    xc = xf - mu
    y = xc * lax.rsqrt(jnp.mean(xc * xc, axis=-1, keepdims=True) + eps)
    return (y * g.astype(jnp.float32) + b.astype(jnp.float32)).astype(x.dtype)

def rope_tables(positions):
    inv_freq = ROPE_THETA ** (-jnp.arange(0, ROT_DIM, 2, dtype=jnp.float32) / ROT_DIM)
    ang = positions.astype(jnp.float32)[..., None] * inv_freq
    return jnp.cos(ang), jnp.sin(ang)

def apply_partial_rope(t, cos, sin):
    half = ROT_DIM // 2
    tf = t.astype(jnp.float32)
    r1 = tf[..., :half]
    r2 = tf[..., half:ROT_DIM]
    c = cos[:, :, None, None, :]
    s = sin[:, :, None, None, :]
    out = jnp.concatenate([r1 * c - r2 * s, r1 * s + r2 * c, tf[..., ROT_DIM:]], axis=-1)
    return out.astype(t.dtype)

def conformer_conv(h, w_pw1, b_pw1, w_dw, b_dw, ln_g, ln_b, w_pw2, b_pw2):
    u = h @ w_pw1 + b_pw1
    a, gate = jnp.split(u, 2, axis=-1)
    u = a * jax.nn.sigmoid(gate)
    u = lax.conv_general_dilated(
        u, w_dw[:, None, :].astype(u.dtype), window_strides=(1,),
        padding=((CONV_WIDTH - 1, 0),),
        dimension_numbers=("NWC", "WIO", "NWC"),
        feature_group_count=D_MODEL) + b_dw
    u = jax.nn.silu(layer_norm(u, ln_g, ln_b))
    return u @ w_pw2 + b_pw2

def shared_kv(x, kv_norm, w_k, w_v, cos, sin):
    B, S, _ = x.shape
    h = rms_norm_2(x, kv_norm)
    k = apply_partial_rope((h @ w_k).reshape(B, S, DIFF_HEADS, 2, DIFF_HEAD_DIM), cos, sin)
    v = (h @ w_v).reshape(B, S, DIFF_HEADS, DIFF_V_DIM)
    return k, v

def diff_attention(h, k, v, cos, sin, w_q, lq1, lk1, lq2, lk2, subln_g, w_o, lambda_init):
    B, S, _ = h.shape
    q = apply_partial_rope((h @ w_q).reshape(B, S, DIFF_HEADS, 2, DIFF_HEAD_DIM), cos, sin)
    lam = (jnp.exp(jnp.sum(lq1.astype(jnp.float32) * lk1.astype(jnp.float32)))
           - jnp.exp(jnp.sum(lq2.astype(jnp.float32) * lk2.astype(jnp.float32)))
           + lambda_init)
    n_blocks = S // Q_BLOCK
    q_blocks = q.reshape(B, n_blocks, Q_BLOCK, DIFF_HEADS, 2, DIFF_HEAD_DIM).swapaxes(0, 1)
    k_pos = jnp.arange(S)
    scale = DIFF_HEAD_DIM ** -0.5

    def one_block(args):
        blk, qb = args
        q_pos = blk * Q_BLOCK + jnp.arange(Q_BLOCK)
        s = jnp.einsum('bqhcd,bkhcd->bhcqk', qb, k,
                       preferred_element_type=jnp.float32) * scale
        mask = k_pos[None, :] <= q_pos[:, None]
        p = jax.nn.softmax(jnp.where(mask, s, -jnp.inf), axis=-1)
        a = p[:, :, 0] - lam * p[:, :, 1]
        return jnp.einsum('bhqk,bkhe->bqhe', a.astype(v.dtype), v)

    o = lax.map(one_block, (jnp.arange(n_blocks), q_blocks))
    o = o.swapaxes(0, 1).reshape(B, S, DIFF_HEADS, DIFF_V_DIM)
    o = rms_norm_2(o, subln_g, SUBLN_EPS) * (1.0 - lambda_init)
    return o.reshape(B, S, DIFF_HEADS * DIFF_V_DIM) @ w_o

def memory_cross_attention(h, mem, w_q, w_k, w_v, w_o):
    B, S, _ = h.shape
    M = mem.shape[1]
    q = (h @ w_q).reshape(B, S, MEM_HEADS, MEM_HEAD_DIM)
    k = (mem @ w_k).reshape(B, M, MEM_HEADS, MEM_HEAD_DIM)
    v = (mem @ w_v).reshape(B, M, MEM_HEADS, MEM_HEAD_DIM)
    s = jnp.einsum('bshd,bmhd->bhsm', q, k, preferred_element_type=jnp.float32) * MEM_HEAD_DIM ** -0.5
    p = jax.nn.softmax(s, axis=-1)
    o = jnp.einsum('bhsm,bmhd->bshd', p.astype(v.dtype), v).reshape(B, S, D_MODEL)
    return o @ w_o

def swiglu(h, w_gate, w_up, w_down):
    return (jax.nn.silu(h @ w_gate) * (h @ w_up)) @ w_down

def second_inputs(seed: int = 0) -> dict:
    key = jax.random.key(seed)
    ks = iter(jax.random.split(key, 40))
    f32 = jnp.float32

    def w(shape, fan_in):
        return jax.random.normal(next(ks), shape, f32) * (fan_in ** -0.5)

    def gain(shape):
        return 1.0 + 0.02 * jax.random.normal(next(ks), shape, f32)

    def small(shape, scale=0.01):
        return scale * jax.random.normal(next(ks), shape, f32)

    D, F, A, Bn = D_MODEL, FFN_HIDDEN, N_A_LAYERS, N_B_LAYERS
    QK = DIFF_HEADS * 2 * DIFF_HEAD_DIM
    VW = DIFF_HEADS * DIFF_V_DIM
    x = jax.random.normal(next(ks), (BATCH, SEQ, D), f32)
    mem = jax.random.normal(next(ks), (BATCH, MEM_TOKENS, D), f32)
    offset = jax.random.randint(next(ks), (BATCH, 1), 0, 1024, dtype=jnp.int32)
    positions = (offset + jnp.arange(SEQ, dtype=jnp.int32)[None, :]).astype(jnp.int32)
    return {
        "x": x, "mem": mem, "positions": positions,
        "norm_mix": gain((DEPTH_2, D)), "norm_mem": gain((DEPTH_2, D)),
        "norm_ffn": gain((DEPTH_2, D)), "norm_final": gain((D,)),
        "conv_w_pw1": w((A, D, 2 * D), D), "conv_b_pw1": small((A, 2 * D)),
        "conv_w_dw": w((A, CONV_WIDTH, D), CONV_WIDTH), "conv_b_dw": small((A, D)),
        "conv_ln_g": gain((A, D)), "conv_ln_b": small((A, D)),
        "conv_w_pw2": w((A, D, D), D), "conv_b_pw2": small((A, D)),
        "kv_norm": gain((D,)), "w_k_shared": w((D, QK), D), "w_v_shared": w((D, VW), D),
        "diff_w_q": w((Bn, D, QK), D),
        "diff_lambda_q1": small((Bn, DIFF_HEAD_DIM), 0.1), "diff_lambda_k1": small((Bn, DIFF_HEAD_DIM), 0.1),
        "diff_lambda_q2": small((Bn, DIFF_HEAD_DIM), 0.1), "diff_lambda_k2": small((Bn, DIFF_HEAD_DIM), 0.1),
        "diff_subln_g": gain((Bn, DIFF_V_DIM)), "diff_w_o": w((Bn, VW, D), VW),
        "mem_w_q": w((DEPTH_2, D, D), D), "mem_w_k": w((DEPTH_2, D, D), D),
        "mem_w_v": w((DEPTH_2, D, D), D), "mem_w_o": w((DEPTH_2, D, D), D),
        "ffn_w_gate": w((DEPTH_2, D, F), D), "ffn_w_up": w((DEPTH_2, D, F), D),
        "ffn_w_down": w((DEPTH_2, F, D), F),
    }

def second_block(x, mem, positions, norm_mix, norm_mem, norm_ffn, norm_final,
              conv_w_pw1, conv_b_pw1, conv_w_dw, conv_b_dw, conv_ln_g, conv_ln_b,
              conv_w_pw2, conv_b_pw2, kv_norm, w_k_shared, w_v_shared,
              diff_w_q, diff_lambda_q1, diff_lambda_k1, diff_lambda_q2, diff_lambda_k2,
              diff_subln_g, diff_w_o, mem_w_q, mem_w_k, mem_w_v, mem_w_o,
              ffn_w_gate, ffn_w_up, ffn_w_down):
    cos, sin = rope_tables(positions)
    k_sh = None
    v_sh = None
    for i in range(DEPTH_2):
        if i < N_A_LAYERS:
            a = i
            h = rms_norm_2(x, norm_mix[i])
            x = x + conformer_conv(h, conv_w_pw1[a], conv_b_pw1[a], conv_w_dw[a], conv_b_dw[a],
                                   conv_ln_g[a], conv_ln_b[a], conv_w_pw2[a], conv_b_pw2[a])
        else:
            b = i - N_A_LAYERS
            if b == 0:
                k_sh, v_sh = shared_kv(x, kv_norm, w_k_shared, w_v_shared, cos, sin)
            lambda_init = 0.8 - 0.6 * math.exp(-0.3 * i)
            h = rms_norm_2(x, norm_mix[i])
            x = x + diff_attention(h, k_sh, v_sh, cos, sin, diff_w_q[b],
                                   diff_lambda_q1[b], diff_lambda_k1[b],
                                   diff_lambda_q2[b], diff_lambda_k2[b],
                                   diff_subln_g[b], diff_w_o[b], lambda_init)
        x = x + memory_cross_attention(rms_norm_2(x, norm_mem[i]), mem,
                                       mem_w_q[i], mem_w_k[i], mem_w_v[i], mem_w_o[i])
        x = x + swiglu(rms_norm_2(x, norm_ffn[i]), ffn_w_gate[i], ffn_w_up[i], ffn_w_down[i])
    return rms_norm_2(x, norm_final)


def setup_inputs(seed=0):
    out = dict(first_inputs(seed))
    for name, value in second_inputs(seed + 1).items():
        if name != "x":
            out[name + "_2"] = value
    return out


def reference(
    x, c, w_ada, b_ada, norm_g, w_in, cmp_pos, cmp_w1, cmp_w2, sink, w_merge, w_br, w_out,
    final_g, mem_2, positions_2, norm_mix_2, norm_mem_2, norm_ffn_2, norm_final_2, conv_w_pw1_2,
    conv_b_pw1_2, conv_w_dw_2, conv_b_dw_2, conv_ln_g_2, conv_ln_b_2, conv_w_pw2_2,
    conv_b_pw2_2, kv_norm_2, w_k_shared_2, w_v_shared_2, diff_w_q_2, diff_lambda_q1_2,
    diff_lambda_k1_2, diff_lambda_q2_2, diff_lambda_k2_2, diff_subln_g_2, diff_w_o_2, mem_w_q_2,
    mem_w_k_2, mem_w_v_2, mem_w_o_2, ffn_w_gate_2, ffn_w_up_2, ffn_w_down_2,
):
    x = first_block(
        x, c, w_ada, b_ada, norm_g, w_in, cmp_pos, cmp_w1, cmp_w2, sink, w_merge, w_br, w_out,
        final_g,
    )
    return second_block(
        x, mem_2, positions_2, norm_mix_2, norm_mem_2, norm_ffn_2, norm_final_2, conv_w_pw1_2,
        conv_b_pw1_2, conv_w_dw_2, conv_b_dw_2, conv_ln_g_2, conv_ln_b_2, conv_w_pw2_2,
        conv_b_pw2_2, kv_norm_2, w_k_shared_2, w_v_shared_2, diff_w_q_2, diff_lambda_q1_2,
        diff_lambda_k1_2, diff_lambda_q2_2, diff_lambda_k2_2, diff_subln_g_2, diff_w_o_2,
        mem_w_q_2, mem_w_k_2, mem_w_v_2, mem_w_o_2, ffn_w_gate_2, ffn_w_up_2, ffn_w_down_2,
    )


_drawn_inputs = setup_inputs


def setup_inputs(seed=0):
    import zlib

    import numpy as np

    out = dict(_drawn_inputs(seed))
    spreads = {}
    factors = {'b_ada': 3.063,
     'norm_g': 3.098,
     'cmp_pos': 8.0,
     'sink': 8.0,
     'norm_mix_2': 3.468,
     'norm_mem_2': 8.0,
     'norm_ffn_2': 3.117,
     'norm_final_2': 2.963,
     'conv_b_pw1_2': 5.93,
     'conv_ln_g_2': 2.907,
     'conv_ln_b_2': 5.5,
     'conv_b_pw2_2': 3.209,
     'kv_norm_2': 4.857,
     'diff_lambda_k1_2': 4.685,
     'diff_lambda_k2_2': 5.248,
     'diff_subln_g_2': 6.195}
    for name, (base, spread) in spreads.items():
        noise = np.random.default_rng([zlib.crc32(name.encode()), seed]).standard_normal(out[name].shape)
        drawn = base * np.exp(spread * noise) if base else spread * noise
        out[name] = jnp.asarray(drawn.astype(out[name].dtype))
    for name, factor in factors.items():
        out[name] = (out[name] * factor).astype(out[name].dtype)
    return out
```

```python
from contextlib import ExitStack

import numpy as np

import concourse.bass as bass
from concourse import mybir

F32 = mybir.dt.float32
F32R = mybir.dt.float32r
I32 = mybir.dt.int32
ALU = mybir.AluOpType
ACT = mybir.ActivationFunctionType
AX = mybir.AxisListType

P = 128
D = 1024
S = 256
NT = S // P
KT = D // P
HD = 64
NH = 4
BW = NH * HD
CMP = 32
NC = S // CMP
TAPS = 31
DH = 8
ROT = 16
MH = 4
MHT = D // MH // P
FF = 2816
FT = FF // P
CK, CN = 4, 512
RMS_EPS, LN_EPS = 1e-6, 1e-5
NEG = -1e30
TINY = 1e-30
LAMBDA_INIT = 0.8 - 0.6 * float(np.exp(-0.3))
TWO_PI = 2.0 * float(np.pi)

W_A_Q, W_A_KV, W_A_G, W_A_Z = 0, 256, 640, 652
W_B_Q, W_B_K, W_B_V, W_B_Z = 908, 1164, 1292, 1420
W_C_Q, W_C_K, W_C_V, W_C_Z = 1676, 1932, 2188, 2444
W_D_Q, W_D_K, W_D_V, W_D_Z = 2700, 2956, 3212, 3468

COMMON = {"ident": (0, 128), "ones": (128, 128), "causal": (256, 256), "invfreq": (512, 8), "half": (520, 8)}
COMMON_W = 528
FIRST = {"alibi": (0, 1024), "window": (1024, 1024), "decay": (2048, 1024), "strict": (3072, 384),
         "after": (3456, 128), "cmp_bias": (3584, 64), "cmp_mask": (3648, 64), "block": (3712, 256)}
FIRST_W = 3968


def constants():
    q, j = np.arange(P)[:, None], np.arange(2 * P)[None, :]
    rel = q + P - j
    slopes = 2.0 ** (-8.0 * (np.arange(NH) + 1) / NH)
    common = np.zeros((P, COMMON_W), np.float32)
    common[:, 0:128] = np.eye(P)
    common[:, 128:256] = 1.0
    common[:, 256:512] = np.where(rel >= 0, 0.0, NEG)
    common[:, 512:520] = (500000.0 ** (-np.arange(0, ROT, 2) / ROT)).astype(np.float32)
    common[:, 520:528] = -0.5
    first = np.zeros((P, FIRST_W), np.float32)
    k, i = np.arange(P)[:, None], np.arange(2 * P)[None, :]
    gamma = 1.0 - 2.0 ** (-5.0 - np.arange(NH))
    for h in range(NH):
        bias = -slopes[h] * rel
        first[:, 256 * h:256 * h + 256] = np.where(rel >= 0, bias, NEG)
        first[:, 1024 + 256 * h:1280 + 256 * h] = np.where((rel >= 0) & (rel < 128), bias, NEG)
        first[:, 2048 + 256 * h:2304 + 256 * h] = np.where(i >= k, gamma[h] ** np.maximum(i - k, 0), 0.0) * HD ** -0.5
    first[:, 3072:3328] = i > k
    first[:, 3328:3456] = i[:, :P] > k
    first[:, 3456:3584] = k > i[:, :P]
    t = np.arange(P)[:, None, None, None] + P * np.arange(NT)[None, :, None, None]
    dist = t - (np.arange(NC) * CMP + CMP - 1)[None, None, None, :] + np.zeros((1, 1, NH, 1))
    first[:, 3584:3648] = np.where(dist >= 0, -slopes[None, None, :, None] * dist, NEG).reshape(P, -1)
    first[:, 3648:3712] = (dist >= 0).reshape(P, -1)
    rows = np.arange(NH * NC)[:, None] // NC
    first[:NH * NC, 3712:3968] = rows == (np.arange(BW)[None, :] // HD)
    return common, first


class Mark:
    def __init__(self, sem, value):
        self.sem, self.value = sem, value


class Lane:
    def __init__(self, eng, sem):
        self.eng, self.sem, self.count, self.met, self.last = eng, sem, 0, {}, None

    def wait(self, *marks):
        for m in marks:
            if m is not None and self.met.get(m.sem.name, 0) < m.value:
                self.eng.wait_ge(m.sem, m.value)
                self.met[m.sem.name] = m.value

    def after(self, *marks):
        self.wait(self.last, *marks)
        return self.eng

    def beside(self, *marks):
        self.wait(*marks)
        return self.eng

    def done(self, instruction):
        instruction.then_inc(self.sem, 1)
        self.count += 1
        self.last = Mark(self.sem, self.count)
        return self.last


class Slot:
    def __init__(self, t):
        self.t, self.marks, self.busy = t, (), False

    @property
    def free(self):
        return self.marks

    @free.setter
    def free(self, marks):
        self.marks, self.busy = marks, False


class Ring:
    def __init__(self, tensors):
        self.slots, self.at = [Slot(t) for t in tensors], 0

    def take(self):
        self.at += 1
        slot = self.slots[(self.at - 1) % len(self.slots)]
        assert not slot.busy
        slot.busy = True
        return slot


class Loads:
    def __init__(self, lane, sem):
        self.lane, self.sem, self.sent, self.own = lane, sem, {}, {}

    def start(self, name, dst, src, *marks):
        if name not in self.own:
            self.own[name], self.sent[name] = self.sem("load_" + name), 0
        self.lane.wait(*marks)
        self.lane.eng.dma_start(dst, src).then_inc(self.own[name], 16)
        self.sent[name] += 16
        return Mark(self.own[name], self.sent[name])


class Weights:
    N_RAW, N_SPLIT = 4, 3

    def __init__(self, k, plan):
        self.k, self.plan = k, plan
        self.raw = [Slot(k.sb(f"w_raw{i}", [P, CK * CN])) for i in range(self.N_RAW)]
        self.high = [k.sb(f"w_high{i}", [P, CK * CN], F32R) for i in range(self.N_SPLIT)]
        self.low = [k.sb(f"w_low{i}", [P, CK * CN], F32R) for i in range(self.N_SPLIT)]
        self.read = [None] * self.N_SPLIT
        self.ready = {}
        self.loaded = {}
        self.used = 0
        for i in range(self.N_RAW):
            self.load(i)
        for i in range(self.N_SPLIT):
            self.split(i)

    def view(self, t, i):
        pieces, nk = self.plan[i]
        w = sum(n for _, n in pieces)
        return t[:, 0:nk * w].rearrange("p (k n) -> p k n", k=nk)

    def load(self, i):
        if i >= len(self.plan):
            return
        slot, at = self.raw[i % self.N_RAW], 0
        pieces, nk = self.plan[i]
        for src, n in pieces:
            self.loaded[i] = self.k.stream.start(f"w{i % self.N_RAW}", self.view(slot.t, i)[:, :, at:at + n], src, *slot.free)
            at += n

    def split(self, i):
        if i >= len(self.plan):
            return
        k, slot, j = self.k, self.raw[i % self.N_RAW], i % self.N_SPLIT
        raw, high, low = self.view(slot.t, i), self.view(self.high[j], i), self.view(self.low[j], i)
        a = k.act.done(k.act.beside(self.loaded[i], self.read[j]).activation(high, raw, ACT.Copy))
        v = k.vec.done(k.vec.beside(a, self.loaded[i], self.read[j]).tensor_tensor(low, raw, high.bitcast(F32), ALU.subtract))
        self.ready[i] = v
        slot.free = (v,)
        self.load(i + self.N_RAW)

    def take(self):
        i = self.used
        self.used += 1
        return self.view(self.high[i % self.N_SPLIT], i), self.view(self.low[i % self.N_SPLIT], i), self.ready[i]

    def give(self, mark):
        i = self.used - 1
        self.read[i % self.N_SPLIT] = mark
        self.split(i + self.N_SPLIT)


class Operand:
    def __init__(self, high, low, ready=()):
        self.high, self.low, self.ready, self.free = high, low, ready, ()


class Kernel:

    def __init__(self, nc, ctx, w):
        self.nc, self.ctx, self.phase, self.w = nc, ctx, ctx, w

        def lane(name, eng):
            return Lane(eng, self.sem(name))

        self.pe, self.vec = lane("pe_done", nc.tensor), lane("vec_done", nc.vector)
        self.act, self.pool = lane("act_done", nc.scalar), lane("pool_done", nc.gpsimd)
        self.stream = Loads(lane("sp_done", nc.sync), self.sem)
        self.side = Loads(self.pool, self.sem)

        def bank(name):
            return ctx.enter_context(nc.psum_tensor(name, [P, 512], F32))

        self.product = Ring([bank(f"product{i}") for i in range(4)])
        self.small = Ring([bank(f"small{i}") for i in range(4)])
        self.stats = self.sb("stats", [P, 768])
        self.stat_at = 0

    def sem(self, name):
        return self.ctx.enter_context(self.nc.semaphore(name))

    def sb(self, name, shape, dt=F32):
        return self.phase.enter_context(self.nc.sbuf_tensor(name, shape, dt))

    def stat(self, n):
        self.stat_at += n
        assert self.stat_at <= 768, self.stat_at
        return self.stats[:, self.stat_at - n:self.stat_at]

    def pair(self, name, tiles, n=S):
        return tuple(self.sb(f"{name}_{part}", [P, tiles, n], F32R)[:, :, :] for part in ("high", "low"))

    def load_gain(self, name, layer):
        v = self.w[name] if layer is None else self.w[name][layer]
        return self.row("gain", self.G[0].t[:, :], v, self.vec.last)

    def ring(self, name, n, shape):
        return Ring([self.sb(f"{name}{i}", shape) for i in range(n)])

    def everyone(self):
        lanes = [self.pe, self.vec, self.act, self.pool]
        marks = [l.last for l in lanes]
        for l in lanes + [self.stream.lane]:
            l.wait(*marks)


    def block(self, x, tiles, items, evacuate):
        pe, n_banks = self.pe, 1 + max(i[0] for i in items)
        banks = [self.product.take() for _ in range(n_banks)]
        started = set()
        for first in range(0, tiles, CK):
            high, low, ready = self.weights.take()
            last_chunk = first + CK >= tiles
            pe.wait(ready, *x.ready)
            if first == 0:
                for b in banks:
                    pe.wait(*b.free)
            for b, off, t, col, w in items:
                for j, kt in enumerate(range(first, min(first + CK, tiles))):
                    for xs, ws in ((x.low, high), (x.high, low), (x.high, high)):
                        if t is None:
                            a, r, n = ws[:, j, col:col + P], xs[:, kt, :], S
                        else:
                            a, r, n = xs[:, kt, t * P:(t + 1) * P], ws[:, j, col:col + w], w
                        mm = self.nc.tensor.matmul(banks[b].t[:, off:off + n], a, r, start=b not in started,
                                                   stop=True, skip_group_check=True)
                        started.add(b)
            m = pe.done(mm)
            if last_chunk:
                x.free = (m,)
                evacuate(banks, m)
            self.weights.give(m)
            yield

    def columns(self, x, tiles, evacuate, w=CN):
        def both(banks, m):
            for t in range(NT):
                evacuate(t, banks[t], m)
        return self.block(x, tiles, [(t, 0, t, 0, w) for t in range(NT)], both)

    def split_operand(self, src, mark, high, low):
        a = self.act.done(self.act.after(mark).activation(high, src, ACT.Copy))
        return self.vec.done(self.vec.after(mark, a).tensor_tensor(low, src, high.bitcast(F32), ALU.subtract))

    def transposed(self, src, cols, x, tile0, t, mark, scale=None):
        for g in range(0, len(cols), 4):
            part = cols[g:g + 4]
            bank = self.small.take()
            self.pe.wait(mark, *bank.free)
            for i, c in enumerate(part):
                tr = self.nc.tensor.transpose(bank.t[:, i * P:(i + 1) * P], src[:, c:c + P], self.ident)
            m = self.pe.done(tr)
            at = slice(tile0 + g, tile0 + g + len(part))
            hi, lo = x.high[:, at, t * P:(t + 1) * P], x.low[:, at, t * P:(t + 1) * P]
            ps = bank.t[:, 0:P * len(part)].rearrange("p (k n) -> p k n", n=P)
            self.act.wait(*x.free)
            self.vec.wait(*x.free)
            if scale is None:
                v = self.split_operand(ps, m, hi, lo)
            else:
                a = self.act.done(self.act.after(m).activation(hi, ps, ACT.Copy, scale=scale))
                v = self.vec.done(self.vec.after(m, a).scalar_tensor_tensor(lo, ps, scale, hi.bitcast(F32), ALU.mult, ALU.subtract))
            bank.free = (v,)
        x.ready = (v,)
        return v

    def row(self, name, dst, vector, *marks):
        return self.side.start(name, dst, vector.rearrange("(a n) -> a n", a=1).broadcast_to((P, vector.shape[0])), *marks)

    def inverse_root(self, sums, width, eps, mark, scale=1.0):
        n = sums.shape[1]
        mean, root = self.stat(n), self.stat(n)
        p = self.pool
        m = p.done(p.after(mark).tensor_scalar(mean, sums, 1.0 / width, eps, ALU.mult, ALU.add))
        m = p.done(p.after(m).tensor_tensor(root, mean, self.half[:, 0:n], ALU.pow))
        if scale != 1.0:
            m = p.done(p.after(m).tensor_scalar(root, root, scale, None, ALU.mult))
        return root, m

    def normed(self, x_marks, gain, gain_mark, out, shift=None):
        marks = []
        for t in range(NT):
            sums = self.stat(1)
            a = self.act.done(self.act.after(*x_marks).activation(self.HN[:, t, :], self.X[:, t, :], ACT.Square, accum_out=sums))
            r, m = self.inverse_root(sums, D, RMS_EPS, a)
            v = self.vec.done(self.vec.after(m, a, gain_mark).scalar_tensor_tensor(out[:, t, :], self.X[:, t, :], r, gain, ALU.mult, ALU.mult))
            if shift is not None:
                v = self.vec.done(self.vec.after().tensor_tensor(out[:, t, :], out[:, t, :], shift, ALU.add))
            marks.append(v)
        return marks

    def norm_operand(self, x_marks, gain, gain_mark, x, shift=None):
        self.act.wait(*self.hn_free)
        marks = self.normed(x_marks, gain, gain_mark, self.HN, shift)
        for t in range(NT):
            self.transposed(self.HN[:, t, :], [P * i for i in range(KT)], x, 0, t, marks[t])
        self.hn_free = (self.pe.last,)

    def add_to_x(self, n):
        def evacuate(t, bank, m):
            x = self.X[:, t, n * CN:(n + 1) * CN]
            v = self.vec.done(self.vec.after(m).tensor_tensor(x, x, bank.t[:, :], ALU.add))
            bank.free = (v,)
            self.x_marks = [v]
        return evacuate

    def copy_to(self, dst_of, func=ACT.Copy):
        def evacuate(t, bank, m):
            dst = dst_of(t)
            a = self.act.done(self.act.after(m).activation(dst, bank.t[:, 0:dst.shape[-1]], func))
            bank.free = (a,)
            self.copied = a
        return evacuate

    def run(self, tasks, fill=()):
        tasks, active, fill = list(tasks), [], iter(fill)
        while tasks or active:
            for task in list(active):
                if next(task, "end") == "end":
                    active.remove(task)
            if tasks and len(active) < 3:
                task = tasks.pop(0)
                if next(task, "end") != "end":
                    active.append(task)
            next(fill, None)
        for _ in fill:
            pass

    def softmax_rows(self, bank, m, nh, nk, bias, scale, floor=None):
        V, A = self.vec, self.act
        slot = self.rows_ring.take()
        s = slot.t[:, 0:nh * nk].rearrange("p (h n) -> p h n", n=nk)
        ps = bank.t[:, 0:nh * nk].rearrange("p (h n) -> p h n", n=nk)
        v = V.done(V.after(m, *slot.free).scalar_tensor_tensor(s, ps, scale, bias, ALU.mult, ALU.add))
        bank.free = (v,)
        top, neg, sums = self.stat(nh), self.stat(nh), self.stat(nh)
        v = V.done(V.after().tensor_reduce(top, s, AX.X, ALU.max))
        if floor is not None:
            v = V.done(V.after().tensor_tensor(top, top, floor, ALU.max))
        v = V.done(V.after().tensor_scalar(neg, top, -1.0, None, ALU.mult))
        A.wait(v)
        for h in range(nh):
            a = A.done(A.beside().activation(s[:, h, :], s[:, h, :], ACT.Exp, bias=neg[:, h:h + 1], accum_out=sums[:, h:h + 1]))
        return slot, s, sums, neg, a

    def turn(self, pieces, mark, done_with):
        bank, slot = self.small.take(), self.turned.take()
        self.pe.wait(mark, *bank.free)
        for i, p in enumerate(pieces):
            tr = self.nc.tensor.transpose(bank.t[:, i * P:(i + 1) * P], p, self.ident)
        m = self.pe.done(tr)
        done_with.free = (m,)
        n = P * len(pieces)
        a = self.act.done(self.act.after(m, *slot.free).activation(slot.t[:, 0:n], bank.t[:, 0:n], ACT.Copy))
        bank.free = (a,)
        return slot, a



def first_block(k, w):
    nc, V, A, T = k.nc, k.vec, k.act, k.nc.tensor
    with ExitStack() as phase:
        k.phase = phase
        gate = k.sb("gate", [P, D])
        with ExitStack() as inner:
            k.phase = inner
            names = {"norm_g": w["norm_g"][0], "b_shift": w["b_ada"][0, 0:D], "b_scale": w["b_ada"][0, D:2 * D],
                     "b_gate": w["b_ada"][0, 2 * D:3 * D]}
            rows = {n: k.sb("row_" + n, [P, D]) for n in names}
            loaded = {n: k.row(n, rows[n][:, :], names[n]) for n in names}
            ch, cl = k.pair("cond", KT, P)
            c_silu = k.sb("c_silu", [P, KT])
            a = A.done(A.after(k.columns_ready).activation(c_silu[:, :], k.vcol["c"], ACT.Silu))
            wide = c_silu[:, :].unsqueeze(2).broadcast_to((P, KT, P))
            v = V.done(V.after(a).tensor_copy(ch, wide))
            v = V.done(V.after(v).tensor_tensor(cl, wide, ch.bitcast(F32), ALU.subtract))
            c_op = Operand(ch, cl, (v,))

            def part(n, base, dst):
                def evacuate(banks, m):
                    at = slice(n * CN, (n + 1) * CN)
                    V.wait(loaded["b_" + base], loaded["norm_g"])
                    v = V.done(V.after(m).tensor_tensor(dst[:, at], banks[0].t[:, :], rows["b_" + base][:, at], ALU.add))
                    banks[0].free = (v,)
                    if base == "scale":
                        v = V.done(V.after().scalar_tensor_tensor(dst[:, at], dst[:, at], 1.0, rows["norm_g"][:, at], ALU.add, ALU.mult))
                    k.mod_mark = v
                return evacuate
            for base, dst in (("scale", k.G[0].t), ("shift", k.G[1].t), ("gate", gate)):
                for n in range(D // CN):
                    for _ in k.block(c_op, KT, [(0, 0, 0, 0, CN)], part(n, base, dst)):
                        pass
                if base == "shift":
                    k.norm_operand([k.x_loaded], k.G[0].t[:, :], k.mod_mark, k.H, k.G[1].t[:, :])
            gate_mark = k.mod_mark
            k.everyone()
        k.phase = phase
        c1 = k.sb("first_constants", [P, FIRST_W])
        c1_mark = k.side.start("first", c1[:, :], w["first_constants"])
        for l in (V, A, k.pe):
            l.wait(c1_mark)

        def table(name, *dims):
            at, n = FIRST[name]
            v = c1[:, at:at + n]
            return v.rearrange("p (a b) -> p a b", a=dims[0]) if dims else v
        k.rows_ring = k.ring("rows", 2, [P, 512])
        k.turned = k.ring("turned", 2, [P, 512])
        two = [P, NT, BW]
        q_c, k_c = k.sb("q_c", [HD, NH, S]), k.sb("k_c", [HD, NH, S])
        q_d, k_d = k.sb("q_d", [HD, NH, S]), k.sb("k_d", [HD, NH, S])
        k_b = k.sb("k_b", [HD, 2, S])
        q_b, q_a = q_d, k_d
        k_sel, k_win, cmp_t = k.sb("k_sel", [HD, S]), k.sb("k_win", [HD, S]), k.sb("cmp_t", [P, S])
        v_sel, v_win = k.sb("v_sel", [P, NT, HD]), k.sb("v_win", [P, NT, HD])
        v_c, v_d = k.sb("v_c", two), k.sb("v_d", two)
        v_b = v_d[:, :, 0:2 * HD]
        z = {b: k.sb("z_" + b, two) for b in "acd"}
        z["b"] = z["d"]
        gates = k.sb("gates", [P, NT, 3 * NH])
        merged = k.sb("merged", [P, NT, D])
        sig = Ring([k.HN[:, i, :].rearrange("p (t n) -> p t n", t=NT) for i in range(NT)])
        A.wait(*k.hn_free)
        y_ring = k.ring("y", 2, two)
        y_op = [Operand(*k.pair(f"y_op{i}", BW // P)) for i in range(2)]
        made = {}

        def heads(bank, off, dst, h0, m):
            for i in range(2):
                a = A.done(A.beside(m).activation(dst[:, h0 + i, :], bank.t[i * HD:(i + 1) * HD, off:off + S], ACT.Copy))
            return a

        def qk_block(q, kk, name):
            def evacuate(banks, m):
                for i in range(4):
                    a = heads(banks[i // 2], S * (i % 2), (q, kk)[i // 2], 2 * (i % 2), m)
                    banks[i // 2].free = (a,)
                made[name] = a
            return k.block(k.H, KT, [(i // 2, S * (i % 2), None, P * i, P) for i in range(4)], evacuate)

        def vz_block(vt, zt, name):
            w_v, w_z = vt.shape[-1], zt.shape[-1]

            def evacuate(t, bank, m):
                A.done(A.beside(m).activation(vt[:, t, :], bank.t[:, 0:w_v], ACT.Copy))
                a = A.done(A.beside(m).activation(zt[:, t, :], bank.t[:, w_v:w_v + w_z], ACT.Silu))
                bank.free = (a,)
                made[name] = a
            return evacuate

        def block_c3():
            inner = vz_block(v_b, z["b"], "b_v")

            def evacuate(banks, m):
                made["b_k"] = heads(banks[0], 0, k_b, 0, m)
                banks[0].free = (made["b_k"],)
                for t in range(NT):
                    inner(t, banks[1 + t], m)
            return k.block(k.H, KT, [(0, 0, None, 0, P)] + [(1 + t, 0, t, P, 384) for t in range(NT)], evacuate)

        def block_c2():
            def evacuate(banks, m):
                for i in range(2):
                    a = heads(banks[0], S * i, q_b, 2 * i, m)
                banks[0].free = (a,)
                for t in range(NT):
                    a = A.done(A.beside(m).activation(z["a"][:, t, :], banks[1 + t].t[:, 0:BW], ACT.Silu))
                    banks[1 + t].free = (a,)
                made["b_q"] = a
            return k.block(k.H, KT, [(0, S * i, None, BW + P * i, P) for i in range(2)]
                           + [(1 + t, 0, t, 0, BW) for t in range(NT)], evacuate)

        def block_c1():
            def evacuate(banks, m):
                for i, dst in enumerate((k_sel, k_win)):
                    a = A.done(A.beside(m).activation(dst[:, :], banks[0].t[0:HD, S * i:S * i + S], ACT.Copy))
                banks[0].free = (a,)
                for t in range(NT):
                    b = banks[1 + t]
                    A.done(A.beside(m).activation(v_sel[:, t, :], b.t[:, 0:HD], ACT.Copy))
                    A.done(A.beside(m).activation(v_win[:, t, :], b.t[:, HD:2 * HD], ACT.Copy))
                    a = A.done(A.beside(m).activation(gates[:, t, :], b.t[:, 2 * HD:2 * HD + 3 * NH], ACT.Sigmoid))
                    b.free = (a,)
                made["a_kv"] = a
            items = [(0, 0, None, 0, P), (0, S, None, P, P)]
            for t in range(NT):
                items += [(1 + t, 0, t, HD, HD), (1 + t, HD, t, P + HD, HD + 3 * NH)]
            return k.block(k.H, KT, items, evacuate)

        def block_c0():
            def evacuate(banks, m):
                for i in range(2):
                    a = heads(banks[0], S * i, q_a, 2 * i, m)
                banks[0].free = (a,)
                a = A.done(A.beside(m).activation(cmp_t[:, :], banks[1].t[:, 0:S], ACT.Copy))
                banks[1].free = (a,)
                made["a_q"] = a
            return k.block(k.H, KT, [(0, 0, None, 0, P), (0, S, None, P, P), (1, 0, None, 2 * P, P)], evacuate)

        def merge(i, x):
            for n in range(D // CN):
                slot = sig.take()
                A.wait(*slot.free)
                yield from k.columns(k.H, KT, k.copy_to(lambda t: slot.t[:, t, :], ACT.Sigmoid))
                sig_mark = k.copied

                def evacuate(t, bank, m):
                    at = merged[:, t, n * CN:(n + 1) * CN]
                    g = slot.t[:, t, :]
                    if i == ORDER[0]:
                        v = V.done(V.after(m, sig_mark).tensor_tensor(at, g, bank.t[:, :], ALU.mult))
                    else:
                        v = V.done(V.after(m, sig_mark).tensor_tensor(g, g, bank.t[:, :], ALU.mult))
                        v = V.done(V.after().tensor_tensor(at, at, g, ALU.add))
                    bank.free = (v,)
                    slot.free = (v,)
                    made["merged"] = v
                yield from k.columns(x, BW // P, evacuate)

        def finish(branch, y, mark, op):
            V.wait(made[{"a": "b_q", "b": "b_v", "c": "c_v", "d": "d_v"}[branch]])
            for t in range(NT):
                v = V.done(V.after(mark).tensor_tensor(y.t[:, t, :], y.t[:, t, :], z[branch][:, t, :], ALU.mult))
                k.transposed(y.t[:, t, :], [0, P], op, 0, t, v)
            y.free = (k.pe.last,)

        def score_keys(q, kk, h, ready):
            bank = k.small.take()
            k.pe.wait(ready, *bank.free)
            T.matmul(bank.t[:, 0:S], kk[:, h, 0:P], q[:, h, :], start=True, stop=True, skip_group_check=True)
            m = k.pe.done(T.matmul(bank.t[:, S:S + P], kk[:, h, P:S], q[:, h, P:S], start=False, stop=True, skip_group_check=True))
            return bank, m

        def mix_keys(slot, mark, v, h, y):
            bank = k.small.take()
            k.pe.wait(mark, *bank.free)
            p, vh = slot.t, slice(h * HD, (h + 1) * HD)
            T.matmul(bank.t[:, 0:HD], p[:, 0:P], v[:, 0, vh], start=True, stop=True, skip_group_check=True)
            T.matmul(bank.t[:, HD:2 * HD], p[:, P:S], v[:, 0, vh], start=False, stop=True, skip_group_check=True)
            m = k.pe.done(T.matmul(bank.t[:, HD:2 * HD], p[:, S:S + P], v[:, 1, vh], start=False, stop=True, skip_group_check=True))
            slot.free = (m,)
            a = A.done(A.after(m).activation(y[:, :, vh], bank.t[:, 0:2 * HD].rearrange("p (t n) -> p t n", t=NT), ACT.Copy))
            bank.free = (a,)
            return a

        def retention(h, y):
            bank, m = score_keys(q_d, k_d, h, made["d_qk"])
            slot = k.rows_ring.take()
            decay = table("decay", NH)
            V.done(V.after(m, *slot.free).tensor_tensor(slot.t[:, 0:S], bank.t[:, 0:S], decay[:, h, :], ALU.mult))
            v = V.done(V.beside().tensor_tensor(slot.t[:, S:S + P], bank.t[:, S:S + P], decay[:, h, 0:P], ALU.mult))
            bank.free = (v,)
            yield
            made["y_d"] = mix_keys(slot, v, v_d, h, y)

        def retention_norm(y):
            g = NT * NH
            o = y[:, :, :].rearrange("p t (h d) -> p (t h) d", d=HD)
            sums, mean, sq_sums = k.stat(g), k.stat(g), k.stat(g)
            slot = k.rows_ring.take()
            sq = slot.t[:, :].rearrange("p (g d) -> p g d", d=HD)

            def wide(s):
                return s.unsqueeze(2).broadcast_to((P, g, HD))
            V.done(V.after(made["y_d"], *slot.free).tensor_reduce(sums, o, AX.X, ALU.add))
            V.done(V.after().tensor_scalar(mean, sums, 1.0 / HD, None, ALU.mult))
            V.done(V.after().tensor_tensor(o, o, wide(mean), ALU.subtract))
            V.done(V.after().tensor_tensor(sq, o, o, ALU.mult))
            v = V.done(V.after().tensor_reduce(sq_sums, sq, AX.X, ALU.add))
            slot.free = (v,)
            r, m = k.inverse_root(sq_sums, HD, LN_EPS, v)
            return V.done(V.after(m).tensor_tensor(o, o, wide(r), ALU.mult))

        def stick(h, y):
            n = S + P
            bank, m = score_keys(q_c, k_c, h, made["c_qk"])
            slot, soft = k.rows_ring.take(), k.turned.take()
            zt, sp, strict = slot.t[:, 0:n], soft.t[:, 0:n], table("strict")
            A.done(A.after(m, *slot.free).activation(zt, bank.t[:, 0:n], ACT.Copy, scale=HD ** -0.5))
            A.done(A.after(*soft.free).activation(sp, bank.t[:, 0:n], ACT.Abs, scale=HD ** -0.5))
            bank.free = (A.last,)
            A.done(A.after().activation(sp, sp, ACT.Exp, scale=-1.0))
            a = A.done(A.after().activation(sp, sp, ACT.Ln, bias=1.0))
            V.done(V.after(a).scalar_tensor_tensor(sp, zt, 0.0, sp, ALU.max, ALU.add))
            V.done(V.after().tensor_tensor(zt, zt, sp, ALU.subtract))
            v = V.done(V.after().tensor_tensor(sp, sp, strict, ALU.mult))
            yield
            bank = k.small.take()
            k.pe.wait(v, *bank.free)
            after, ones = table("after"), k.ones
            T.matmul(bank.t[:, 0:S], after, sp[:, 0:S], start=True, stop=True, skip_group_check=True)
            T.matmul(bank.t[:, P:S], ones, sp[:, S:n], start=False, stop=True, skip_group_check=True)
            m = k.pe.done(T.matmul(bank.t[:, S:n], after, sp[:, S:n], start=False, stop=True, skip_group_check=True))
            soft.free = (m,)
            v = V.done(V.after(m).tensor_tensor(zt, zt, bank.t[:, 0:n], ALU.subtract))
            bank.free = (v,)
            a = A.done(A.after(v).activation(zt, zt, ACT.Exp))
            v = V.done(V.after(a).tensor_tensor(zt, zt, strict, ALU.mult))
            yield
            made["y_c"] = mix_keys(slot, v, v_c, h, y)

        def softmax_group(q, kk_of, v_of, bias, heads_, t, ready, out):
            nh, nk = len(heads_), P * (t + 1)
            bank = k.small.take()
            k.pe.wait(ready, *bank.free)
            for i, h in enumerate(heads_):
                mm = T.matmul(bank.t[:, i * nk:(i + 1) * nk], q[:, h, t * P:(t + 1) * P], kk_of(h)[:, 0:nk],
                              start=i == 0, stop=True, skip_group_check=True)
            m = k.pe.done(mm)
            h0 = heads_[0]
            floor = sink[:, h0:h0 + nh] if out.sink else None
            slot, s, sums, neg, a = k.softmax_rows(bank, m, nh, nk, table(bias, NH)[:, h0:h0 + nh, 2 * P - nk:2 * P], HD ** -0.5, floor)
            yield
            turned, tm = k.turn([s[:, i, j * P:(j + 1) * P] for i in range(nh) for j in range(t + 1)], a, slot)
            yield
            bank = k.small.take()
            k.pe.wait(tm, *bank.free)
            for i, h in enumerate(heads_):
                for j in range(t + 1):
                    b = i * (t + 1) + j
                    mm = T.matmul(bank.t[:, i * HD:(i + 1) * HD], turned.t[:, b * P:(b + 1) * P], v_of(h, j),
                                  start=b == 0, stop=True, skip_group_check=True)
            m = k.pe.done(mm)
            turned.free = (m,)
            out(bank, m, sums, neg, heads_, t)

        class Out:
            def __init__(self, y, first, gate_index=None, use_sink=False):
                self.y, self.first, self.gate, self.sink = y, first, gate_index, use_sink

            def __call__(self, bank, m, sums, neg, heads_, t):
                nh, h0 = len(heads_), heads_[0]
                inv = k.stat(nh)
                if self.sink:
                    tail = k.stat(nh)
                    V.done(V.after(m).tensor_tensor(tail, sink[:, h0:h0 + nh], neg, ALU.add))
                    a = A.done(A.after(V.last).activation(tail, tail, ACT.Exp))
                    V.done(V.after(a).tensor_tensor(sums, sums, tail, ALU.add))
                V.done(V.after(m).reciprocal(inv, sums))
                if self.gate is not None:
                    g = gates[:, t, :].rearrange("p (h c) -> p c h", c=3)[:, self.gate, h0:h0 + nh]
                    V.done(V.after().tensor_tensor(inv, inv, g, ALU.mult))
                wide = inv.unsqueeze(2).broadcast_to((P, nh, HD))
                o = bank.t[:, 0:nh * HD].rearrange("p (h d) -> p h d", d=HD)
                y = self.y[:, t, h0 * HD:(h0 + nh) * HD].rearrange("p (h d) -> p h d", d=HD)
                if self.first:
                    bank.free = (V.done(V.after().tensor_tensor(y, o, wide, ALU.mult)),)
                else:
                    slot = k.part_ring.take()
                    part = slot.t[:, 0:nh * HD].rearrange("p (h d) -> p h d", d=HD)
                    bank.free = (V.done(V.after().tensor_tensor(part, o, wide, ALU.mult)),)
                    slot.free = (V.done(V.after().tensor_tensor(y, y, part, ALU.add)),)

        groups = [([0, 1], 1), ([2, 3], 1), ([0, 1, 2, 3], 0)]
        k.part_ring = k.ring("part", 1, [P, BW])
        sink = k.sb("sink_row", [P, NH])
        V.wait(k.row("sink", sink[:, :], w["sink"][0]))

        def compressed(y):
            w1 = [k.G[i].t[:, :].rearrange("p (t m) -> p t m", m=HD) for i in range(2)]
            w2, half = k.sb("cmp_w2", [P, HD]), CMP // 2
            pos = k.sb("cmp_pos", [CMP, P])
            for j in range(2):
                for i in range(2):
                    l1 = k.side.start("cmp_w1", w1[i][j * HD:(j + 1) * HD, :, :],
                                      w["cmp_w1"][0, j].rearrange("(t d) m -> d t m", d=HD)[:, i * half:(i + 1) * half, :], V.last)
            l2 = k.side.start("cmp_w2", w2[:, :], w["cmp_w2"][0].rearrange("j d m -> (j d) m"))
            l3 = k.side.start("cmp_pos", pos[:, 0:HD], w["cmp_pos"][0, 0])
            l3 = k.side.start("cmp_pos", pos[:, HD:P], w["cmp_pos"][0, 1])
            yield
            bank = k.small.take()
            k.pe.wait(l3, *bank.free)
            m = k.pe.done(T.transpose(bank.t[:, 0:CMP], pos[:, :], k.ident[0:CMP, 0:CMP]))
            pos_t = k.stat(CMP)
            v = V.done(V.after(m).tensor_copy(pos_t, bank.t[:, 0:CMP]))
            bank.free = (v,)
            blocks = cmp_t[:, :].rearrange("p (c t) -> p c t", t=CMP)
            v = V.done(V.after(made["a_q"]).tensor_tensor(blocks, blocks, pos_t.unsqueeze(1).broadcast_to((P, NC, CMP)), ALU.add))
            yield
            hid, hid4 = k.stat(NC), k.stat(NH * NC)
            for j in range(2):
                bank = k.small.take()
                r = slice(j * HD, (j + 1) * HD)
                k.pe.wait(v, l1, *bank.free)
                for t in range(CMP):
                    mm = T.matmul(bank.t[r, 0:NC], w1[t // half][r, t % half, :], blocks[r, :, t], start=t == 0, stop=t == CMP - 1)
                m = k.pe.done(mm)
                a = A.done(A.after(m).activation(hid[r, :], bank.t[r, 0:NC], ACT.Silu))
                bank.free = (a,)
            v = V.done(V.after(a).tensor_copy(hid4[HD:P, :].rearrange("p (h c) -> p h c", h=NH),
                                              hid[HD:P, :].unsqueeze(1).broadcast_to((HD, NH, NC))))
            yield
            kc, vc = k.stat(NC), k_c[0:NH * NC, 0, :]
            b0, b1 = k.small.take(), k.small.take()
            k.pe.wait(a, v, l2, *b0.free, *b1.free)
            m = k.pe.done(T.matmul(b0.t[0:HD, 0:NC], w2[0:HD, :], hid[0:HD, :], start=True, stop=True))
            v0 = V.done(V.after(m).tensor_copy(kc[0:HD, :], b0.t[0:HD, 0:NC]))
            b0.free = (v0,)
            m = k.pe.done(T.matmul(b1.t[0:NH * NC, 0:HD], hid4[HD:P, :], w2[HD:P, :], start=True, stop=True))
            v1 = V.done(V.after(m).tensor_tensor(
                vc.rearrange("p (h d) -> p h d", d=HD),
                b1.t[0:NH * NC, 0:HD].unsqueeze(1).broadcast_to((NH * NC, NH, HD)),
                table("block")[0:NH * NC, :].rearrange("p (h d) -> p h d", d=HD), ALU.mult))
            b1.free = (v1,)
            yield
            bank = k.small.take()
            k.pe.wait(v0, *bank.free)
            for t in range(NT):
                for h in range(NH):
                    c = (t * NH + h) * NC
                    mm = T.matmul(bank.t[:, c:c + NC], q_a[:, h, t * P:(t + 1) * P], kc[0:HD, :],
                                  start=c == 0, stop=True, skip_group_check=True)
            m = k.pe.done(mm)
            g, n = NT * NH, NT * NH * NC
            slot = k.rows_ring.take()
            s = slot.t[:, 0:n]
            s3 = s.rearrange("p (g c) -> p g c", c=NC)
            top, sums, inv = k.stat(g), k.stat(g), k.stat(g)

            def wide(x):
                return x.unsqueeze(2).broadcast_to((P, g, NC))
            v = V.done(V.after(m, *slot.free).scalar_tensor_tensor(s, bank.t[:, 0:n], HD ** -0.5, table("cmp_bias"), ALU.mult, ALU.add))
            bank.free = (v,)
            V.done(V.after().tensor_reduce(top, s3, AX.X, ALU.max))
            v = V.done(V.after().tensor_tensor(s3, s3, wide(top), ALU.subtract))
            a = A.done(A.after(v).activation(s, s, ACT.Exp))
            V.done(V.after(a).tensor_tensor(s, s, table("cmp_mask"), ALU.mult))
            V.done(V.after().tensor_reduce(sums, s3, AX.X, ALU.add))
            V.done(V.after().tensor_scalar(sums, sums, TINY, None, ALU.max))
            V.done(V.after().reciprocal(inv, sums))
            gg = gates[:, :, :].rearrange("p t (h c) -> p (t h) c", c=3)[:, :, 0]
            V.done(V.after().tensor_tensor(inv, inv, gg, ALU.mult))
            v = V.done(V.after().tensor_tensor(s3, s3, wide(inv), ALU.mult))
            yield
            bank, turned = k.small.take(), k.turned.take()
            k.pe.wait(v, *bank.free)
            half = NH * NC
            for t in range(NT):
                tr = T.transpose(bank.t[0:half, t * P:(t + 1) * P], s[:, t * half:(t + 1) * half], k.ident)
            m = k.pe.done(tr)
            slot.free = (m,)
            a = A.done(A.after(m, *turned.free).activation(turned.t[0:half, 0:S], bank.t[0:half, 0:S], ACT.Copy))
            bank.free = (a,)
            yield
            bank = k.small.take()
            k.pe.wait(a, v1, *bank.free)
            for t in range(NT):
                mm = T.matmul(bank.t[:, t * BW:(t + 1) * BW], turned.t[0:half, t * P:(t + 1) * P], vc,
                              start=t == 0, stop=True, skip_group_check=True)
            m = k.pe.done(mm)
            turned.free = (m,)
            v = V.done(V.after(m).tensor_tensor(y[:, :, :], y[:, :, :], bank.t[:, :].rearrange("p (t n) -> p t n", t=NT), ALU.add))
            bank.free = (v,)

        def chain(*gens):
            for g in gens:
                yield from g

        def all_of(gen):
            for _ in gen:
                pass

        all_of(qk_block(q_d, k_d, "d_qk"))
        all_of(k.columns(k.H, KT, vz_block(v_d, z["d"], "d_v")))
        k.pe.wait(made["d_v"])
        y = y_ring.take()
        A.wait(*y.free)
        k.run([retention(h, y.t) for h in range(NH)],
              chain(qk_block(q_c, k_c, "c_qk"), k.columns(k.H, KT, vz_block(v_c, z["c"], "c_v"))))
        finish("d", y, retention_norm(y.t), y_op[0])

        k.pe.wait(made["c_v"])
        A.wait(k.pe.last, V.last)
        y = y_ring.take()
        A.wait(*y.free)
        k.run([stick(h, y.t) for h in range(NH)], chain(block_c3(), block_c2(), merge(3, y_op[0])))
        finish("c", y, made["y_c"], y_op[1])

        k.pe.wait(made["b_v"], made["b_q"])
        y = y_ring.take()
        V.wait(*y.free)
        k.run([softmax_group(q_b, lambda h: k_b[:, h // 2, :], lambda h, j: v_b[:, j, (h // 2) * HD:(h // 2 + 1) * HD],
                             "window", hs, t, made["b_q"], Out(y.t, True, use_sink=True)) for hs, t in groups],
              chain(block_c1(), block_c0(), merge(2, y_op[1])))
        finish("b", y, V.last, y_op[0])

        k.pe.wait(made["a_kv"], made["a_q"])
        V.wait(made["a_kv"], k.pe.last)
        y = y_ring.take()
        V.wait(*y.free)
        k.run([softmax_group(q_a, lambda h: kk[:, :], lambda h, j: vv[:, j, :], "alibi", hs, t, made["a_q"], Out(y.t, first, gi))
               for kk, vv, gi, first in ((k_sel, v_sel, 1, True),) for hs, t in groups]
              + [compressed(y.t)]
              + [softmax_group(q_a, lambda h: k_win[:, :], lambda h, j: v_win[:, j, :], "alibi", hs, t, made["a_q"], Out(y.t, False, 2))
                 for hs, t in groups],
              merge(1, y_op[0]))
        finish("a", y, V.last, y_op[1])
        all_of(merge(0, y_op[1]))

        for t in range(NT):
            k.transposed(merged[:, t, :], [P * i for i in range(KT)], k.H, 0, t, made["merged"])
        for n in range(D // CN):
            def evacuate(t, bank, m):
                at = slice(n * CN, (n + 1) * CN)
                part = sig.slots[0].t[:, t, :]
                v = V.done(V.after(m, gate_mark).tensor_tensor(part, bank.t[:, :], gate[:, at], ALU.mult))
                bank.free = (v,)
                k.x_marks = [V.done(V.after().tensor_tensor(k.X[:, t, at], k.X[:, t, at], part, ALU.add))]
            all_of(k.columns(k.H, KT, evacuate))
        k.everyone()
    k.phase = k.ctx


ORDER = (3, 2, 1, 0)



def drain(gen):
    for _ in gen:
        pass


def memory_keys(k, layer, mem, keys, values, made):
    for n in range(D // CN):
        def to_keys(banks, m):
            for b in range(2):
                a = k.act.done(k.act.after(m).activation(keys[:, 4 * n + 2 * b:4 * n + 2 * b + 2, :],
                                                         banks[b].t[:, :].rearrange("p (k n) -> p k n", n=S), ACT.Copy))
                banks[b].free = (a,)
            made["keys", layer] = a
        yield from k.block(mem, KT, [(i // 2, S * (i % 2), None, P * i, P) for i in range(4)], to_keys)
    for n in range(D // CN):
        yield from k.columns(mem, KT, k.copy_to(lambda t: values[:, t, n * CN:(n + 1) * CN]))
    made["values", layer] = k.copied


def memory_attention(k, layer, keys, values, made):
    V, A, T = k.vec, k.act, k.nc.tensor
    k.rows_ring, k.turned = k.ring(f"mrows{layer}_", 2, [P, 512]), k.ring(f"mturned{layer}_", 2, [P, 512])
    q = k.sb(f"q_mem{layer}", [P, KT, S])
    k.norm_operand(k.x_marks, k.G[0].t[:, :], k.load_gain("norm_mem_2", layer), k.H)
    for n in range(D // CN):
        def to_q(banks, m):
            for b in range(2):
                a = A.done(A.after(m).activation(q[:, 4 * n + 2 * b:4 * n + 2 * b + 2, :],
                                                 banks[b].t[:, :].rearrange("p (k n) -> p k n", n=S), ACT.Copy))
                banks[b].free = (a,)
            made["q"] = a
        drain(k.block(k.H, KT, [(i // 2, S * (i % 2), None, P * i, P) for i in range(4)], to_q))
    A.wait(*k.H.free)
    V.wait(*k.H.free)
    scale = (D // MH) ** -0.5

    def head(h):
        bank, slot = k.small.take(), k.rows_ring.take()
        k.pe.wait(made["q"], made["keys", layer], *bank.free)
        for t in range(NT):
            for j in range(MHT):
                kt = h * MHT + j
                mm = T.matmul(bank.t[:, t * S:(t + 1) * S], q[:, kt, t * P:(t + 1) * P], keys[:, kt, :],
                              start=t == 0 and j == 0, stop=True, skip_group_check=True)
        m = k.pe.done(mm)
        s = slot.t[:, :].rearrange("p (t n) -> p t n", t=NT)
        ps = bank.t[:, :].rearrange("p (t n) -> p t n", t=NT)
        top, neg, sums, inv = k.stat(NT), k.stat(NT), k.stat(NT), k.stat(NT)
        v = V.done(V.after(m).tensor_reduce(top, ps, AX.X, ALU.max))
        v = V.done(V.after().tensor_scalar(neg, top, -scale, None, ALU.mult))
        A.wait(v, *slot.free)
        for t in range(NT):
            a = A.done(A.beside().activation(s[:, t, :], ps[:, t, :], ACT.Exp, bias=neg[:, t:t + 1], scale=scale, accum_out=sums[:, t:t + 1]))
        bank.free = (a,)
        V.done(V.after(a).reciprocal(inv, sums))
        v = V.done(V.after().tensor_tensor(s, s, inv.unsqueeze(2).broadcast_to((P, NT, S)), ALU.mult))
        yield
        turned, tm = k.turn([s[:, t, j * P:(j + 1) * P] for j in range(2) for t in range(NT)], v, slot)
        yield
        bank = k.small.take()
        k.pe.wait(tm, made["values", layer], *bank.free)
        for f in range(MHT):
            c = (h * MHT + f) * P
            for j in range(2):
                mm = T.matmul(bank.t[:, f * S:(f + 1) * S], values[:, j, c:c + P], turned.t[:, j * S:(j + 1) * S],
                              start=f == 0 and j == 0, stop=True, skip_group_check=True)
        m = k.pe.done(mm)
        turned.free = (m,)
        at = slice(h * MHT, (h + 1) * MHT)
        v = k.split_operand(bank.t[:, :].rearrange("p (k n) -> p k n", n=S), m, k.H.high[:, at, :], k.H.low[:, at, :])
        bank.free = (v,)
        k.H.ready = (v,)
    k.run([head(h) for h in range(MH)])
    for n in range(D // CN):
        drain(k.columns(k.H, KT, k.add_to_x(n)))


def feed_forward(k, layer):
    V, A = k.vec, k.act
    with ExitStack() as phase:
        k.phase = phase
        k.norm_operand(k.x_marks, k.G[0].t[:, :], k.load_gain("norm_ffn_2", layer), k.H)
        hidden = Operand(*k.pair(f"hidden{layer}", FT))
        mids = k.ring(f"mid{layer}_", 2, [P, NT, CN])
        pending = []

        def up_to(slot):
            def evacuate(t, bank, m):
                w = slot.w
                v = V.done(V.after(m, slot.gated).tensor_tensor(slot.t[:, t, 0:w], slot.t[:, t, 0:w], bank.t[:, slot.at:slot.at + w], ALU.mult))
                bank.free = (v,)
                slot.mark = v
            return evacuate

        def turn_mid():
            slot, n = pending.pop(0)
            for t in range(NT):
                k.transposed(slot.t[:, t, :], [P * i for i in range(slot.w // P)], hidden, n * (CN // P), t, slot.mark)
            slot.free = (k.pe.last,)
        full = FF // CN
        for n in range(full):
            slot = mids.take()
            slot.w, slot.at = CN, 0
            A.wait(*slot.free)
            drain(k.columns(k.H, KT, k.copy_to(lambda t: slot.t[:, t, :], ACT.Silu)))
            slot.gated = k.copied
            if pending:
                turn_mid()
            drain(k.columns(k.H, KT, up_to(slot)))
            pending.append((slot, n))
        slot = mids.take()
        slot.w, slot.at = FF - full * CN, FF - full * CN
        A.wait(*slot.free)

        def last(t, bank, m):
            a = A.done(A.after(m).activation(slot.t[:, t, 0:slot.w], bank.t[:, 0:slot.w], ACT.Silu))
            slot.gated = a
            up_to(slot)(t, bank, m)
        gen = k.columns(k.H, KT, last)
        next(gen)
        turn_mid()
        drain(gen)
        pending.append((slot, full))
        turn_mid()
        for n in range(D // CN):
            drain(k.columns(hidden, FT, k.add_to_x(n)))
        k.everyone()
    k.phase = k.ctx


def conv_layer(k, w, mem, kv, made):
    V, A, T = k.vec, k.act, k.nc.tensor
    with ExitStack() as phase:
        k.phase = phase
        pad = TAPS - 1
        u, y = k.sb("conv_in", [P, KT, pad + S]), k.sb("conv_out", [P, KT, S])
        taps = k.sb("taps", [P, KT, TAPS])
        tap_rows = k.sb("tap_rows", [TAPS, D])
        sig = k.ring("glu", 2, [P, 2, S])
        b2 = k.sb("b_pw2", [P, D])
        b2_mark = k.row("b_pw2", b2[:, :], w["conv_b_pw2_2"][0])
        taps_mark = k.side.start("taps", tap_rows[:, :], w["conv_w_dw_2"][0])
        k.norm_operand(k.x_marks, k.G[0].t[:, :], k.load_gain("norm_mix_2", 0), k.H)
        zeroed = V.done(V.after().memset(u[:, :, 0:pad], 0.0))
        for g in range(0, KT, 4):
            bank = k.small.take()
            k.pe.wait(taps_mark, *bank.free)
            for i in range(4):
                tr = T.transpose(bank.t[:, i * P:i * P + TAPS], tap_rows[:, (g + i) * P:(g + i + 1) * P], k.ident[0:TAPS, 0:TAPS])
            m = k.pe.done(tr)
            v = V.done(V.after(m).tensor_copy(taps[:, g:g + 4, :], bank.t[:, :].rearrange("p (k n) -> p k n", n=P)[:, :, 0:TAPS]))
            bank.free = (v,)
        fill = memory_keys(k, 0, mem, *kv, made)
        for n in range(KT // 2):
            def evacuate(banks, m):
                slot = sig.take()
                for i in range(2):
                    f = 2 * n + i
                    a = A.done(A.after(m, *slot.free).activation(slot.t[:, i, :], banks[1].t[:, i * S:(i + 1) * S], ACT.Sigmoid,
                                                                bias=k.vcol["b_pw1"][:, KT + f:KT + f + 1]))
                for i in range(2):
                    f = 2 * n + i
                    v = V.done(V.after(m, a).scalar_tensor_tensor(u[:, f, pad:pad + S], banks[0].t[:, i * S:(i + 1) * S],
                                                                  k.vcol["b_pw1"][:, f:f + 1], slot.t[:, i, :], ALU.add, ALU.mult))
                banks[1].free, banks[0].free, slot.free = (a,), (v,), (v,)
            drain(k.block(k.H, KT, [(0, 0, None, 0, P), (0, S, None, P, P), (1, 0, None, 2 * P, P), (1, S, None, 3 * P, P)], evacuate))
        marks = [V.last] * KT
        for tap in range(TAPS):
            for f in range(KT):
                src, wt = u[:, f, tap:tap + S], taps[:, f, tap:tap + 1]
                if tap == 0:
                    marks[f] = V.done(V.beside(marks[f]).tensor_scalar(y[:, f, :], src, wt, k.vcol["b_dw"][:, f:f + 1], ALU.mult, ALU.add))
                else:
                    marks[f] = V.done(V.beside(marks[f]).scalar_tensor_tensor(y[:, f, :], src, wt, y[:, f, :], ALU.mult, ALU.add))
            if tap % 2:
                next(fill, None)
        drain(fill)
        sq, var, root, tmp = k.HN[:, :, :].rearrange("p t (k n) -> p (t k) n", n=S), k.sb("ln_var", [P, S]), k.sb("ln_root", [P, S]), k.sb("ln_tmp", [P, S])
        bank = k.small.take()
        k.pe.wait(marks[KT - 1], *bank.free)
        for f in range(KT):
            mm = T.matmul(bank.t[:, 0:S], k.ones, y[:, f, :], start=f == 0, stop=f == KT - 1)
        m = k.pe.done(mm)
        V.done(V.after(m).tensor_scalar(tmp[:, :], bank.t[:, 0:S], 1.0 / D, None, ALU.mult))

        def wide(x):
            return x[:, :].unsqueeze(1).broadcast_to((P, KT, S))
        v = V.done(V.after().tensor_tensor(y[:, :, :], y[:, :, :], wide(tmp), ALU.subtract))
        bank.free = (v,)
        a = A.done(A.after(v, *k.hn_free).activation(sq, y[:, :, :], ACT.Square))
        bank = k.small.take()
        k.pe.wait(a, *bank.free)
        for f in range(KT):
            mm = T.matmul(bank.t[:, 0:S], k.ones, sq[:, f, :], start=f == 0, stop=f == KT - 1)
        m = k.pe.done(mm)
        k.hn_free = (m,)
        v = V.done(V.after(m).tensor_scalar(var[:, :], bank.t[:, 0:S], 1.0 / D, LN_EPS, ALU.mult, ALU.add))
        bank.free = (v,)
        A.done(A.after(v).activation(root[:, :], var[:, :], ACT.Ln))
        a = A.done(A.after().activation(root[:, :], root[:, :], ACT.Exp, scale=-0.5))
        V.done(V.after(a).tensor_tensor(tmp[:, :], root[:, :], root[:, :], ALU.mult))
        V.done(V.after().tensor_tensor(tmp[:, :], tmp[:, :], var[:, :], ALU.mult))
        V.done(V.after().tensor_scalar(tmp[:, :], tmp[:, :], -0.5, 1.5, ALU.mult, ALU.add))
        V.done(V.after().tensor_tensor(root[:, :], root[:, :], tmp[:, :], ALU.mult))
        v = V.done(V.after().tensor_tensor(y[:, :, :], y[:, :, :], wide(root), ALU.mult))
        A.wait(v)
        for f in range(KT):
            a = A.done(A.beside().activation(y[:, f, :], y[:, f, :], ACT.Silu, scale=k.vcol["ln_g"][:, f:f + 1], bias=k.vcol["ln_b"][:, f:f + 1]))
        V.wait(*k.H.free)
        v = V.done(V.after(a).tensor_copy(k.H.high[:, :, :], y[:, :, :]))
        k.H.ready = (V.done(V.after(v).tensor_tensor(k.H.low[:, :, :], y[:, :, :], k.H.high[:, :, :].bitcast(F32), ALU.subtract)),)
        for t in range(NT):
            V.done(V.after(b2_mark).tensor_tensor(k.X[:, t, :], k.X[:, t, :], b2[:, :], ALU.add))
        for n in range(D // CN):
            drain(k.columns(k.H, KT, k.add_to_x(n)))
        k.everyone()
    k.phase = k.ctx


def rope_tables(k, w, cos, sin):
    V, A, n = k.vec, k.act, ROT // 2
    raw, pos = k.sb("positions", [P, NT], I32), k.stat(NT)
    with k.nc.allow_non_contiguous_dma(reason="256 numbers, a row of partitions each"):
        l = k.side.start("positions", raw[:, :], w["positions_2"][0].rearrange("(t p) -> p t", p=P))
    V.done(V.after(l).tensor_copy(pos, raw[:, :]))
    step = 1.5 * 2.0 ** 23
    ang, turns, r = k.stat(NT * n), k.stat(NT * n), k.stat(NT * n)
    for t in range(NT):
        V.done(V.after().tensor_scalar(ang[:, t * n:(t + 1) * n], k.invfreq, pos[:, t:t + 1], None, ALU.mult))
    c1 = 6.28125
    c2 = round((TWO_PI - c1) * 2.0 ** 20) / 2.0 ** 20
    c3 = TWO_PI - c1 - c2
    for dst, quarter in ((cos, 0.25), (sin, 0.0)):
        V.done(V.after().tensor_scalar(turns, ang, 1.0 / TWO_PI, quarter, ALU.mult, ALU.add))
        V.done(V.after().tensor_scalar(turns, turns, step, None, ALU.add))
        V.done(V.after().tensor_scalar(turns, turns, step, None, ALU.subtract))
        V.done(V.after().scalar_tensor_tensor(r, turns, -c1, ang, ALU.mult, ALU.add))
        V.done(V.after().scalar_tensor_tensor(r, turns, -c2, r, ALU.mult, ALU.add))
        V.done(V.after().scalar_tensor_tensor(r, turns, -c3, r, ALU.mult, ALU.add))
        V.done(V.after().tensor_scalar(r, r, quarter * TWO_PI, 3.1415925, ALU.add, ALU.min))
        v = V.done(V.after().tensor_scalar(r, r, -3.1415925, None, ALU.max))
        a = A.done(A.after(v).activation(dst, r, ACT.Sin))
        V.wait(a)
    return a


def differential_layer(k, w, mem, kv, made):
    V, A, T = k.vec, k.act, k.nc.tensor
    with ExitStack() as phase:
        k.phase = phase
        tok = k.HN
        qt, kt_ = k.sb("q_t", [P, DH, S]), k.sb("k_t", [P, DH, S])
        vals, out = k.sb("vals", [P, NT, D]), k.sb("attended", [P, NT, D])
        k.rows_ring = k.ring("drows", 4, [P, 512])
        k.turned = k.ring("dturned", 2, [P, 512])
        cos, sin = k.stat(NT * ROT // 2), k.stat(NT * ROT // 2)
        rope_tables(k, w, cos, sin)
        lrow = k.sb("lambda_rows", [P, 4, HD])
        for i, n in enumerate(("q1", "k1", "q2", "k2")):
            l = k.row("lambda", lrow[:, i, :], w[f"diff_lambda_{n}_2"][0])
        e, neg_lam = k.stat(2), k.stat(1)
        V.done(V.after(l).tensor_tensor(lrow[:, 0, :], lrow[:, 0, :], lrow[:, 1, :], ALU.mult))
        V.done(V.after().tensor_tensor(lrow[:, 1, :], lrow[:, 2, :], lrow[:, 3, :], ALU.mult))
        v = V.done(V.after().tensor_reduce(e, lrow[:, 0:2, :], AX.X, ALU.add))
        a = A.done(A.after(v).activation(e, e, ACT.Exp))
        V.done(V.after(a).tensor_tensor(neg_lam, e[:, 1:2], e[:, 0:1], ALU.subtract))
        V.done(V.after().tensor_scalar(neg_lam, neg_lam, LAMBDA_INIT, None, ALU.subtract))

        def rotate(t, mark):
            n = ROT // 2
            heads = tok[:, t, :].rearrange("p (h d) -> p h d", d=HD)
            r1, r2 = heads[:, :, 0:n], heads[:, :, n:2 * n]
            c = cos[:, t * n:(t + 1) * n].unsqueeze(1).broadcast_to((P, 2 * DH, n))
            s = sin[:, t * n:(t + 1) * n].unsqueeze(1).broadcast_to((P, 2 * DH, n))
            slot = k.rows_ring.take()
            q4 = slot.t[:, :].rearrange("p (f h d) -> p f h d", f=4, d=n)
            V.done(V.after(mark, *slot.free).tensor_tensor(q4[:, 0], r1, c, ALU.mult))
            V.done(V.beside().tensor_tensor(q4[:, 1], r2, s, ALU.mult))
            V.done(V.beside().tensor_tensor(q4[:, 2], r1, s, ALU.mult))
            V.done(V.beside().tensor_tensor(q4[:, 3], r2, c, ALU.mult))
            V.done(V.after().tensor_tensor(r1, q4[:, 0], q4[:, 1], ALU.subtract))
            v = V.done(V.after().tensor_tensor(r2, q4[:, 2], q4[:, 3], ALU.add))
            slot.free = (v,)
            return v

        def project_heads(dst):
            for n in range(D // CN):
                A.wait(k.pe.last)
                drain(k.columns(k.H, KT, k.copy_to(lambda t: tok[:, t, n * CN:(n + 1) * CN])))
            for t in range(NT):
                v = rotate(t, k.copied)
                for g in range(0, DH, 4):
                    bank = k.small.take()
                    k.pe.wait(v, *bank.free)
                    for i in range(4):
                        tr = T.transpose(bank.t[:, i * P:(i + 1) * P], tok[:, t, (g + i) * P:(g + i + 1) * P], k.ident)
                    m = k.pe.done(tr)
                    a = A.done(A.after(m).activation(dst[:, g:g + 4, t * P:(t + 1) * P], bank.t[:, :].rearrange("p (k n) -> p k n", n=P), ACT.Copy))
                    bank.free = (a,)
            k.hn_free = (k.pe.last,)
            return a
        k.norm_operand(k.x_marks, k.G[0].t[:, :], k.load_gain("kv_norm_2", None), k.H)
        made["k"] = project_heads(kt_)
        for n in range(D // CN):
            drain(k.columns(k.H, KT, k.copy_to(lambda t: vals[:, t, n * CN:(n + 1) * CN])))
        made["v"] = k.copied
        k.norm_operand(k.x_marks, k.G[0].t[:, :], k.load_gain("norm_mix_2", 1), k.H)
        made["q"] = project_heads(qt)
        k.pe.wait(made["k"], made["v"], made["q"])
        scale = HD ** -0.5
        causal = k.causal

        def group(heads, t):
            nh, nk = len(heads), P * (t + 1)
            parts = []
            for c in range(2):
                r = slice(c * HD, (c + 1) * HD)
                bank, slot = k.small.take(), k.rows_ring.take()
                k.pe.wait(*bank.free)
                for i, h in enumerate(heads):
                    mm = T.matmul(bank.t[:, i * nk:(i + 1) * nk], qt[r, h, t * P:(t + 1) * P], kt_[r, h, 0:nk],
                                  start=i == 0, stop=True, skip_group_check=True)
                m = k.pe.done(mm)
                s = slot.t[:, :].rearrange("p (h n) -> p h n", n=nk)
                mask = causal[:, 2 * P - nk:2 * P].unsqueeze(1).broadcast_to((P, nh, nk))
                top, neg, sums = k.stat(nh), k.stat(nh), k.stat(nh)
                v = V.done(V.after(m, *slot.free).tensor_tensor(s, bank.t[:, :].rearrange("p (h n) -> p h n", n=nk), mask, ALU.add))
                bank.free = (v,)
                V.done(V.after().tensor_reduce(top, s, AX.X, ALU.max))
                v = V.done(V.after().tensor_scalar(neg, top, -scale, None, ALU.mult))
                A.wait(v)
                for i in range(nh):
                    a = A.done(A.beside().activation(s[:, i, :], s[:, i, :], ACT.Exp, bias=neg[:, i:i + 1], scale=scale, accum_out=sums[:, i:i + 1]))
                parts.append((slot, s, sums, a))
            yield
            (slot0, s0, sum0, _), (slot1, s1, sum1, a) = parts
            V.done(V.after(a).reciprocal(sum0, sum0))
            V.done(V.after().reciprocal(sum1, sum1))
            V.done(V.after().tensor_scalar(sum1, sum1, neg_lam, None, ALU.mult))
            for i in range(nh):
                V.done(V.after().tensor_scalar(s0[:, i, :], s0[:, i, :], sum0[:, i:i + 1], None, ALU.mult))
            for i in range(nh):
                v = V.done(V.after().scalar_tensor_tensor(s0[:, i, :], s1[:, i, :], sum1[:, i:i + 1], s0[:, i, :], ALU.mult, ALU.add))
            slot1.free = (v,)
            turned, tm = k.turn([s0[:, i, j * P:(j + 1) * P] for i in range(nh) for j in range(t + 1)], v, slot0)
            yield
            bank = k.small.take()
            k.pe.wait(tm, *bank.free)
            for i, h in enumerate(heads):
                for j in range(t + 1):
                    b = i * (t + 1) + j
                    mm = T.matmul(bank.t[:, i * P:(i + 1) * P], turned.t[:, b * P:(b + 1) * P], vals[:, j, h * P:(h + 1) * P],
                                  start=b == 0, stop=True, skip_group_check=True)
            m = k.pe.done(mm)
            turned.free = (m,)
            a = A.done(A.after(m).activation(out[:, t, heads[0] * P:(heads[0] + nh) * P], bank.t[:, 0:nh * P], ACT.Copy))
            bank.free = (a,)
            made["out"] = a
        groups = [([h, h + 1], 1) for h in range(0, DH, 2)] + [([h, h + 1, h + 2, h + 3], 0) for h in range(0, DH, 4)]
        k.run([group(hs, t) for hs, t in groups], memory_keys(k, 1, mem, *kv, made))
        for t in range(NT):
            o = out[:, t, :].rearrange("p (h d) -> p h d", d=P)
            sq = tok[:, t, :]
            sums = k.stat(DH)
            V.done(V.after(made["out"], *k.hn_free).tensor_tensor(sq, out[:, t, :], out[:, t, :], ALU.mult))
            v = V.done(V.after().tensor_reduce(sums, sq.rearrange("p (h d) -> p h d", d=P), AX.X, ALU.add))
            r, m = k.inverse_root(sums, P, 1e-5, v, 1.0 - LAMBDA_INIT)
            v = V.done(V.after(m).tensor_tensor(o, o, r.unsqueeze(2).broadcast_to((P, DH, P)), ALU.mult))
            k.transposed(out[:, t, :], [P * i for i in range(KT)], k.H, 0, t, v, scale=k.vcol["subln_g"])
        for n in range(D // CN):
            drain(k.columns(k.H, KT, k.add_to_x(n)))
        k.everyone()
    k.phase = k.ctx


def chunks(w, tiles, cols):
    view = w.rearrange("(k p) n -> p k n", p=P)
    return [([(view[:, f:min(f + CK, tiles), c:c + n], n) for c, n in cols], min(CK, tiles - f)) for f in range(0, tiles, CK)]


def weight_plan(w):
    plan = []

    def add(m, *blocks, tiles=KT):
        for cols in blocks:
            plan.extend(chunks(m, tiles, cols))

    def even(m, tiles=KT):
        add(m, *[[(c, CN)] for c in range(0, D, CN)], tiles=tiles)

    ada, w_in = w["w_ada"][0], w["w_in"][0]
    add(ada, *[[(c, CN)] for c in (D, D + CN, 0, CN, 2 * D, 2 * D + CN)])
    add(w_in, [(W_D_Q, 512)], [(W_D_V, 512)], [(W_C_Q, 512)], [(W_C_V, 512)])
    add(w_in, [(W_B_K, 512)], [(W_A_Z, 512)])

    def merge(i):
        for c in range(0, D, CN):
            add(w["w_merge"][0, i], [(c, CN)])
            add(w["w_br"][0, i], [(c, CN)], tiles=BW // P)
    merge(3)
    add(w_in, [(W_A_KV + 2 * HD, 268)], [(W_A_Q, 384)])
    merge(2)
    merge(1)
    merge(0)
    even(w["w_out"][0])

    pw1 = w["conv_w_pw1_2"][0]
    add(pw1, *[[(c, S), (D + c, S)] for c in range(0, D, S)])

    def memory(layer):
        even(w["mem_w_k_2"][layer])
        even(w["mem_w_v_2"][layer])

    def memory_use(layer):
        even(w["mem_w_q_2"][layer])
        even(w["mem_w_o_2"][layer])

    def feed(layer):
        g, u, d = w["ffn_w_gate_2"][layer], w["ffn_w_up_2"][layer], w["ffn_w_down_2"][layer]
        for c in range(0, FF - CN + 1, CN):
            add(g, [(c, CN)])
            add(u, [(c, CN)])
        c = FF // CN * CN
        gv, uv = (m.rearrange("(k p) n -> p k n", p=P) for m in (g, u))
        for f in range(0, KT, CK):
            plan.append(([(gv[:, f:f + CK, c:FF], FF - c), (uv[:, f:f + CK, c:FF], FF - c)], CK))
        even(d, tiles=FT)
    memory(0)
    even(w["conv_w_pw2_2"][0])
    memory_use(0)
    feed(0)
    even(w["w_k_shared_2"])
    even(w["w_v_shared_2"])
    even(w["diff_w_q_2"][0])
    memory(1)
    even(w["diff_w_o_2"][0])
    memory_use(1)
    feed(1)
    return plan


def build(nc, w, out):
    with ExitStack() as ctx:
        k = Kernel(nc, ctx, w)
        common = k.sb("common", [P, COMMON_W])
        common_mark = k.side.start("common", common[:, :], w["common_constants"])

        def const(name):
            at, n = COMMON[name]
            return common[:, at:at + n]
        k.ident, k.ones, k.causal, k.invfreq, k.half = (const(n) for n in ("ident", "ones", "causal", "invfreq", "half"))
        k.X, k.HN = k.sb("X", [P, NT, D]), k.sb("HN", [P, NT, D])
        k.G = [Slot(k.sb(f"gain{i}", [P, D])) for i in range(2)]
        k.H = Operand(*k.pair("H", KT))
        k.hn_free, k.x_marks, made = (), [], {}
        k.x_loaded = k.side.start("x", k.X[:, :, :], w["x"][0].rearrange("(t p) n -> p t n", p=P))
        vectors = [("c", w["c"][0]), ("b_pw1", w["conv_b_pw1_2"][0]), ("b_dw", w["conv_b_dw_2"][0]),
                   ("ln_g", w["conv_ln_g_2"][0]), ("ln_b", w["conv_ln_b_2"][0]), ("subln_g", w["diff_subln_g_2"][0])]
        n_rows = sum(v.shape[0] // P for _, v in vectors)
        rows, cols, at = k.sb("vector_rows", [n_rows, P]), k.sb("vector_cols", [P, n_rows]), 0
        k.vcol = {}
        for name, v in vectors:
            n = v.shape[0] // P
            loaded = k.side.start("vectors", rows[at:at + n, :], v.rearrange("(k p) -> k p", p=P))
            k.vcol[name] = cols[:, at:at + n]
            at += n
        k.weights = Weights(k, weight_plan(w))
        bank = k.small.take()
        k.pe.wait(common_mark, loaded)
        k.pool.wait(common_mark)
        k.vec.wait(common_mark)
        m = k.pe.done(nc.tensor.transpose(bank.t[:, 0:n_rows], rows[:, :], k.ident[0:n_rows, 0:n_rows]))
        k.columns_ready = k.vec.done(k.vec.after(m).tensor_copy(cols[:, :], bank.t[:, 0:n_rows]))
        bank.free = (k.columns_ready,)
        k.act.wait(k.columns_ready)

        first_block(k, w)

        gain = k.load_gain("final_g", None)
        k.x_marks = k.normed(k.x_marks, k.G[0].t[:, :], gain, k.X)
        with ExitStack() as phase:
            k.phase = phase
            mem = Operand(*k.pair("mem", KT))
            loaded = k.side.start("mem", k.HN[:, :, :], w["mem_2"][0].rearrange("(t p) n -> p t n", p=P), k.vec.last, *k.hn_free)
            for t in range(NT):
                k.transposed(k.HN[:, t, :], [P * i for i in range(KT)], mem, 0, t, loaded)
            k.hn_free = (k.pe.last,)
            for layer in range(2):
                with ExitStack() as kv_phase:
                    k.phase = kv_phase
                    kv = k.sb(f"mem_keys{layer}", [P, KT, S]), k.sb(f"mem_values{layer}", [P, NT, D])
                    (conv_layer, differential_layer)[layer](k, w, mem, kv, made)
                    with ExitStack() as inner:
                        k.phase = inner
                        memory_attention(k, layer, *kv, made)
                        k.everyone()
                feed_forward(k, layer)
        gain = k.load_gain("norm_final_2", None)
        marks = k.normed(k.x_marks, k.G[0].t[:, :], gain, k.HN)
        for t in range(NT):
            stored = k.stream.start("result", out[0, t * P:(t + 1) * P, :], k.HN[:, t, :], marks[t])
        k.stream.lane.wait(stored)


_INS = ["x", "c", "w_ada", "b_ada", "norm_g", "w_in", "cmp_pos", "cmp_w1", "cmp_w2", "sink", "w_merge", "w_br", "w_out",
        "final_g", "mem_2", "positions_2", "norm_mix_2", "norm_mem_2", "norm_ffn_2", "norm_final_2", "conv_w_pw1_2",
        "conv_b_pw1_2", "conv_w_dw_2", "conv_b_dw_2", "conv_ln_g_2", "conv_ln_b_2", "conv_w_pw2_2", "conv_b_pw2_2",
        "kv_norm_2", "w_k_shared_2", "w_v_shared_2", "diff_w_q_2", "diff_lambda_q1_2", "diff_lambda_k1_2",
        "diff_lambda_q2_2", "diff_lambda_k2_2", "diff_subln_g_2", "diff_w_o_2", "mem_w_q_2", "mem_w_k_2", "mem_w_v_2",
        "mem_w_o_2", "ffn_w_gate_2", "ffn_w_up_2", "ffn_w_down_2"]


def kernel(**inputs):
    import concourse.bacc as bacc
    from concourse.bass_utils import run_bass_kernel_spmd

    nc = bacc.Bacc("TRN2", target_bir_lowering=False, num_devices=1)
    common, first = constants()
    arrays = {name: np.ascontiguousarray(inputs[name]) for name in _INS}
    arrays.update(common_constants=common, first_constants=first)
    arrays = {f"in_{name}": a for name, a in arrays.items()}
    w = {name[3:]: nc.dram_tensor(name, a.shape, mybir.dt.from_np(a.dtype), kind="ExternalInput").ap()
         for name, a in arrays.items()}
    out = nc.dram_tensor("result", (1, S, D), F32, kind="ExternalOutput").ap()
    build(nc, w, out)
    r = run_bass_kernel_spmd(nc, [arrays], core_ids=[0])
    return r.results[0]["result"]
```

```python
from contextlib import ExitStack

import numpy as np

import concourse.bass as bass
from concourse import mybir

F32 = mybir.dt.float32
F32R = mybir.dt.float32r
I32 = mybir.dt.int32
ALU = mybir.AluOpType
ACT = mybir.ActivationFunctionType
AX = mybir.AxisListType

P = 128
D = 1024
S = 256
NT = S // P
KT = D // P
HD = 64
NH = 4
BW = NH * HD
CMP = 32
NC = S // CMP
TAPS = 31
DH = 8
ROT = 16
MH = 4
MHT = D // MH // P
FF = 2816
FT = FF // P
CK, CN = 4, 512
RMS_EPS, LN_EPS = 1e-6, 1e-5
NEG = -1e30
TINY = 1e-30
LAMBDA_INIT = 0.8 - 0.6 * float(np.exp(-0.3))
TWO_PI = 2.0 * float(np.pi)

W_A_Q, W_A_KV, W_A_G, W_A_Z = 0, 256, 640, 652
W_B_Q, W_B_K, W_B_V, W_B_Z = 908, 1164, 1292, 1420
W_C_Q, W_C_K, W_C_V, W_C_Z = 1676, 1932, 2188, 2444
W_D_Q, W_D_K, W_D_V, W_D_Z = 2700, 2956, 3212, 3468

COMMON = {"ident": (0, 128), "ones": (128, 128), "causal": (256, 256), "invfreq": (512, 8), "half": (520, 8)}
COMMON_W = 528
FIRST = {"alibi": (0, 1024), "window": (1024, 1024), "decay": (2048, 1024), "strict": (3072, 384),
         "after": (3456, 128), "cmp_bias": (3584, 64), "cmp_mask": (3648, 64), "block": (3712, 256)}
FIRST_W = 3968


def constants():
    q, j = np.arange(P)[:, None], np.arange(2 * P)[None, :]
    rel = q + P - j
    slopes = 2.0 ** (-8.0 * (np.arange(NH) + 1) / NH)
    common = np.zeros((P, COMMON_W), np.float32)
    common[:, 0:128] = np.eye(P)
    common[:, 128:256] = 1.0
    common[:, 256:512] = np.where(rel >= 0, 0.0, NEG)
    common[:, 512:520] = (500000.0 ** (-np.arange(0, ROT, 2) / ROT)).astype(np.float32)
    common[:, 520:528] = -0.5
    first = np.zeros((P, FIRST_W), np.float32)
    k, i = np.arange(P)[:, None], np.arange(2 * P)[None, :]
    gamma = 1.0 - 2.0 ** (-5.0 - np.arange(NH))
    for h in range(NH):
        bias = -slopes[h] * rel
        first[:, 256 * h:256 * h + 256] = np.where(rel >= 0, bias, NEG)
        first[:, 1024 + 256 * h:1280 + 256 * h] = np.where((rel >= 0) & (rel < 128), bias, NEG)
        first[:, 2048 + 256 * h:2304 + 256 * h] = np.where(i >= k, gamma[h] ** np.maximum(i - k, 0), 0.0) * HD ** -0.5
    first[:, 3072:3328] = i > k
    first[:, 3328:3456] = i[:, :P] > k
    first[:, 3456:3584] = k > i[:, :P]
    t = np.arange(P)[:, None, None, None] + P * np.arange(NT)[None, :, None, None]
    dist = t - (np.arange(NC) * CMP + CMP - 1)[None, None, None, :] + np.zeros((1, 1, NH, 1))
    first[:, 3584:3648] = np.where(dist >= 0, -slopes[None, None, :, None] * dist, NEG).reshape(P, -1)
    first[:, 3648:3712] = (dist >= 0).reshape(P, -1)
    rows = np.arange(NH * NC)[:, None] // NC
    first[:NH * NC, 3712:3968] = rows == (np.arange(BW)[None, :] // HD)
    return common, first


class Mark:
    def __init__(self, sem, value):
        self.sem, self.value = sem, value


class Lane:
    def __init__(self, eng, sem):
        self.eng, self.sem, self.count, self.met, self.last = eng, sem, 0, {}, None

    def wait(self, *marks):
        for m in marks:
            if m is not None and self.met.get(m.sem.name, 0) < m.value:
                self.eng.wait_ge(m.sem, m.value)
                self.met[m.sem.name] = m.value

    def after(self, *marks):
        self.wait(self.last, *marks)
        return self.eng

    def beside(self, *marks):
        self.wait(*marks)
        return self.eng

    def done(self, instruction):
        instruction.then_inc(self.sem, 1)
        self.count += 1
        self.last = Mark(self.sem, self.count)
        return self.last


class Slot:
    def __init__(self, t):
        self.t, self.marks, self.busy = t, (), False

    @property
    def free(self):
        return self.marks

    @free.setter
    def free(self, marks):
        self.marks, self.busy = marks, False


class Ring:
    def __init__(self, tensors):
        self.slots, self.at = [Slot(t) for t in tensors], 0

    def take(self):
        self.at += 1
        slot = self.slots[(self.at - 1) % len(self.slots)]
        assert not slot.busy
        slot.busy = True
        return slot


class Loads:
    def __init__(self, lane, sem):
        self.lane, self.sem, self.sent, self.own = lane, sem, {}, {}

    def start(self, name, dst, src, *marks):
        if name not in self.own:
            self.own[name], self.sent[name] = self.sem("load_" + name), 0
        self.lane.wait(*marks)
        self.lane.eng.dma_start(dst, src).then_inc(self.own[name], 16)
        self.sent[name] += 16
        return Mark(self.own[name], self.sent[name])


class Weights:
    N_RAW, N_SPLIT = 4, 3

    def __init__(self, k, plan):
        self.k, self.plan = k, plan
        self.raw = [Slot(k.sb(f"w_raw{i}", [P, CK * CN])) for i in range(self.N_RAW)]
        self.high = [k.sb(f"w_high{i}", [P, CK * CN], F32R) for i in range(self.N_SPLIT)]
        self.low = [k.sb(f"w_low{i}", [P, CK * CN], F32R) for i in range(self.N_SPLIT)]
        self.read = [None] * self.N_SPLIT
        self.ready = {}
        self.loaded = {}
        self.used, self.due = 0, None
        for i in range(self.N_RAW):
            self.load(i)
        for i in range(self.N_SPLIT):
            self.split(i)

    def view(self, t, i):
        pieces, nk = self.plan[i]
        w = sum(n for _, n in pieces)
        return t[:, 0:nk * w].rearrange("p (k n) -> p k n", k=nk)

    def load(self, i):
        if i >= len(self.plan):
            return
        slot, at = self.raw[i % self.N_RAW], 0
        pieces, nk = self.plan[i]
        for src, n in pieces:
            self.loaded[i] = self.k.stream.start(f"w{i % self.N_RAW}", self.view(slot.t, i)[:, :, at:at + n], src, *slot.free)
            at += n

    def split(self, i):
        if i >= len(self.plan):
            return
        k, slot, j = self.k, self.raw[i % self.N_RAW], i % self.N_SPLIT
        raw, high, low = self.view(slot.t, i), self.view(self.high[j], i), self.view(self.low[j], i)
        a = k.act.done(k.act.beside(self.loaded[i], self.read[j]).activation(high, raw, ACT.Copy))
        v = k.vec.done(k.vec.beside(a, self.loaded[i], self.read[j]).tensor_tensor(low, raw, high.bitcast(F32), ALU.subtract))
        self.ready[i] = v
        slot.free = (v,)
        self.load(i + self.N_RAW)

    def take(self):
        if self.due is not None:
            self.split(self.due)
        i = self.used
        self.used += 1
        return self.view(self.high[i % self.N_SPLIT], i), self.view(self.low[i % self.N_SPLIT], i), self.ready[i]

    def give(self, mark):
        i = self.used - 1
        self.read[i % self.N_SPLIT] = mark
        self.due = i + self.N_SPLIT


class Operand:
    def __init__(self, high, low, ready=()):
        self.high, self.low = high, low
        n = -(-high.shape[1] // CK)
        self.ready, self.free = [ready] * n, [()] * n


class Norm:
    def __init__(self, k, name, layer, slot=0):
        self.k, self.gain, self.slot = k, k.load_gain(name, layer, slot), slot
        self.sums = k.stat(2 * NT)
        self.seen, self.squares = [0] * NT, {}
        self.roots = k.stat(NT)

    def take(self, n, t, mark, squares=True):
        k, at = self.k, slice(n * CN, (n + 1) * CN)
        x, hn = k.X[:, t, at], k.HN[:, t, at]
        v = k.vec.done(k.vec.after(mark, self.gain, *k.hn_free).tensor_tensor(hn, x, k.G[self.slot].t[:, at], ALU.mult))
        if t == NT - 1:
            k.late.append(lambda: self.turn(n, v))
        if squares:
            i = n * NT + t
            a = k.act.done(k.act.after(mark).activation(k.junk[:, :], x, ACT.Square, accum_out=self.sums[:, i:i + 1]))
            self.seen[t] += 1
            if min(self.seen) == 2:
                self.finish(a)

    def turn(self, n, mark):
        k = self.k
        for t in range(NT):
            k.transposed(k.HN[:, t, :], [n * CN + P * i for i in range(CK)], k.H, n * CK, t, mark)
        k.hn_free = (k.pe.last,)

    def finish(self, mark):
        p, k = self.k.pool, self.k
        mean = k.stat(NT)
        p.done(p.after(mark).tensor_tensor(mean, self.sums[:, 0:NT], self.sums[:, NT:2 * NT], ALU.add))
        p.done(p.after().tensor_scalar(mean, mean, 1.0 / D, RMS_EPS, ALU.mult, ALU.add))
        self.mark = p.done(p.after().tensor_tensor(self.roots, mean, k.half[:, 0:NT], ALU.pow))

    def root(self, t):
        for l in (self.k.act, self.k.vec):
            l.wait(self.mark)
        return self.roots[:, t:t + 1]


class Kernel:

    def __init__(self, nc, ctx, w):
        self.nc, self.ctx, self.phase, self.w = nc, ctx, ctx, w

        def lane(name, eng):
            return Lane(eng, self.sem(name))

        self.pe, self.vec = lane("pe_done", nc.tensor), lane("vec_done", nc.vector)
        self.act, self.pool = lane("act_done", nc.scalar), lane("pool_done", nc.gpsimd)
        self.stream = Loads(lane("sp_done", nc.sync), self.sem)
        self.side = Loads(self.pool, self.sem)

        def bank(name):
            return ctx.enter_context(nc.psum_tensor(name, [P, 512], F32))

        self.product = Ring([bank(f"product{i}") for i in range(4)])
        self.small = Ring([bank(f"small{i}") for i in range(4)])
        self.stats = self.sb("stats", [P, 768])
        self.stat_at = 0
        self.late = []

    def sem(self, name):
        return self.ctx.enter_context(self.nc.semaphore(name))

    def sb(self, name, shape, dt=F32):
        return self.phase.enter_context(self.nc.sbuf_tensor(name, shape, dt))

    def stat(self, n):
        self.stat_at += n
        assert self.stat_at <= 768, self.stat_at
        return self.stats[:, self.stat_at - n:self.stat_at]

    def pair(self, name, tiles, n=S):
        return tuple(self.sb(f"{name}_{part}", [P, tiles, n], F32R)[:, :, :] for part in ("high", "low"))

    def load_gain(self, name, layer, slot=0):
        v = self.w[name] if layer is None else self.w[name][layer]
        return self.row(f"gain{slot}", self.G[slot].t[:, :], v, self.vec.last)

    def ring(self, name, n, shape):
        return Ring([self.sb(f"{name}{i}", shape) for i in range(n)])

    def so_far(self):
        return [l.last for l in (self.pe, self.vec, self.act, self.pool)]

    def hand_over(self, marks):
        for l in (self.pe, self.vec, self.act, self.pool):
            l.wait(*marks)

    def everyone(self):
        self.hand_over(self.so_far())


    def block(self, x, tiles, items, evacuate, order=None):
        pe = self.pe
        banks = [self.product.take() for _ in range(1 + max(i[0] for i in items))]
        if order is None:
            order = [(first, items, banks if first + CK >= tiles else []) for first in range(0, tiles, CK)]
        else:
            order = [(first, [i for i in items if i[0] in mine], [banks[b] for b in mine if complete])
                     for first, mine, complete in order]
        started = set()
        for first, part, complete in order:
            high, low, ready = self.weights.take()
            pe.wait(ready, *x.ready[first // CK])
            for b, off, t, col, w in part:
                if b not in started:
                    pe.wait(*banks[b].free)
                for j, kt in enumerate(range(first, min(first + CK, tiles))):
                    for xs, ws in ((x.low, high), (x.high, low), (x.high, high)):
                        if t is None:
                            a, r, n = ws[:, j, col:col + P], xs[:, kt, :], S
                        else:
                            a, r, n = xs[:, kt, t * P:(t + 1) * P], ws[:, j, col:col + w], w
                        mm = self.nc.tensor.matmul(banks[b].t[:, off:off + n], a, r, start=b not in started,
                                                   stop=True, skip_group_check=True)
                        started.add(b)
            m = pe.done(mm)
            x.free[first // CK] = (m,)
            self.flush()
            if complete:
                evacuate(complete, m)
            self.weights.give(m)
            yield

    def flush(self):
        late, self.late = self.late, []
        for f in late:
            f()

    def columns(self, x, tiles, evacuate, w=CN):
        def both(banks, m):
            for t in range(NT):
                evacuate(t, banks[t], m)
        return self.block(x, tiles, [(t, 0, t, 0, w) for t in range(NT)], both)

    def square(self, x, evacuate):
        done = []

        def both(banks, m):
            n = len(done)
            done.append(n)
            for t in range(NT):
                evacuate(n, t, banks[t], m)
        return self.block(x, KT, [(2 * n + t, 0, t, 0, CN) for n in range(2) for t in range(NT)], both,
                          [(first, (2 * n, 2 * n + 1), first + CK == KT) for first in range(0, KT, CK) for n in range(2)])

    def split_operand(self, src, mark, high, low):
        a = self.act.done(self.act.beside(mark).activation(high, src, ACT.Copy))
        return self.vec.done(self.vec.beside(mark, a).tensor_tensor(low, src, high.bitcast(F32), ALU.subtract))

    def transposed(self, src, cols, x, tile0, t, mark, scale=None):
        for g in range(0, len(cols), 4):
            part = cols[g:g + 4]
            bank = self.small.take()
            self.pe.wait(mark, *bank.free)
            for i, c in enumerate(part):
                tr = self.nc.tensor.transpose(bank.t[:, i * P:(i + 1) * P], src[:, c:c + P], self.ident)
            m = self.pe.done(tr)
            at = slice(tile0 + g, tile0 + g + len(part))
            hi, lo = x.high[:, at, t * P:(t + 1) * P], x.low[:, at, t * P:(t + 1) * P]
            ps = bank.t[:, 0:P * len(part)].rearrange("p (k n) -> p k n", n=P)
            chunk = (tile0 + g) // CK
            self.act.wait(*x.free[chunk])
            self.vec.wait(*x.free[chunk])
            if scale is None:
                v = self.split_operand(ps, m, hi, lo)
            else:
                a = self.act.done(self.act.beside(m).activation(hi, ps, ACT.Copy, scale=scale))
                v = self.vec.done(self.vec.beside(m, a).scalar_tensor_tensor(lo, ps, scale, hi.bitcast(F32), ALU.mult, ALU.subtract))
            bank.free = (v,)
            x.ready[chunk] = (v,)
        return v

    def row(self, name, dst, vector, *marks):
        return self.side.start(name, dst, vector.rearrange("(a n) -> a n", a=1).broadcast_to((P, vector.shape[0])), *marks)

    def inverse_root(self, sums, width, eps, mark, scale=1.0):
        n = sums.shape[1]
        mean, root = self.stat(n), self.stat(n)
        p = self.pool
        m = p.done(p.after(mark).tensor_scalar(mean, sums, 1.0 / width, eps, ALU.mult, ALU.add))
        m = p.done(p.after(m).tensor_tensor(root, mean, self.half[:, 0:n], ALU.pow))
        if scale != 1.0:
            m = p.done(p.after(m).tensor_scalar(root, root, scale, None, ALU.mult))
        return root, m

    def normed(self, x_marks, gain, gain_mark, out, shift=None):
        marks = []
        for t in range(NT):
            sums = self.stat(1)
            a = self.act.done(self.act.after(*x_marks).activation(self.HN[:, t, :], self.X[:, t, :], ACT.Square, accum_out=sums))
            r, m = self.inverse_root(sums, D, RMS_EPS, a)
            v = self.vec.done(self.vec.after(m, a, gain_mark).scalar_tensor_tensor(out[:, t, :], self.X[:, t, :], r, gain, ALU.mult, ALU.mult))
            if shift is not None:
                v = self.vec.done(self.vec.after().tensor_tensor(out[:, t, :], out[:, t, :], shift, ALU.add))
            marks.append(v)
        return marks

    def norm_operand(self, x_marks, gain, gain_mark, x, shift=None):
        self.act.wait(*self.hn_free)
        marks = self.normed(x_marks, gain, gain_mark, self.HN, shift)
        for t in range(NT):
            self.transposed(self.HN[:, t, :], [P * i for i in range(KT)], x, 0, t, marks[t])
        self.hn_free = (self.pe.last,)

    def add_to_x(self, n, t, bank, m):
        V, x = self.vec, self.X[:, t, n * CN:(n + 1) * CN]
        v = V.done(V.beside(m).tensor_tensor(x, x, bank.t[:, :], ALU.add))
        bank.free = (v,)
        self.x_marks = [v]
        if self.next_norm is not None:
            self.next_norm.take(n, t, v)

    def add_block(self, n):
        return lambda t, bank, m: self.add_to_x(n, t, bank, m)

    def copy_to(self, dst_of, func=ACT.Copy, scale_of=None):
        def evacuate(t, bank, m):
            dst = dst_of(t)
            scale = 1.0 if scale_of is None else scale_of(t)
            a = self.act.done(self.act.beside(m).activation(dst, bank.t[:, 0:dst.shape[-1]], func, scale=scale))
            bank.free = (a,)
            self.copied = a
        return evacuate

    def run(self, tasks, fill=(), limit=3):
        tasks, active, fill = list(tasks), [], iter(fill)
        while tasks or active:
            for task in list(active):
                if next(task, "end") == "end":
                    active.remove(task)
            if tasks and len(active) < limit:
                task = tasks.pop(0)
                if next(task, "end") != "end":
                    active.append(task)
            next(fill, None)
        for _ in fill:
            pass

    def softmax_rows(self, bank, m, nh, nk, bias, scale, floor=None):
        V, A = self.vec, self.act
        slot = self.rows_ring.take()
        s = slot.t[:, 0:nh * nk].rearrange("p (h n) -> p h n", n=nk)
        ps = bank.t[:, 0:nh * nk].rearrange("p (h n) -> p h n", n=nk)
        v = V.done(V.after(m, *slot.free).scalar_tensor_tensor(s, ps, scale, bias, ALU.mult, ALU.add))
        bank.free = (v,)
        top, neg, sums = self.stat(nh), self.stat(nh), self.stat(nh)
        v = V.done(V.after().tensor_reduce(top, s, AX.X, ALU.max))
        if floor is not None:
            v = V.done(V.after().tensor_tensor(top, top, floor, ALU.max))
        v = V.done(V.after().tensor_scalar(neg, top, -1.0, None, ALU.mult))
        A.wait(v)
        for h in range(nh):
            a = A.done(A.beside().activation(s[:, h, :], s[:, h, :], ACT.Exp, bias=neg[:, h:h + 1], accum_out=sums[:, h:h + 1]))
        return slot, s, sums, neg, a

    def turn(self, pieces, mark, done_with):
        bank, slot = self.small.take(), self.turned.take()
        self.pe.wait(mark, *bank.free)
        for i, p in enumerate(pieces):
            tr = self.nc.tensor.transpose(bank.t[:, i * P:(i + 1) * P], p, self.ident)
        m = self.pe.done(tr)
        done_with.free = (m,)
        n = P * len(pieces)
        a = self.act.done(self.act.after(m, *slot.free).activation(slot.t[:, 0:n], bank.t[:, 0:n], ACT.Copy))
        bank.free = (a,)
        return slot, a



def first_block(k, w):
    nc, V, A, T = k.nc, k.vec, k.act, k.nc.tensor
    with ExitStack() as phase:
        k.phase = phase
        gate = k.sb("gate", [P, D])
        with ExitStack() as inner:
            k.phase = inner
            names = {"norm_g": w["norm_g"][0], "b_shift": w["b_ada"][0, 0:D], "b_scale": w["b_ada"][0, D:2 * D],
                     "b_gate": w["b_ada"][0, 2 * D:3 * D]}
            rows = {n: k.sb("row_" + n, [P, D]) for n in names}
            loaded = {n: k.row(n, rows[n][:, :], names[n]) for n in names}
            ch, cl = k.pair("cond", KT, P)
            c_silu = k.sb("c_silu", [P, KT])
            a = A.done(A.after(k.columns_ready).activation(c_silu[:, :], k.vcol["c"], ACT.Silu))
            wide = c_silu[:, :].unsqueeze(2).broadcast_to((P, KT, P))
            v = V.done(V.after(a).tensor_copy(ch, wide))
            v = V.done(V.after(v).tensor_tensor(cl, wide, ch.bitcast(F32), ALU.subtract))
            c_op = Operand(ch, cl, (v,))

            def part(n, base, dst):
                def evacuate(banks, m):
                    at = slice(n * CN, (n + 1) * CN)
                    V.wait(loaded["b_" + base], loaded["norm_g"])
                    v = V.done(V.after(m).tensor_tensor(dst[:, at], banks[0].t[:, :], rows["b_" + base][:, at], ALU.add))
                    banks[0].free = (v,)
                    if base == "scale":
                        v = V.done(V.after().scalar_tensor_tensor(dst[:, at], dst[:, at], 1.0, rows["norm_g"][:, at], ALU.add, ALU.mult))
                    k.mod_mark = v
                return evacuate
            for base, dst in (("scale", k.G[0].t), ("shift", k.G[1].t), ("gate", gate)):
                for n in range(D // CN):
                    for _ in k.block(c_op, KT, [(0, 0, 0, 0, CN)], part(n, base, dst)):
                        pass
                if base == "shift":
                    k.norm_operand([k.x_loaded], k.G[0].t[:, :], k.mod_mark, k.H, k.G[1].t[:, :])
            gate_mark = k.mod_mark
            k.everyone()
        k.phase = phase
        c1 = k.sb("first_constants", [P, FIRST_W])
        c1_mark = k.side.start("first", c1[:, :], w["first_constants"])
        for l in (V, A, k.pe):
            l.wait(c1_mark)

        def table(name, *dims):
            at, n = FIRST[name]
            v = c1[:, at:at + n]
            return v.rearrange("p (a b) -> p a b", a=dims[0]) if dims else v
        k.rows_ring = k.ring("rows", 2, [P, 512])
        k.turned = k.ring("turned", 2, [P, 512])
        two = [P, NT, BW]
        q_c, k_c = k.sb("q_c", [HD, NH, S]), k.sb("k_c", [HD, NH, S])
        q_d, k_d = k.sb("q_d", [HD, NH, S]), k.sb("k_d", [HD, NH, S])
        k_b = k.sb("k_b", [HD, 2, S])
        q_b, q_a = q_d, k_d
        k_sel, k_win, cmp_t = k.sb("k_sel", [HD, S]), k.sb("k_win", [HD, S]), k.sb("cmp_t", [P, S])
        v_sel, v_win = k.sb("v_sel", [P, NT, HD]), k.sb("v_win", [P, NT, HD])
        v_c, v_d = k.sb("v_c", two), k.sb("v_d", two)
        v_b = v_d[:, :, 0:2 * HD]
        z = {b: k.sb("z_" + b, two) for b in "acd"}
        z["b"] = z["d"]
        gates = k.sb("gates", [P, NT, 3 * NH])
        merged = k.sb("merged", [P, NT, D])
        sig = Ring([k.HN[:, i, :].rearrange("p (t n) -> p t n", t=NT) for i in range(NT)])
        A.wait(*k.hn_free)
        y_ring = k.ring("y", 2, two)
        y_op = [Operand(*k.pair(f"y_op{i}", BW // P)) for i in range(2)]
        made = {}

        def heads(bank, off, dst, h0, m):
            for i in range(2):
                a = A.done(A.beside(m).activation(dst[:, h0 + i, :], bank.t[i * HD:(i + 1) * HD, off:off + S], ACT.Copy))
            return a

        def qk_block(q, kk, name):
            def evacuate(banks, m):
                for i in range(4):
                    a = heads(banks[i // 2], S * (i % 2), (q, kk)[i // 2], 2 * (i % 2), m)
                    banks[i // 2].free = (a,)
                made[name] = a
            return k.block(k.H, KT, [(i // 2, S * (i % 2), None, P * i, P) for i in range(4)], evacuate)

        def vz_block(vt, zt, name):
            w_v, w_z = vt.shape[-1], zt.shape[-1]

            def evacuate(t, bank, m):
                A.done(A.beside(m).activation(vt[:, t, :], bank.t[:, 0:w_v], ACT.Copy))
                a = A.done(A.beside(m).activation(zt[:, t, :], bank.t[:, w_v:w_v + w_z], ACT.Silu))
                bank.free = (a,)
                made[name] = a
            return evacuate

        def block_c3():
            inner = vz_block(v_b, z["b"], "b_v")

            def evacuate(banks, m):
                made["b_k"] = heads(banks[0], 0, k_b, 0, m)
                banks[0].free = (made["b_k"],)
                for t in range(NT):
                    inner(t, banks[1 + t], m)
            return k.block(k.H, KT, [(0, 0, None, 0, P)] + [(1 + t, 0, t, P, 384) for t in range(NT)], evacuate)

        def block_c2():
            def evacuate(banks, m):
                for i in range(2):
                    a = heads(banks[0], S * i, q_b, 2 * i, m)
                banks[0].free = (a,)
                for t in range(NT):
                    a = A.done(A.beside(m).activation(z["a"][:, t, :], banks[1 + t].t[:, 0:BW], ACT.Silu))
                    banks[1 + t].free = (a,)
                made["b_q"] = a
            return k.block(k.H, KT, [(0, S * i, None, BW + P * i, P) for i in range(2)]
                           + [(1 + t, 0, t, 0, BW) for t in range(NT)], evacuate)

        def block_c1():
            def evacuate(banks, m):
                for i, dst in enumerate((k_sel, k_win)):
                    a = A.done(A.beside(m).activation(dst[:, :], banks[0].t[0:HD, S * i:S * i + S], ACT.Copy))
                banks[0].free = (a,)
                for t in range(NT):
                    b = banks[1 + t]
                    A.done(A.beside(m).activation(v_sel[:, t, :], b.t[:, 0:HD], ACT.Copy))
                    A.done(A.beside(m).activation(v_win[:, t, :], b.t[:, HD:2 * HD], ACT.Copy))
                    a = A.done(A.beside(m).activation(gates[:, t, :], b.t[:, 2 * HD:2 * HD + 3 * NH], ACT.Sigmoid))
                    b.free = (a,)
                made["a_kv"] = a
            items = [(0, 0, None, 0, P), (0, S, None, P, P)]
            for t in range(NT):
                items += [(1 + t, 0, t, HD, HD), (1 + t, HD, t, P + HD, HD + 3 * NH)]
            return k.block(k.H, KT, items, evacuate)

        def block_c0():
            def evacuate(banks, m):
                for i in range(2):
                    a = heads(banks[0], S * i, q_a, 2 * i, m)
                banks[0].free = (a,)
                a = A.done(A.beside(m).activation(cmp_t[:, :], banks[1].t[:, 0:S], ACT.Copy))
                banks[1].free = (a,)
                made["a_q"] = a
            return k.block(k.H, KT, [(0, 0, None, 0, P), (0, S, None, P, P), (1, 0, None, 2 * P, P)], evacuate)

        def merge(i, x):
            for n in range(D // CN):
                slot = sig.take()
                A.wait(*slot.free)
                yield from k.columns(k.H, KT, k.copy_to(lambda t: slot.t[:, t, :], ACT.Sigmoid))
                sig_mark = k.copied

                def evacuate(t, bank, m):
                    at = merged[:, t, n * CN:(n + 1) * CN]
                    g = slot.t[:, t, :]
                    if i == ORDER[0]:
                        v = V.done(V.after(m, sig_mark).tensor_tensor(at, g, bank.t[:, :], ALU.mult))
                    else:
                        v = V.done(V.after(m, sig_mark).tensor_tensor(g, g, bank.t[:, :], ALU.mult))
                        v = V.done(V.after().tensor_tensor(at, at, g, ALU.add))
                    bank.free = (v,)
                    slot.free = (v,)
                    made["merged"] = v
                yield from k.columns(x, BW // P, evacuate)

        def finish(branch, y, mark, op):
            V.wait(made[{"a": "b_q", "b": "b_v", "c": "c_v", "d": "d_v"}[branch]])
            for t in range(NT):
                v = V.done(V.after(mark).tensor_tensor(y.t[:, t, :], y.t[:, t, :], z[branch][:, t, :], ALU.mult))
                k.transposed(y.t[:, t, :], [0, P], op, 0, t, v)
            y.free = (k.pe.last,)

        def score_keys(q, kk, h, ready):
            bank = k.small.take()
            k.pe.wait(ready, *bank.free)
            T.matmul(bank.t[:, 0:S], kk[:, h, 0:P], q[:, h, :], start=True, stop=True, skip_group_check=True)
            m = k.pe.done(T.matmul(bank.t[:, S:S + P], kk[:, h, P:S], q[:, h, P:S], start=False, stop=True, skip_group_check=True))
            return bank, m

        def mix_keys(slot, mark, v, h, y):
            bank = k.small.take()
            k.pe.wait(mark, *bank.free)
            p, vh = slot.t, slice(h * HD, (h + 1) * HD)
            T.matmul(bank.t[:, 0:HD], p[:, 0:P], v[:, 0, vh], start=True, stop=True, skip_group_check=True)
            T.matmul(bank.t[:, HD:2 * HD], p[:, P:S], v[:, 0, vh], start=False, stop=True, skip_group_check=True)
            m = k.pe.done(T.matmul(bank.t[:, HD:2 * HD], p[:, S:S + P], v[:, 1, vh], start=False, stop=True, skip_group_check=True))
            slot.free = (m,)
            a = A.done(A.after(m).activation(y[:, :, vh], bank.t[:, 0:2 * HD].rearrange("p (t n) -> p t n", t=NT), ACT.Copy))
            bank.free = (a,)
            return a

        def retention(h, y):
            bank, m = score_keys(q_d, k_d, h, made["d_qk"])
            slot = k.rows_ring.take()
            decay = table("decay", NH)
            V.done(V.after(m, *slot.free).tensor_tensor(slot.t[:, 0:S], bank.t[:, 0:S], decay[:, h, :], ALU.mult))
            v = V.done(V.beside().tensor_tensor(slot.t[:, S:S + P], bank.t[:, S:S + P], decay[:, h, 0:P], ALU.mult))
            bank.free = (v,)
            yield
            made["y_d"] = mix_keys(slot, v, v_d, h, y)

        def retention_norm(y):
            g = NT * NH
            o = y[:, :, :].rearrange("p t (h d) -> p (t h) d", d=HD)
            sums, mean, sq_sums = k.stat(g), k.stat(g), k.stat(g)
            slot = k.rows_ring.take()
            sq = slot.t[:, :].rearrange("p (g d) -> p g d", d=HD)

            def wide(s):
                return s.unsqueeze(2).broadcast_to((P, g, HD))
            V.done(V.after(made["y_d"], *slot.free).tensor_reduce(sums, o, AX.X, ALU.add))
            V.done(V.after().tensor_scalar(mean, sums, 1.0 / HD, None, ALU.mult))
            V.done(V.after().tensor_tensor(o, o, wide(mean), ALU.subtract))
            V.done(V.after().tensor_tensor(sq, o, o, ALU.mult))
            v = V.done(V.after().tensor_reduce(sq_sums, sq, AX.X, ALU.add))
            slot.free = (v,)
            r, m = k.inverse_root(sq_sums, HD, LN_EPS, v)
            return V.done(V.after(m).tensor_tensor(o, o, wide(r), ALU.mult))

        def stick(h, y):
            n = S + P
            bank, m = score_keys(q_c, k_c, h, made["c_qk"])
            slot, soft = k.rows_ring.take(), k.turned.take()
            zt, sp, strict = slot.t[:, 0:n], soft.t[:, 0:n], table("strict")
            A.done(A.after(m, *slot.free).activation(zt, bank.t[:, 0:n], ACT.Copy, scale=HD ** -0.5))
            A.done(A.after(*soft.free).activation(sp, bank.t[:, 0:n], ACT.Abs, scale=HD ** -0.5))
            bank.free = (A.last,)
            A.done(A.after().activation(sp, sp, ACT.Exp, scale=-1.0))
            a = A.done(A.after().activation(sp, sp, ACT.Ln, bias=1.0))
            V.done(V.after(a).scalar_tensor_tensor(sp, zt, 0.0, sp, ALU.max, ALU.add))
            V.done(V.after().tensor_tensor(zt, zt, sp, ALU.subtract))
            v = V.done(V.after().tensor_tensor(sp, sp, strict, ALU.mult))
            yield
            bank = k.small.take()
            k.pe.wait(v, *bank.free)
            after, ones = table("after"), k.ones
            T.matmul(bank.t[:, 0:S], after, sp[:, 0:S], start=True, stop=True, skip_group_check=True)
            T.matmul(bank.t[:, P:S], ones, sp[:, S:n], start=False, stop=True, skip_group_check=True)
            m = k.pe.done(T.matmul(bank.t[:, S:n], after, sp[:, S:n], start=False, stop=True, skip_group_check=True))
            soft.free = (m,)
            v = V.done(V.after(m).tensor_tensor(zt, zt, bank.t[:, 0:n], ALU.subtract))
            bank.free = (v,)
            a = A.done(A.after(v).activation(zt, zt, ACT.Exp))
            v = V.done(V.after(a).tensor_tensor(zt, zt, strict, ALU.mult))
            yield
            made["y_c"] = mix_keys(slot, v, v_c, h, y)

        def softmax_group(q, kk_of, v_of, bias, heads_, t, ready, out):
            nh, nk = len(heads_), P * (t + 1)
            bank = k.small.take()
            k.pe.wait(ready, *bank.free)
            for i, h in enumerate(heads_):
                mm = T.matmul(bank.t[:, i * nk:(i + 1) * nk], q[:, h, t * P:(t + 1) * P], kk_of(h)[:, 0:nk],
                              start=i == 0, stop=True, skip_group_check=True)
            m = k.pe.done(mm)
            h0 = heads_[0]
            floor = sink[:, h0:h0 + nh] if out.sink else None
            slot, s, sums, neg, a = k.softmax_rows(bank, m, nh, nk, table(bias, NH)[:, h0:h0 + nh, 2 * P - nk:2 * P], HD ** -0.5, floor)
            yield
            turned, tm = k.turn([s[:, i, j * P:(j + 1) * P] for i in range(nh) for j in range(t + 1)], a, slot)
            yield
            bank = k.small.take()
            k.pe.wait(tm, *bank.free)
            for i, h in enumerate(heads_):
                for j in range(t + 1):
                    b = i * (t + 1) + j
                    mm = T.matmul(bank.t[:, i * HD:(i + 1) * HD], turned.t[:, b * P:(b + 1) * P], v_of(h, j),
                                  start=b == 0, stop=True, skip_group_check=True)
            m = k.pe.done(mm)
            turned.free = (m,)
            out(bank, m, sums, neg, heads_, t)

        class Out:
            def __init__(self, y, first, gate_index=None, use_sink=False):
                self.y, self.first, self.gate, self.sink = y, first, gate_index, use_sink

            def __call__(self, bank, m, sums, neg, heads_, t):
                nh, h0 = len(heads_), heads_[0]
                inv = k.stat(nh)
                if self.sink:
                    tail = k.stat(nh)
                    V.done(V.after(m).tensor_tensor(tail, sink[:, h0:h0 + nh], neg, ALU.add))
                    a = A.done(A.after(V.last).activation(tail, tail, ACT.Exp))
                    V.done(V.after(a).tensor_tensor(sums, sums, tail, ALU.add))
                V.done(V.after(m).reciprocal(inv, sums))
                if self.gate is not None:
                    g = gates[:, t, :].rearrange("p (h c) -> p c h", c=3)[:, self.gate, h0:h0 + nh]
                    V.done(V.after().tensor_tensor(inv, inv, g, ALU.mult))
                wide = inv.unsqueeze(2).broadcast_to((P, nh, HD))
                o = bank.t[:, 0:nh * HD].rearrange("p (h d) -> p h d", d=HD)
                y = self.y[:, t, h0 * HD:(h0 + nh) * HD].rearrange("p (h d) -> p h d", d=HD)
                if self.first:
                    bank.free = (V.done(V.after().tensor_tensor(y, o, wide, ALU.mult)),)
                else:
                    slot = k.part_ring.take()
                    part = slot.t[:, 0:nh * HD].rearrange("p (h d) -> p h d", d=HD)
                    bank.free = (V.done(V.after().tensor_tensor(part, o, wide, ALU.mult)),)
                    slot.free = (V.done(V.after().tensor_tensor(y, y, part, ALU.add)),)

        groups = [([0, 1], 1), ([2, 3], 1), ([0, 1, 2, 3], 0)]
        k.part_ring = k.ring("part", 1, [P, BW])
        sink = k.sb("sink_row", [P, NH])
        V.wait(k.row("sink", sink[:, :], w["sink"][0]))

        def compressed(y):
            w1 = [k.G[i].t[:, :].rearrange("p (t m) -> p t m", m=HD) for i in range(2)]
            w2, half = k.sb("cmp_w2", [P, HD]), CMP // 2
            pos = k.sb("cmp_pos", [CMP, P])
            for j in range(2):
                for i in range(2):
                    l1 = k.side.start("cmp_w1", w1[i][j * HD:(j + 1) * HD, :, :],
                                      w["cmp_w1"][0, j].rearrange("(t d) m -> d t m", d=HD)[:, i * half:(i + 1) * half, :], V.last)
            l2 = k.side.start("cmp_w2", w2[:, :], w["cmp_w2"][0].rearrange("j d m -> (j d) m"))
            l3 = k.side.start("cmp_pos", pos[:, 0:HD], w["cmp_pos"][0, 0])
            l3 = k.side.start("cmp_pos", pos[:, HD:P], w["cmp_pos"][0, 1])
            yield
            bank = k.small.take()
            k.pe.wait(l3, *bank.free)
            m = k.pe.done(T.transpose(bank.t[:, 0:CMP], pos[:, :], k.ident[0:CMP, 0:CMP]))
            pos_t = k.stat(CMP)
            v = V.done(V.after(m).tensor_copy(pos_t, bank.t[:, 0:CMP]))
            bank.free = (v,)
            blocks = cmp_t[:, :].rearrange("p (c t) -> p c t", t=CMP)
            v = V.done(V.after(made["a_q"]).tensor_tensor(blocks, blocks, pos_t.unsqueeze(1).broadcast_to((P, NC, CMP)), ALU.add))
            yield
            hid, hid4 = k.stat(NC), k.stat(NH * NC)
            for j in range(2):
                bank = k.small.take()
                r = slice(j * HD, (j + 1) * HD)
                k.pe.wait(v, l1, *bank.free)
                for t in range(CMP):
                    mm = T.matmul(bank.t[r, 0:NC], w1[t // half][r, t % half, :], blocks[r, :, t], start=t == 0, stop=t == CMP - 1)
                m = k.pe.done(mm)
                a = A.done(A.after(m).activation(hid[r, :], bank.t[r, 0:NC], ACT.Silu))
                bank.free = (a,)
            v = V.done(V.after(a).tensor_copy(hid4[HD:P, :].rearrange("p (h c) -> p h c", h=NH),
                                              hid[HD:P, :].unsqueeze(1).broadcast_to((HD, NH, NC))))
            yield
            kc, vc = k.stat(NC), k_c[0:NH * NC, 0, :]
            b0, b1 = k.small.take(), k.small.take()
            k.pe.wait(a, v, l2, *b0.free, *b1.free)
            m = k.pe.done(T.matmul(b0.t[0:HD, 0:NC], w2[0:HD, :], hid[0:HD, :], start=True, stop=True))
            v0 = V.done(V.after(m).tensor_copy(kc[0:HD, :], b0.t[0:HD, 0:NC]))
            b0.free = (v0,)
            m = k.pe.done(T.matmul(b1.t[0:NH * NC, 0:HD], hid4[HD:P, :], w2[HD:P, :], start=True, stop=True))
            v1 = V.done(V.after(m).tensor_tensor(
                vc.rearrange("p (h d) -> p h d", d=HD),
                b1.t[0:NH * NC, 0:HD].unsqueeze(1).broadcast_to((NH * NC, NH, HD)),
                table("block")[0:NH * NC, :].rearrange("p (h d) -> p h d", d=HD), ALU.mult))
            b1.free = (v1,)
            yield
            bank = k.small.take()
            k.pe.wait(v0, *bank.free)
            for t in range(NT):
                for h in range(NH):
                    c = (t * NH + h) * NC
                    mm = T.matmul(bank.t[:, c:c + NC], q_a[:, h, t * P:(t + 1) * P], kc[0:HD, :],
                                  start=c == 0, stop=True, skip_group_check=True)
            m = k.pe.done(mm)
            g, n = NT * NH, NT * NH * NC
            slot = k.rows_ring.take()
            s = slot.t[:, 0:n]
            s3 = s.rearrange("p (g c) -> p g c", c=NC)
            top, sums, inv = k.stat(g), k.stat(g), k.stat(g)

            def wide(x):
                return x.unsqueeze(2).broadcast_to((P, g, NC))
            v = V.done(V.after(m, *slot.free).scalar_tensor_tensor(s, bank.t[:, 0:n], HD ** -0.5, table("cmp_bias"), ALU.mult, ALU.add))
            bank.free = (v,)
            V.done(V.after().tensor_reduce(top, s3, AX.X, ALU.max))
            v = V.done(V.after().tensor_tensor(s3, s3, wide(top), ALU.subtract))
            a = A.done(A.after(v).activation(s, s, ACT.Exp))
            V.done(V.after(a).tensor_tensor(s, s, table("cmp_mask"), ALU.mult))
            V.done(V.after().tensor_reduce(sums, s3, AX.X, ALU.add))
            V.done(V.after().tensor_scalar(sums, sums, TINY, None, ALU.max))
            V.done(V.after().reciprocal(inv, sums))
            gg = gates[:, :, :].rearrange("p t (h c) -> p (t h) c", c=3)[:, :, 0]
            V.done(V.after().tensor_tensor(inv, inv, gg, ALU.mult))
            v = V.done(V.after().tensor_tensor(s3, s3, wide(inv), ALU.mult))
            yield
            bank, turned = k.small.take(), k.turned.take()
            k.pe.wait(v, *bank.free)
            half = NH * NC
            for t in range(NT):
                tr = T.transpose(bank.t[0:half, t * P:(t + 1) * P], s[:, t * half:(t + 1) * half], k.ident)
            m = k.pe.done(tr)
            slot.free = (m,)
            a = A.done(A.after(m, *turned.free).activation(turned.t[0:half, 0:S], bank.t[0:half, 0:S], ACT.Copy))
            bank.free = (a,)
            yield
            bank = k.small.take()
            k.pe.wait(a, v1, *bank.free)
            for t in range(NT):
                mm = T.matmul(bank.t[:, t * BW:(t + 1) * BW], turned.t[0:half, t * P:(t + 1) * P], vc,
                              start=t == 0, stop=True, skip_group_check=True)
            m = k.pe.done(mm)
            turned.free = (m,)
            v = V.done(V.after(m).tensor_tensor(y[:, :, :], y[:, :, :], bank.t[:, :].rearrange("p (t n) -> p t n", t=NT), ALU.add))
            bank.free = (v,)

        def chain(*gens):
            for g in gens:
                yield from g

        def all_of(gen):
            for _ in gen:
                pass

        all_of(qk_block(q_d, k_d, "d_qk"))
        all_of(k.columns(k.H, KT, vz_block(v_d, z["d"], "d_v")))
        k.pe.wait(made["d_v"])
        y = y_ring.take()
        A.wait(*y.free)
        k.run([retention(h, y.t) for h in range(NH)],
              chain(qk_block(q_c, k_c, "c_qk"), k.columns(k.H, KT, vz_block(v_c, z["c"], "c_v"))))
        finish("d", y, retention_norm(y.t), y_op[0])

        k.pe.wait(made["c_v"])
        A.wait(k.pe.last, V.last)
        y = y_ring.take()
        A.wait(*y.free)
        k.run([stick(h, y.t) for h in range(NH)], chain(block_c3(), block_c2(), merge(3, y_op[0])))
        finish("c", y, made["y_c"], y_op[1])

        k.pe.wait(made["b_v"], made["b_q"])
        y = y_ring.take()
        V.wait(*y.free)
        k.run([softmax_group(q_b, lambda h: k_b[:, h // 2, :], lambda h, j: v_b[:, j, (h // 2) * HD:(h // 2 + 1) * HD],
                             "window", hs, t, made["b_q"], Out(y.t, True, use_sink=True)) for hs, t in groups],
              chain(block_c1(), block_c0(), merge(2, y_op[1])))
        finish("b", y, V.last, y_op[0])

        k.pe.wait(made["a_kv"], made["a_q"])
        V.wait(made["a_kv"], k.pe.last)
        y = y_ring.take()
        V.wait(*y.free)
        k.run([softmax_group(q_a, lambda h: kk[:, :], lambda h, j: vv[:, j, :], "alibi", hs, t, made["a_q"], Out(y.t, first, gi))
               for kk, vv, gi, first in ((k_sel, v_sel, 1, True),) for hs, t in groups]
              + [compressed(y.t)]
              + [softmax_group(q_a, lambda h: k_win[:, :], lambda h, j: v_win[:, j, :], "alibi", hs, t, made["a_q"], Out(y.t, False, 2))
                 for hs, t in groups],
              merge(1, y_op[0]))
        finish("a", y, V.last, y_op[1])
        all_of(merge(0, y_op[1]))

        for t in range(NT):
            k.transposed(merged[:, t, :], [P * i for i in range(KT)], k.H, 0, t, made["merged"])

        def to_x(n, t, bank, m):
            at, part = slice(n * CN, (n + 1) * CN), sig.slots[n].t[:, t, :]
            v = V.done(V.after(m, gate_mark).tensor_tensor(part, bank.t[:, :], gate[:, at], ALU.mult))
            bank.free = (v,)
            k.x_marks = [V.done(V.after().tensor_tensor(k.X[:, t, at], k.X[:, t, at], part, ALU.add))]
        all_of(k.square(k.H, to_x))
        k.everyone()
    k.phase = k.ctx


ORDER = (3, 2, 1, 0)



def drain(gen):
    for _ in gen:
        pass


def memory_keys(k, layer, mem, keys, values, made):
    for n in range(D // CN):
        def to_keys(banks, m):
            for b in range(2):
                a = k.act.done(k.act.after(m).activation(keys[:, 4 * n + 2 * b:4 * n + 2 * b + 2, :],
                                                         banks[b].t[:, :].rearrange("p (k n) -> p k n", n=S), ACT.Copy))
                banks[b].free = (a,)
            made["keys", layer] = a
        yield from k.block(mem, KT, [(i // 2, S * (i % 2), None, P * i, P) for i in range(4)], to_keys)
    for n in range(D // CN):
        yield from k.columns(mem, KT, k.copy_to(lambda t: values[:, t, n * CN:(n + 1) * CN]))
    made["values", layer] = k.copied


def memory_attention(k, layer, keys, values, made):
    V, A, T = k.vec, k.act, k.nc.tensor
    norm = k.next_norm
    k.rows_ring, k.turned = k.ring(f"mrows{layer}_", 3, [P, 512]), k.ring(f"mturned{layer}_", 2, [P, 512])
    q = k.sb(f"q_mem{layer}", [P, KT, S])
    o = Operand(*k.pair(f"o_mem{layer}", KT))

    def q_block(n):
        def to_q(banks, m):
            for b in range(2):
                a = A.done(A.beside(m).activation(q[:, 4 * n + 2 * b:4 * n + 2 * b + 2, :],
                                                  banks[b].t[:, :].rearrange("p (k n) -> p k n", n=S), ACT.Copy))
                banks[b].free = (a,)
            made["q", n] = a
        return k.block(k.H, KT, [(i // 2, S * (i % 2), None, P * i, P) for i in range(4)], to_q)
    drain(q_block(0))
    scale = (D // MH) ** -0.5
    norm.root(0)
    scales, neg_scales = k.stat(NT), k.stat(NT)
    V.done(V.after().tensor_scalar(scales, norm.roots, scale, None, ALU.mult))
    scale_mark = V.done(V.after().tensor_scalar(neg_scales, norm.roots, -scale, None, ALU.mult))

    def head(h):
        bank, slot = k.small.take(), k.rows_ring.take()
        k.pe.wait(made["q", h // 2], made["keys", layer], *bank.free)
        for t in range(NT):
            for j in range(MHT):
                kt = h * MHT + j
                mm = T.matmul(bank.t[:, t * S:(t + 1) * S], q[:, kt, t * P:(t + 1) * P], keys[:, kt, :],
                              start=t == 0 and j == 0, stop=True, skip_group_check=True)
        m = k.pe.done(mm)
        s = slot.t[:, :].rearrange("p (t n) -> p t n", t=NT)
        ps = bank.t[:, :].rearrange("p (t n) -> p t n", t=NT)
        top, neg, sums, inv = k.stat(NT), k.stat(NT), k.stat(NT), k.stat(NT)
        v = V.done(V.beside(m).tensor_reduce(top, ps, AX.X, ALU.max))
        v = V.done(V.after().tensor_tensor(neg, top, neg_scales, ALU.mult))
        A.wait(v, scale_mark, *slot.free)
        for t in range(NT):
            a = A.done(A.beside().activation(s[:, t, :], ps[:, t, :], ACT.Exp, bias=neg[:, t:t + 1], scale=scales[:, t:t + 1],
                                             accum_out=sums[:, t:t + 1]))
        bank.free = (a,)
        V.done(V.beside(a).reciprocal(inv, sums))
        v = V.done(V.after().tensor_tensor(s, s, inv.unsqueeze(2).broadcast_to((P, NT, S)), ALU.mult))
        yield
        turned, tm = k.turn([s[:, t, j * P:(j + 1) * P] for j in range(2) for t in range(NT)], v, slot)
        yield
        bank = k.small.take()
        k.pe.wait(tm, made["values", layer], *bank.free)
        for f in range(MHT):
            c = (h * MHT + f) * P
            for j in range(2):
                mm = T.matmul(bank.t[:, f * S:(f + 1) * S], values[:, j, c:c + P], turned.t[:, j * S:(j + 1) * S],
                              start=f == 0 and j == 0, stop=True, skip_group_check=True)
        m = k.pe.done(mm)
        turned.free = (m,)
        at = slice(h * MHT, (h + 1) * MHT)
        v = k.split_operand(bank.t[:, :].rearrange("p (k n) -> p k n", n=S), m, o.high[:, at, :], o.low[:, at, :])
        bank.free = (v,)
        o.ready[h // 2] = (v,)

    def fill():
        yield from q_block(1)
        yield
        yield from k.square(o, k.add_to_x)
    k.next_norm = Norm(k, "norm_ffn_2", layer, 1)
    k.run([head(h) for h in range(MH)], fill())


def feed_forward(k, layer, following):
    V, A = k.vec, k.act
    with ExitStack() as phase:
        k.phase = phase
        norm = k.next_norm
        hidden = Operand(*k.pair(f"hidden{layer}", FT))
        mids = k.ring(f"mid{layer}_", 2, [P, NT, CN])

        def up_to(slot, n):
            def evacuate(t, bank, m):
                w = slot.w
                v = V.done(V.beside(m, slot.gated).scalar_tensor_tensor(slot.t[:, t, 0:w], bank.t[:, slot.at:slot.at + w], norm.root(t),
                                                                        slot.t[:, t, 0:w], ALU.mult, ALU.mult))
                bank.free = (v,)

                def turn():
                    k.transposed(slot.t[:, t, :], [P * i for i in range(w // P)], hidden, n * (CN // P), t, v)
                    slot.free = (k.pe.last,)
                k.late.append(turn)
            return evacuate
        full = FF // CN
        for n in range(full):
            slot = mids.take()
            slot.w, slot.at = CN, 0

            def gate_to(t, bank, m):
                A.wait(*slot.free)
                k.copy_to(lambda t: slot.t[:, t, :], ACT.Silu, norm.root)(t, bank, m)
                slot.gated = k.copied
            drain(k.columns(k.H, KT, gate_to))
            drain(k.columns(k.H, KT, up_to(slot, n)))
        slot = mids.take()
        slot.w, slot.at = FF - full * CN, FF - full * CN

        def last(t, bank, m):
            A.wait(*slot.free)
            a = A.done(A.beside(m).activation(slot.t[:, t, 0:slot.w], bank.t[:, 0:slot.w], ACT.Silu, scale=norm.root(t)))
            slot.gated = a
            up_to(slot, full)(t, bank, m)
        drain(k.columns(k.H, KT, last))
        k.next_norm = following()
        for n in range(D // CN):
            drain(k.columns(hidden, FT, k.add_block(n)))
        k.everyone()
    k.phase = k.ctx


def conv_layer(k, w, mem, kv, made):
    V, A, T = k.vec, k.act, k.nc.tensor
    with ExitStack() as phase:
        k.phase = phase
        pad = TAPS - 1
        u, y = k.sb("conv_in", [P, KT, pad + S]), k.sb("conv_out", [P, KT, S])
        taps = k.sb("taps", [P, KT, TAPS])
        tap_rows = k.sb("tap_rows", [TAPS, D])
        sig = k.ring("glu", 2, [P, 2, S])
        diagonals = k.ring("diagonal", 3, [P, 4, P])
        mean_of, diag_root = k.sb("mean_of", [P, P]), k.sb("diag_root", [P, NT, P])
        variance = k.sb("ln_variance", [P, S])
        taps_mark = k.side.start("taps", tap_rows[:, :], w["conv_w_dw_2"][0])
        b2_mark = k.load_gain("conv_b_pw2_2", 0, 1)
        k.norm_operand(k.x_marks, k.G[0].t[:, :], k.load_gain("norm_mix_2", 0), k.H)
        k.next_norm = Norm(k, "norm_mem_2", 0)
        V.done(V.after().memset(u[:, :, 0:pad], 0.0))
        mean_mark = V.done(V.after().memset(mean_of[:, :], 1.0 / D))
        for g in range(0, KT, 4):
            bank = k.small.take()
            k.pe.wait(taps_mark, *bank.free)
            for i in range(4):
                tr = T.transpose(bank.t[:, i * P:i * P + TAPS], tap_rows[:, (g + i) * P:(g + i + 1) * P], k.ident[0:TAPS, 0:TAPS])
            m = k.pe.done(tr)
            v = V.done(V.after(m).tensor_copy(taps[:, g:g + 4, :], bank.t[:, :].rearrange("p (k n) -> p k n", n=P)[:, :, 0:TAPS]))
            bank.free = (v,)
        A.wait(v)
        for t in range(NT):
            V.done(V.after(b2_mark).tensor_tensor(k.X[:, t, :], k.X[:, t, :], k.G[1].t[:, :], ALU.add))

        ready, marks = {}, {}

        def tap_steps(tiles):
            for tap in range(TAPS):
                for i, f in enumerate(tiles):
                    if tap > 0 and i % 2 == 0:
                        V.wait(marks[tiles[min(i + 1, len(tiles) - 1)]])
                    src, wt = u[:, f, tap:tap + S], taps[:, f, tap:tap + 1]
                    if tap == 0:
                        marks[f] = V.done(V.beside(ready[f]).tensor_scalar(y[:, f, :], src, wt, k.vcol["b_dw"][:, f:f + 1], ALU.mult, ALU.add))
                    else:
                        marks[f] = V.done(V.beside(marks[f]).scalar_tensor_tensor(y[:, f, :], src, wt, y[:, f, :], ALU.mult, ALU.add))
                    yield

        def tap_products(f):
            bank = k.small.take()
            k.pe.wait(ready[f], *bank.free)
            groups = [range(g, min(g + 4, TAPS)) for g in range(0, TAPS, 4)]

            def diagonal(group):
                slot = diagonals.take()
                A.wait(*slot.free)
                for i, tap in enumerate(group):
                    a = A.done(A.beside().activation(slot.t[:, i, :], k.ident, ACT.Copy, scale=taps[:, f, tap:tap + 1]))
                return slot, a
            made_d = [diagonal(g) for g in groups[:2]]
            yield
            for n, group in enumerate(groups):
                slot, a = made_d[n]
                k.pe.wait(a)
                for i, tap in enumerate(group):
                    mm = T.matmul(bank.t[:, 0:S], slot.t[:, i, :], u[:, f, tap:tap + S], start=tap == 0, stop=tap == TAPS - 1)
                m = k.pe.done(mm)
                slot.free = (m,)
                if n + 2 < len(groups):
                    made_d.append(diagonal(groups[n + 2]))
                if n % 2:
                    yield
            marks[f] = V.done(V.beside(m).tensor_scalar(y[:, f, :], bank.t[:, 0:S], k.vcol["b_dw"][:, f:f + 1], None, ALU.add))
            bank.free = (marks[f],)

        def chain(*gens):
            for g in gens:
                yield from g

        def steps(gen, n):
            for _ in range(n):
                next(gen, None)
        on_pe = 3
        vec_taps = chain(tap_steps([0, 1]), tap_steps(list(range(2, KT - on_pe))))
        fill = memory_keys(k, 0, mem, *kv, made)
        for n in range(KT // 2):
            def evacuate(banks, m):
                slot = sig.take()
                for i in range(2):
                    f = 2 * n + i
                    a = A.done(A.after(m, *slot.free).activation(slot.t[:, i, :], banks[1].t[:, i * S:(i + 1) * S], ACT.Sigmoid,
                                                                bias=k.vcol["b_pw1"][:, KT + f:KT + f + 1]))
                for i in range(2):
                    f = 2 * n + i
                    v = V.done(V.beside(m, a).scalar_tensor_tensor(u[:, f, pad:pad + S], banks[0].t[:, i * S:(i + 1) * S],
                                                                   k.vcol["b_pw1"][:, f:f + 1], slot.t[:, i, :], ALU.add, ALU.mult))
                    ready[f] = v
                banks[1].free, banks[0].free, slot.free = (a,), (v,), (v,)
            for _ in k.block(k.H, KT, [(0, 0, None, 0, P), (0, S, None, P, P), (1, 0, None, 2 * P, P), (1, S, None, 3 * P, P)], evacuate):
                if n:
                    steps(vec_taps, 5)
        pe_taps = chain(*(tap_products(f) for f in range(KT - on_pe, KT)))
        rounds = on_pe * (1 + TAPS // 8)
        for i in range(rounds):
            next(pe_taps, None)
            if i % 3 == 1:
                next(fill, None)
            steps(vec_taps, 9)
        drain(pe_taps)
        drain(vec_taps)

        halves = [slice(h * CK, (h + 1) * CK) for h in range(2)]
        order = [*range(KT - on_pe, KT), *range(KT - on_pe)]
        bank = k.small.take()
        k.pe.wait(mean_mark, *bank.free)
        for f in order:
            k.pe.wait(marks[f])
            mm = T.matmul(bank.t[:, 0:S], mean_of[:, :], y[:, f, :], start=f == order[0], stop=f == order[-1])
        m = k.pe.done(mm)
        sq, sq_marks = k.HN[:, :, :].rearrange("p t (k n) -> p (t k) n", n=S), []
        A.wait(*k.hn_free)
        for at in halves:
            v = V.done(V.beside(m).tensor_tensor(y[:, at, :], y[:, at, :], bank.t[:, 0:S].unsqueeze(1).broadcast_to((P, CK, S)), ALU.subtract))
            sq_marks.append(A.done(A.beside(v).activation(sq[:, at, :], y[:, at, :], ACT.Square)))
        bank.free = (v,)
        next(fill, None)
        bank = k.small.take()
        k.pe.wait(*bank.free)
        for f in range(KT):
            k.pe.wait(sq_marks[f // CK])
            mm = T.matmul(bank.t[:, 0:S], mean_of[:, :], sq[:, f, :], start=f == 0, stop=f == KT - 1)
        m = k.pe.done(mm)
        k.hn_free = (m,)
        v = V.done(V.beside(m).tensor_scalar(variance[:, :], bank.t[:, 0:S], LN_EPS, None, ALU.add))
        bank.free = (v,)
        bank, root = k.small.take(), k.stat(NT)
        k.pe.wait(v, *bank.free)
        for t in range(NT):
            mm = T.matmul(bank.t[:, t:t + 1], variance[:, t * P:(t + 1) * P], k.ident[:, 0:1], start=t == 0, stop=True, skip_group_check=True)
        m = k.pe.done(mm)
        next(fill, None)
        v = V.done(V.beside(m).tensor_copy(root, bank.t[:, 0:NT]))
        bank.free = (v,)
        p = k.pool.done(k.pool.after(v).tensor_tensor(root, root, k.half[:, 0:NT], ALU.pow))
        for t in range(NT):
            v = V.done(V.beside(p).tensor_scalar(diag_root[:, t, :], k.ident, root[:, t:t + 1], None, ALU.mult))
        bank = k.small.take()
        k.pe.wait(v, *bank.free)
        m = k.pe.done(T.matmul(bank.t[:, 0:S], k.ones, diag_root[:, :, :].rearrange("p t n -> p (t n)"), start=True, stop=True))
        wide_root = bank.t[:, 0:S].unsqueeze(1).broadcast_to((P, CK, S))
        o = k.H
        for h, at in enumerate(halves):
            v = V.done(V.beside(m).tensor_tensor(y[:, at, :], y[:, at, :], wide_root, ALU.mult))
            A.wait(v)
            for f in range(h * CK, (h + 1) * CK):
                a = A.done(A.beside().activation(y[:, f, :], y[:, f, :], ACT.Silu, scale=k.vcol["ln_g"][:, f:f + 1], bias=k.vcol["ln_b"][:, f:f + 1]))
            halves[h] = (at, a)
        bank.free = (v,)
        for h, (at, a) in enumerate(halves):
            v = V.done(V.beside(a, *o.free[h]).tensor_copy(o.high[:, at, :], y[:, at, :]))
            o.ready[h] = (V.done(V.after(v).tensor_tensor(o.low[:, at, :], y[:, at, :], o.high[:, at, :].bitcast(F32), ALU.subtract)),)
        drain(fill)
        ended = k.so_far()
        drain(k.square(o, k.add_to_x))
        k.hand_over(ended)
    k.phase = k.ctx


def rope_tables(k, w, cos, sin):
    V, A, n = k.vec, k.act, ROT // 2
    raw, pos = k.sb("positions", [P, NT], I32), k.stat(NT)
    with k.nc.allow_non_contiguous_dma(reason="256 numbers, a row of partitions each"):
        l = k.side.start("positions", raw[:, :], w["positions_2"][0].rearrange("(t p) -> p t", p=P))
    V.done(V.after(l).tensor_copy(pos, raw[:, :]))
    step = 1.5 * 2.0 ** 23
    ang, turns, r = k.stat(NT * n), k.stat(NT * n), k.stat(NT * n)
    for t in range(NT):
        V.done(V.after().tensor_scalar(ang[:, t * n:(t + 1) * n], k.invfreq, pos[:, t:t + 1], None, ALU.mult))
    c1 = 6.28125
    c2 = round((TWO_PI - c1) * 2.0 ** 20) / 2.0 ** 20
    c3 = TWO_PI - c1 - c2
    for dst, quarter in ((cos, 0.25), (sin, 0.0)):
        V.done(V.after().tensor_scalar(turns, ang, 1.0 / TWO_PI, quarter, ALU.mult, ALU.add))
        V.done(V.after().tensor_scalar(turns, turns, step, None, ALU.add))
        V.done(V.after().tensor_scalar(turns, turns, step, None, ALU.subtract))
        V.done(V.after().scalar_tensor_tensor(r, turns, -c1, ang, ALU.mult, ALU.add))
        V.done(V.after().scalar_tensor_tensor(r, turns, -c2, r, ALU.mult, ALU.add))
        V.done(V.after().scalar_tensor_tensor(r, turns, -c3, r, ALU.mult, ALU.add))
        V.done(V.after().tensor_scalar(r, r, quarter * TWO_PI, 3.1415925, ALU.add, ALU.min))
        v = V.done(V.after().tensor_scalar(r, r, -3.1415925, None, ALU.max))
        a = A.done(A.after(v).activation(dst, r, ACT.Sin))
        V.wait(a)
    return a


def differential_layer(k, w, mem, kv, made):
    V, A, T = k.vec, k.act, k.nc.tensor
    with ExitStack() as phase:
        k.phase = phase
        norm = k.next_norm
        vals, out = k.sb("vals", [P, NT, D]), k.sb("attended", [P, NT, D])
        tok = out
        qt, kt_ = k.sb("q_t", [P, DH, S]), k.sb("k_t", [P, DH, S])
        k.rows_ring = k.ring("drows", 4, [P, 512])
        k.turned = k.ring("dturned", 2, [P, 512])
        cos, sin = k.stat(NT * ROT // 2), k.stat(NT * ROT // 2)
        rope_tables(k, w, cos, sin)
        lrow = k.sb("lambda_rows", [P, 4, HD])
        for i, n in enumerate(("q1", "k1", "q2", "k2")):
            l = k.row("lambda", lrow[:, i, :], w[f"diff_lambda_{n}_2"][0])
        e, neg_lam = k.stat(2), k.stat(1)
        V.done(V.after(l).tensor_tensor(lrow[:, 0, :], lrow[:, 0, :], lrow[:, 1, :], ALU.mult))
        V.done(V.after().tensor_tensor(lrow[:, 1, :], lrow[:, 2, :], lrow[:, 3, :], ALU.mult))
        v = V.done(V.after().tensor_reduce(e, lrow[:, 0:2, :], AX.X, ALU.add))
        a = A.done(A.after(v).activation(e, e, ACT.Exp))
        V.done(V.after(a).tensor_tensor(neg_lam, e[:, 1:2], e[:, 0:1], ALU.subtract))
        V.done(V.after().tensor_scalar(neg_lam, neg_lam, LAMBDA_INIT, None, ALU.subtract))
        tok_free = [()]

        def rotate(t, n, mark):
            r, nh = ROT // 2, DH
            heads = tok[:, t, n * CN:(n + 1) * CN].rearrange("p (h d) -> p h d", d=HD)
            r1, r2 = heads[:, :, 0:r], heads[:, :, r:2 * r]
            c = cos[:, t * r:(t + 1) * r].unsqueeze(1).broadcast_to((P, nh, r))
            s = sin[:, t * r:(t + 1) * r].unsqueeze(1).broadcast_to((P, nh, r))
            slot = k.rows_ring.take()
            q4 = slot.t[:, 0:4 * nh * r].rearrange("p (f h d) -> p f h d", f=4, d=r)
            V.done(V.after(mark, *slot.free).tensor_tensor(q4[:, 0], r1, c, ALU.mult))
            V.done(V.beside().tensor_tensor(q4[:, 1], r2, s, ALU.mult))
            V.done(V.beside().tensor_tensor(q4[:, 2], r1, s, ALU.mult))
            V.done(V.beside().tensor_tensor(q4[:, 3], r2, c, ALU.mult))
            V.done(V.after().tensor_tensor(r1, q4[:, 0], q4[:, 1], ALU.subtract))
            v = V.done(V.beside().tensor_tensor(r2, q4[:, 2], q4[:, 3], ALU.add))
            slot.free = (v,)
            return v

        def to_heads(dst, name):
            def evacuate(n, t, bank, m):
                A.wait(*tok_free[0])
                k.copy_to(lambda t: tok[:, t, n * CN:(n + 1) * CN], scale_of=norm.root)(t, bank, m)
                v = rotate(t, n, k.copied)

                def turn():
                    g, bank = n * CK, k.small.take()
                    k.pe.wait(v, *bank.free)
                    for i in range(4):
                        tr = T.transpose(bank.t[:, i * P:(i + 1) * P], tok[:, t, (g + i) * P:(g + i + 1) * P], k.ident)
                    m = k.pe.done(tr)
                    a = A.done(A.beside(m).activation(dst[:, g:g + 4, t * P:(t + 1) * P],
                                                      bank.t[:, :].rearrange("p (k n) -> p k n", n=P), ACT.Copy))
                    bank.free = (a,)
                    made[name] = a
                    if n == 1 and t == 1:
                        tok_free[0] = (m,)
                k.late.append(turn)
            return evacuate
        drain(k.square(k.H, to_heads(kt_, "k")))
        q_norm = Norm(k, "norm_mix_2", 1, 1)

        def to_vals(n, t, bank, m):
            k.copy_to(lambda t: vals[:, t, n * CN:(n + 1) * CN], scale_of=norm.root)(t, bank, m)
            made["v"] = k.copied
            if t == 1:
                for tt in range(NT):
                    q_norm.take(n, tt, None, squares=False)
        drain(k.square(k.H, to_vals))
        drain(k.square(k.H, to_heads(qt, "q")))
        k.flush()
        k.pe.wait(made["k"], made["v"], made["q"])
        scale = HD ** -0.5
        causal = k.causal

        def group(heads, t):
            nh, nk = len(heads), P * (t + 1)
            parts = []
            for c in range(2):
                r = slice(c * HD, (c + 1) * HD)
                bank, slot = k.small.take(), k.rows_ring.take()
                k.pe.wait(*bank.free)
                for i, h in enumerate(heads):
                    mm = T.matmul(bank.t[:, i * nk:(i + 1) * nk], qt[r, h, t * P:(t + 1) * P], kt_[r, h, 0:nk],
                                  start=i == 0, stop=True, skip_group_check=True)
                m = k.pe.done(mm)
                s = slot.t[:, :].rearrange("p (h n) -> p h n", n=nk)
                mask = causal[:, 2 * P - nk:2 * P].unsqueeze(1).broadcast_to((P, nh, nk))
                top, neg, sums = k.stat(nh), k.stat(nh), k.stat(nh)
                v = V.done(V.after(m, *slot.free).tensor_tensor(s, bank.t[:, :].rearrange("p (h n) -> p h n", n=nk), mask, ALU.add))
                bank.free = (v,)
                V.done(V.after().tensor_reduce(top, s, AX.X, ALU.max))
                v = V.done(V.after().tensor_scalar(neg, top, -scale, None, ALU.mult))
                A.wait(v)
                for i in range(nh):
                    a = A.done(A.beside().activation(s[:, i, :], s[:, i, :], ACT.Exp, bias=neg[:, i:i + 1], scale=scale, accum_out=sums[:, i:i + 1]))
                parts.append((slot, s, sums, a))
            yield
            (slot0, s0, sum0, _), (slot1, s1, sum1, a) = parts
            V.done(V.after(a).reciprocal(sum0, sum0))
            V.done(V.after().reciprocal(sum1, sum1))
            V.done(V.after().tensor_scalar(sum1, sum1, neg_lam, None, ALU.mult))
            for i in range(nh):
                V.done(V.after().tensor_scalar(s0[:, i, :], s0[:, i, :], sum0[:, i:i + 1], None, ALU.mult))
            for i in range(nh):
                v = V.done(V.after().scalar_tensor_tensor(s0[:, i, :], s1[:, i, :], sum1[:, i:i + 1], s0[:, i, :], ALU.mult, ALU.add))
            slot1.free = (v,)
            turned, tm = k.turn([s0[:, i, j * P:(j + 1) * P] for i in range(nh) for j in range(t + 1)], v, slot0)
            yield
            bank = k.small.take()
            k.pe.wait(tm, *bank.free)
            for i, h in enumerate(heads):
                for j in range(t + 1):
                    b = i * (t + 1) + j
                    mm = T.matmul(bank.t[:, i * P:(i + 1) * P], turned.t[:, b * P:(b + 1) * P], vals[:, j, h * P:(h + 1) * P],
                                  start=b == 0, stop=True, skip_group_check=True)
            m = k.pe.done(mm)
            turned.free = (m,)
            a = A.done(A.after(m).activation(out[:, t, heads[0] * P:(heads[0] + nh) * P], bank.t[:, 0:nh * P], ACT.Copy))
            bank.free = (a,)
            made["out"] = a
        def finish_half(half):
            hs, at = DH // 2, slice(half * CN, (half + 1) * CN)
            for t in range(NT):
                o_t = out[:, t, at].rearrange("p (h d) -> p h d", d=P)
                sums, slot = k.stat(hs), k.rows_ring.take()
                V.done(V.after(made["out"], *slot.free).tensor_tensor(slot.t[:, :], out[:, t, at], out[:, t, at], ALU.mult))
                v = V.done(V.after().tensor_reduce(sums, slot.t[:, :].rearrange("p (h d) -> p h d", d=P), AX.X, ALU.add))
                slot.free = (v,)
                r, m = k.inverse_root(sums, P, 1e-5, v, 1.0 - LAMBDA_INIT)
                v = V.done(V.after(m).tensor_tensor(o_t, o_t, r.unsqueeze(2).broadcast_to((P, hs, P)), ALU.mult))
                yield
                k.transposed(out[:, t, :], [half * CN + P * i for i in range(CK)], k.H, half * CK, t, v, scale=k.vcol["subln_g"])

        def half_groups(h0):
            return [group([h0, h0 + 1], 1), group([h0 + 2, h0 + 3], 1), group([h0, h0 + 1, h0 + 2, h0 + 3], 0)]

        def fill():
            yield from memory_keys(k, 1, mem, *kv, made)
        k.next_norm = Norm(k, "norm_mem_2", 1)
        k.run(half_groups(0) + half_groups(4), fill())
        drain(finish_half(0))
        drain(finish_half(1))
        drain(k.square(k.H, k.add_to_x))
        k.everyone()
    k.phase = k.ctx


def chunks(w, tiles, cols):
    view = w.rearrange("(k p) n -> p k n", p=P)
    return [([(view[:, f:min(f + CK, tiles), c:c + n], n) for c, n in cols], min(CK, tiles - f)) for f in range(0, tiles, CK)]


def weight_plan(w):
    plan = []

    def add(m, *blocks, tiles=KT):
        for cols in blocks:
            plan.extend(chunks(m, tiles, cols))

    def square(m):
        for f in range(0, KT, CK):
            for c in range(0, D, CN):
                plan.append(chunks(m, KT, [(c, CN)])[f // CK])

    def even(m, tiles=KT):
        add(m, *[[(c, CN)] for c in range(0, D, CN)], tiles=tiles)

    ada, w_in = w["w_ada"][0], w["w_in"][0]
    add(ada, *[[(c, CN)] for c in (D, D + CN, 0, CN, 2 * D, 2 * D + CN)])
    add(w_in, [(W_D_Q, 512)], [(W_D_V, 512)], [(W_C_Q, 512)], [(W_C_V, 512)])
    add(w_in, [(W_B_K, 512)], [(W_A_Z, 512)])

    def merge(i):
        for c in range(0, D, CN):
            add(w["w_merge"][0, i], [(c, CN)])
            add(w["w_br"][0, i], [(c, CN)], tiles=BW // P)
    merge(3)
    add(w_in, [(W_A_KV + 2 * HD, 268)], [(W_A_Q, 384)])
    merge(2)
    merge(1)
    merge(0)
    square(w["w_out"][0])

    pw1 = w["conv_w_pw1_2"][0]
    add(pw1, *[[(c, S), (D + c, S)] for c in range(0, D, S)])

    def memory(layer):
        even(w["mem_w_k_2"][layer])
        even(w["mem_w_v_2"][layer])

    def memory_use(layer):
        even(w["mem_w_q_2"][layer])
        square(w["mem_w_o_2"][layer])

    def feed(layer):
        g, u, d = w["ffn_w_gate_2"][layer], w["ffn_w_up_2"][layer], w["ffn_w_down_2"][layer]
        for c in range(0, FF - CN + 1, CN):
            add(g, [(c, CN)])
            add(u, [(c, CN)])
        c = FF // CN * CN
        gv, uv = (m.rearrange("(k p) n -> p k n", p=P) for m in (g, u))
        for f in range(0, KT, CK):
            plan.append(([(gv[:, f:f + CK, c:FF], FF - c), (uv[:, f:f + CK, c:FF], FF - c)], CK))
        even(d, tiles=FT)
    memory(0)
    square(w["conv_w_pw2_2"][0])
    memory_use(0)
    feed(0)
    square(w["w_k_shared_2"])
    square(w["w_v_shared_2"])
    square(w["diff_w_q_2"][0])
    memory(1)
    square(w["diff_w_o_2"][0])
    memory_use(1)
    feed(1)
    return plan


def build(nc, w, out):
    with ExitStack() as ctx:
        k = Kernel(nc, ctx, w)
        common = k.sb("common", [P, COMMON_W])
        common_mark = k.side.start("common", common[:, :], w["common_constants"])

        def const(name):
            at, n = COMMON[name]
            return common[:, at:at + n]
        k.ident, k.ones, k.causal, k.invfreq, k.half = (const(n) for n in ("ident", "ones", "causal", "invfreq", "half"))
        k.X, k.HN = k.sb("X", [P, NT, D]), k.sb("HN", [P, NT, D])
        k.G = [Slot(k.sb(f"gain{i}", [P, D])) for i in range(2)]
        k.H = Operand(*k.pair("H", KT))
        k.next_norm = None
        k.hn_free, k.x_marks, made = (), [], {}
        k.x_loaded = k.side.start("x", k.X[:, :, :], w["x"][0].rearrange("(t p) n -> p t n", p=P))
        vectors = [("c", w["c"][0]), ("b_pw1", w["conv_b_pw1_2"][0]), ("b_dw", w["conv_b_dw_2"][0]),
                   ("ln_g", w["conv_ln_g_2"][0]), ("ln_b", w["conv_ln_b_2"][0]), ("subln_g", w["diff_subln_g_2"][0])]
        n_rows = sum(v.shape[0] // P for _, v in vectors)
        rows, cols, at = k.sb("vector_rows", [n_rows, P]), k.sb("vector_cols", [P, n_rows]), 0
        k.vcol = {}
        for name, v in vectors:
            n = v.shape[0] // P
            loaded = k.side.start("vectors", rows[at:at + n, :], v.rearrange("(k p) -> k p", p=P))
            k.vcol[name] = cols[:, at:at + n]
            at += n
        k.weights = Weights(k, weight_plan(w))
        bank = k.small.take()
        k.pe.wait(common_mark, loaded)
        k.pool.wait(common_mark)
        k.vec.wait(common_mark)
        m = k.pe.done(nc.tensor.transpose(bank.t[:, 0:n_rows], rows[:, :], k.ident[0:n_rows, 0:n_rows]))
        k.columns_ready = k.vec.done(k.vec.after(m).tensor_copy(cols[:, :], bank.t[:, 0:n_rows]))
        bank.free = (k.columns_ready,)
        k.act.wait(k.columns_ready)

        first_block(k, w)

        gain = k.load_gain("final_g", None)
        k.x_marks = k.normed(k.x_marks, k.G[0].t[:, :], gain, k.X)
        with ExitStack() as phase:
            k.phase = phase
            k.junk = k.sb("junk", [P, CN])
            mem = Operand(*k.pair("mem", KT))
            loaded = k.side.start("mem", k.HN[:, :, :], w["mem_2"][0].rearrange("(t p) n -> p t n", p=P), k.vec.last, *k.hn_free)
            for t in range(NT):
                k.transposed(k.HN[:, t, :], [P * i for i in range(KT)], mem, 0, t, loaded)
            k.hn_free = (k.pe.last,)
            for layer in range(2):
                with ExitStack() as kv_phase:
                    k.phase = kv_phase
                    kv = k.sb(f"mem_keys{layer}", [P, KT, S]), k.sb(f"mem_values{layer}", [P, NT, D])
                    (conv_layer, differential_layer)[layer](k, w, mem, kv, made)
                    with ExitStack() as inner:
                        k.phase = inner
                        memory_attention(k, layer, *kv, made)
                        k.everyone()
                feed_forward(k, layer, (lambda: Norm(k, "kv_norm_2", None)) if layer == 0 else (lambda: None))
        gain = k.load_gain("norm_final_2", None)
        marks = k.normed(k.x_marks, k.G[0].t[:, :], gain, k.HN)
        for t in range(NT):
            stored = k.stream.start("result", out[0, t * P:(t + 1) * P, :], k.HN[:, t, :], marks[t])
        k.stream.lane.wait(stored)


_INS = ["x", "c", "w_ada", "b_ada", "norm_g", "w_in", "cmp_pos", "cmp_w1", "cmp_w2", "sink", "w_merge", "w_br", "w_out",
        "final_g", "mem_2", "positions_2", "norm_mix_2", "norm_mem_2", "norm_ffn_2", "norm_final_2", "conv_w_pw1_2",
        "conv_b_pw1_2", "conv_w_dw_2", "conv_b_dw_2", "conv_ln_g_2", "conv_ln_b_2", "conv_w_pw2_2", "conv_b_pw2_2",
        "kv_norm_2", "w_k_shared_2", "w_v_shared_2", "diff_w_q_2", "diff_lambda_q1_2", "diff_lambda_k1_2",
        "diff_lambda_q2_2", "diff_lambda_k2_2", "diff_subln_g_2", "diff_w_o_2", "mem_w_q_2", "mem_w_k_2", "mem_w_v_2",
        "mem_w_o_2", "ffn_w_gate_2", "ffn_w_up_2", "ffn_w_down_2"]


def kernel(**inputs):
    import concourse.bacc as bacc
    from concourse.bass_utils import run_bass_kernel_spmd

    nc = bacc.Bacc("TRN2", target_bir_lowering=False, num_devices=1)
    common, first = constants()
    arrays = {name: np.ascontiguousarray(inputs[name]) for name in _INS}
    arrays.update(common_constants=common, first_constants=first)
    arrays = {f"in_{name}": a for name, a in arrays.items()}
    w = {name[3:]: nc.dram_tensor(name, a.shape, mybir.dt.from_np(a.dtype), kind="ExternalInput").ap()
         for name, a in arrays.items()}
    out = nc.dram_tensor("result", (1, S, D), F32, kind="ExternalOutput").ap()
    build(nc, w, out)
    r = run_bass_kernel_spmd(nc, [arrays], core_ids=[0])
    return r.results[0]["result"]
```

```python
from contextlib import ExitStack

import numpy as np

import concourse.bass as bass
from concourse import mybir

F32 = mybir.dt.float32
F32R = mybir.dt.float32r
I32 = mybir.dt.int32
ALU = mybir.AluOpType
ACT = mybir.ActivationFunctionType
AX = mybir.AxisListType

P = 128
D = 1024
S = 256
NT = S // P
KT = D // P
HD = 64
NH = 4
BW = NH * HD
CMP = 32
NC = S // CMP
TAPS = 31
DH = 8
ROT = 16
MH = 4
MHT = D // MH // P
FF = 2816
FT = FF // P
CK, CN = 4, 512
RMS_EPS, LN_EPS = 1e-6, 1e-5
NEG = -1e30
TINY = 1e-30
LAMBDA_INIT = 0.8 - 0.6 * float(np.exp(-0.3))
TWO_PI = 2.0 * float(np.pi)

VECTORS = {"b_pw1": ("conv_b_pw1_2", 2 * KT), "b_dw": ("conv_b_dw_2", KT), "ln_g": ("conv_ln_g_2", KT), "ln_b": ("conv_ln_b_2", KT),
           "subln_g": ("diff_subln_g_2", 1)}
N_VECTOR_ROWS = sum(n for _, n in VECTORS.values())

W_A_Q, W_A_KV, W_A_G, W_A_Z = 0, 256, 640, 652
W_B_Q, W_B_K, W_B_V, W_B_Z = 908, 1164, 1292, 1420
W_C_Q, W_C_K, W_C_V, W_C_Z = 1676, 1932, 2188, 2444
W_D_Q, W_D_K, W_D_V, W_D_Z = 2700, 2956, 3212, 3468

COMMON = {"ident": (0, 128), "ones": (128, 128), "causal": (256, 256), "invfreq": (512, 8), "half": (520, 8)}
COMMON_W = 528
FIRST = {"alibi": (0, 1024), "window": (1024, 1024), "decay": (2048, 1024), "strict": (3072, 384),
         "after": (3456, 128), "cmp_bias": (3584, 64), "cmp_mask": (3648, 64), "block": (3712, 256)}
FIRST_W = 3968


def constants():
    q, j = np.arange(P)[:, None], np.arange(2 * P)[None, :]
    rel = q + P - j
    slopes = 2.0 ** (-8.0 * (np.arange(NH) + 1) / NH)
    common = np.zeros((P, COMMON_W), np.float32)
    common[:, 0:128] = np.eye(P)
    common[:, 128:256] = 1.0
    common[:, 256:512] = np.where(rel >= 0, 0.0, NEG)
    common[:, 512:520] = (500000.0 ** (-np.arange(0, ROT, 2) / ROT)).astype(np.float32)
    common[:, 520:528] = -0.5
    first = np.zeros((P, FIRST_W), np.float32)
    k, i = np.arange(P)[:, None], np.arange(2 * P)[None, :]
    gamma = 1.0 - 2.0 ** (-5.0 - np.arange(NH))
    for h in range(NH):
        bias = -slopes[h] * rel
        first[:, 256 * h:256 * h + 256] = np.where(rel >= 0, bias, NEG)
        first[:, 1024 + 256 * h:1280 + 256 * h] = np.where((rel >= 0) & (rel < 128), bias, NEG)
        first[:, 2048 + 256 * h:2304 + 256 * h] = np.where(i >= k, gamma[h] ** np.maximum(i - k, 0), 0.0) * HD ** -0.5
    first[:, 3072:3328] = i > k
    first[:, 3328:3456] = i[:, :P] > k
    first[:, 3456:3584] = k > i[:, :P]
    t = np.arange(P)[:, None, None, None] + P * np.arange(NT)[None, :, None, None]
    dist = t - (np.arange(NC) * CMP + CMP - 1)[None, None, None, :] + np.zeros((1, 1, NH, 1))
    first[:, 3584:3648] = np.where(dist >= 0, -slopes[None, None, :, None] * dist, NEG).reshape(P, -1)
    first[:, 3648:3712] = (dist >= 0).reshape(P, -1)
    rows = np.arange(NH * NC)[:, None] // NC
    first[:NH * NC, 3712:3968] = rows == (np.arange(BW)[None, :] // HD)
    return common, first


class Mark:
    def __init__(self, sem, value):
        self.sem, self.value = sem, value


class Lane:
    def __init__(self, eng, sem):
        self.eng, self.sem, self.count, self.met, self.last = eng, sem, 0, {}, None

    def wait(self, *marks):
        for m in marks:
            if m is not None and self.met.get(m.sem.name, 0) < m.value:
                self.eng.wait_ge(m.sem, m.value)
                self.met[m.sem.name] = m.value

    def after(self, *marks):
        self.wait(self.last, *marks)
        return self.eng

    def beside(self, *marks):
        self.wait(*marks)
        return self.eng

    def done(self, instruction):
        instruction.then_inc(self.sem, 1)
        self.count += 1
        self.last = Mark(self.sem, self.count)
        return self.last


class Slot:
    def __init__(self, t):
        self.t, self.marks, self.busy = t, (), False

    @property
    def free(self):
        return self.marks

    @free.setter
    def free(self, marks):
        self.marks, self.busy = marks, False


class Ring:
    def __init__(self, tensors):
        self.slots, self.at = [Slot(t) for t in tensors], 0

    def take(self):
        self.at += 1
        slot = self.slots[(self.at - 1) % len(self.slots)]
        assert not slot.busy
        slot.busy = True
        return slot


class Loads:
    def __init__(self, lane, sem):
        self.lane, self.sem, self.sent, self.own = lane, sem, {}, {}

    def start(self, name, dst, src, *marks):
        if name not in self.own:
            self.own[name], self.sent[name] = self.sem("load_" + name), 0
        self.lane.wait(*marks)
        self.lane.eng.dma_start(dst, src).then_inc(self.own[name], 16)
        self.sent[name] += 16
        return Mark(self.own[name], self.sent[name])


class Weights:
    N_RAW, N_SPLIT = 4, 3

    def __init__(self, k, plan):
        self.k, self.plan = k, plan
        self.raw = [Slot(k.sb(f"w_raw{i}", [P, CK * CN])) for i in range(self.N_RAW)]
        self.high = [k.sb(f"w_high{i}", [P, CK * CN], F32R) for i in range(self.N_SPLIT)]
        self.low = [k.sb(f"w_low{i}", [P, CK * CN], F32R) for i in range(self.N_SPLIT)]
        self.read = [None] * self.N_SPLIT
        self.ready = {}
        self.loaded = {}
        self.used, self.due = 0, None

    def begin(self):
        for i in range(self.N_RAW):
            self.load(i)

    def begin_splits(self):
        for i in range(self.N_SPLIT):
            self.split(i)

    def view(self, t, i):
        pieces, nk = self.plan[i]
        w = sum(n for _, n in pieces)
        return t[:, 0:nk * w].rearrange("p (k n) -> p k n", k=nk)

    def load(self, i):
        if i >= len(self.plan):
            return
        slot, at = self.raw[i % self.N_RAW], 0
        pieces, nk = self.plan[i]
        for src, n in pieces:
            self.loaded[i] = self.k.stream.start(f"w{i % self.N_RAW}", self.view(slot.t, i)[:, :, at:at + n], src, *slot.free)
            at += n

    def split(self, i):
        if i >= len(self.plan):
            return
        k, slot, j = self.k, self.raw[i % self.N_RAW], i % self.N_SPLIT
        raw, high, low = self.view(slot.t, i), self.view(self.high[j], i), self.view(self.low[j], i)
        a = k.act.done(k.act.beside(self.loaded[i], self.read[j]).activation(high, raw, ACT.Copy))
        v = k.vec.done(k.vec.beside(a, self.loaded[i], self.read[j]).tensor_tensor(low, raw, high.bitcast(F32), ALU.subtract))
        self.ready[i] = v
        slot.free = (v,)
        self.load(i + self.N_RAW)

    def take(self):
        if self.due is not None:
            self.split(self.due)
        i = self.used
        self.used += 1
        return self.view(self.high[i % self.N_SPLIT], i), self.view(self.low[i % self.N_SPLIT], i), self.ready[i]

    def give(self, mark):
        i = self.used - 1
        self.read[i % self.N_SPLIT] = mark
        self.due = i + self.N_SPLIT


class Operand:
    def __init__(self, high, low, ready=()):
        self.high, self.low = high, low
        n = -(-high.shape[1] // CK)
        self.ready, self.free = [ready] * n, [()] * n


class Norm:
    def __init__(self, k, name, layer, slot=0, transposed=True):
        self.transposed = transposed
        self.k, self.gain, self.slot = k, k.load_gain(name, layer, slot), slot
        self.sums = k.stat(2 * NT)
        self.seen, self.squares = [0] * NT, {}
        self.roots = k.stat(NT)

    def take(self, n, t, mark, squares=True):
        k, at = self.k, slice(n * CN, (n + 1) * CN)
        x, hn = k.X[:, t, at], k.HN[:, t, at]
        v = k.vec.done(k.vec.after(mark, self.gain, *k.hn_free).tensor_tensor(hn, x, k.G[self.slot].t[:, at], ALU.mult))
        if t == NT - 1 and self.transposed:
            k.late.append(lambda: self.turn(n, v))
        if squares:
            i = n * NT + t
            a = k.act.done(k.act.after(mark).activation(k.junk[:, :], x, ACT.Square, accum_out=self.sums[:, i:i + 1]))
            self.seen[t] += 1
            if min(self.seen) == 2:
                self.finish(a)

    def turn(self, n, mark):
        k = self.k
        for t in range(NT):
            k.transposed(k.HN[:, t, :], [n * CN + P * i for i in range(CK)], k.H, n * CK, t, mark)
        k.hn_free = (k.pe.last,)

    def finish(self, mark):
        p, k = self.k.pool, self.k
        mean = k.stat(NT)
        p.done(p.after(mark).tensor_tensor(mean, self.sums[:, 0:NT], self.sums[:, NT:2 * NT], ALU.add))
        p.done(p.after().tensor_scalar(mean, mean, 1.0 / D, RMS_EPS, ALU.mult, ALU.add))
        self.mark = p.done(p.after().tensor_tensor(self.roots, mean, k.half[:, 0:NT], ALU.pow))

    def root(self, t):
        for l in (self.k.act, self.k.vec):
            l.wait(self.mark)
        return self.roots[:, t:t + 1]


class Kernel:

    def __init__(self, nc, ctx, w):
        self.nc, self.ctx, self.phase, self.w = nc, ctx, ctx, w

        def lane(name, eng):
            return Lane(eng, self.sem(name))

        self.pe, self.vec = lane("pe_done", nc.tensor), lane("vec_done", nc.vector)
        self.act, self.pool = lane("act_done", nc.scalar), lane("pool_done", nc.gpsimd)
        self.stream = Loads(lane("sp_done", nc.sync), self.sem)
        self.side = Loads(self.pool, self.sem)

        def bank(name):
            return ctx.enter_context(nc.psum_tensor(name, [P, 512], F32))

        self.product = Ring([bank(f"product{i}") for i in range(4)])
        self.small = Ring([bank(f"small{i}") for i in range(4)])
        self.stats = self.sb("stats", [P, 768])
        self.stat_at = 0
        self.late = []

    def sem(self, name):
        return self.ctx.enter_context(self.nc.semaphore(name))

    def sb(self, name, shape, dt=F32):
        return self.phase.enter_context(self.nc.sbuf_tensor(name, shape, dt))

    def stat(self, n):
        self.stat_at += n
        assert self.stat_at <= 768, self.stat_at
        return self.stats[:, self.stat_at - n:self.stat_at]

    def pair(self, name, tiles, n=S):
        return tuple(self.sb(f"{name}_{part}", [P, tiles, n], F32R)[:, :, :] for part in ("high", "low"))

    def load_gain(self, name, layer, slot=0):
        v = self.w[name] if layer is None else self.w[name][layer]
        return self.row(f"gain{slot}", self.G[slot].t[:, :], v, self.vec.last)

    def ring(self, name, n, shape):
        return Ring([self.sb(f"{name}{i}", shape) for i in range(n)])

    def so_far(self):
        return [l.last for l in (self.pe, self.vec, self.act, self.pool)]

    def hand_over(self, marks):
        for l in (self.vec, self.act, self.pool):
            l.wait(*marks)

    def everyone(self):
        self.hand_over(self.so_far())


    def block(self, x, tiles, items, evacuate, order=None):
        pe = self.pe
        banks = [self.product.take() for _ in range(1 + max(i[0] for i in items))]
        if order is None:
            order = [(first, items, banks if first + CK >= tiles else []) for first in range(0, tiles, CK)]
        else:
            order = [(first, [i for i in items if i[0] in mine], [banks[b] for b in mine if complete])
                     for first, mine, complete in order]
        started = set()
        for first, part, complete in order:
            high, low, ready = self.weights.take()
            pe.wait(ready, *x.ready[first // CK])
            for b, off, t, col, w in part:
                if b not in started:
                    pe.wait(*banks[b].free)
                for j, kt in enumerate(range(first, min(first + CK, tiles))):
                    for xs, ws in ((x.low, high), (x.high, low), (x.high, high)):
                        if t is None:
                            a, r, n = ws[:, j, col:col + P], xs[:, kt, :], S
                        else:
                            a, r, n = xs[:, kt, t * P:(t + 1) * P], ws[:, j, col:col + w], w
                        mm = self.nc.tensor.matmul(banks[b].t[:, off:off + n], a, r, start=b not in started,
                                                   stop=True, skip_group_check=True)
                        started.add(b)
            m = pe.done(mm)
            x.free[first // CK] = (m,)
            self.flush()
            if complete:
                evacuate(complete, m)
            self.weights.give(m)
            yield

    def flush(self):
        late, self.late = self.late, []
        for f in late:
            f()

    def columns(self, x, tiles, evacuate, w=CN):
        def both(banks, m):
            for t in range(NT):
                evacuate(t, banks[t], m)
        return self.block(x, tiles, [(t, 0, t, 0, w) for t in range(NT)], both)

    def square(self, x, evacuate=None, both=None):
        done = []

        def each(banks, m):
            n = len(done)
            done.append(n)
            for t in range(NT):
                evacuate(n, t, banks[t], m)
        return self.block(x, KT, [(2 * n + t, 0, t, 0, CN) for n in range(2) for t in range(NT)], both or each,
                          [(first, (2 * n, 2 * n + 1), first + CK == KT) for first in range(0, KT, CK) for n in range(2)])

    def split_operand(self, src, mark, high, low):
        a = self.act.done(self.act.beside(mark).activation(high, src, ACT.Copy))
        return self.vec.done(self.vec.beside(mark, a).tensor_tensor(low, src, high.bitcast(F32), ALU.subtract))

    def transposed(self, src, cols, x, tile0, t, mark, scale=None):
        for g in range(0, len(cols), 4):
            part = cols[g:g + 4]
            bank = self.small.take()
            self.pe.wait(mark, *bank.free)
            for i, c in enumerate(part):
                tr = self.nc.tensor.transpose(bank.t[:, i * P:(i + 1) * P], src[:, c:c + P], self.ident)
            m = self.pe.done(tr)
            at = slice(tile0 + g, tile0 + g + len(part))
            hi, lo = x.high[:, at, t * P:(t + 1) * P], x.low[:, at, t * P:(t + 1) * P]
            ps = bank.t[:, 0:P * len(part)].rearrange("p (k n) -> p k n", n=P)
            chunk = (tile0 + g) // CK
            self.act.wait(*x.free[chunk])
            self.vec.wait(*x.free[chunk])
            if scale is None:
                v = self.split_operand(ps, m, hi, lo)
            else:
                a = self.act.done(self.act.beside(m).activation(hi, ps, ACT.Copy, scale=scale))
                v = self.vec.done(self.vec.beside(m, a).scalar_tensor_tensor(lo, ps, scale, hi.bitcast(F32), ALU.mult, ALU.subtract))
            bank.free = (v,)
            x.ready[chunk] = (v,)
        return v

    def row(self, name, dst, vector, *marks):
        return self.side.start(name, dst, vector.rearrange("(a n) -> a n", a=1).broadcast_to((P, vector.shape[0])), *marks)

    def inverse_root(self, sums, width, eps, mark, scale=1.0):
        n = sums.shape[1]
        mean, root = self.stat(n), self.stat(n)
        p = self.pool
        m = p.done(p.after(mark).tensor_scalar(mean, sums, 1.0 / width, eps, ALU.mult, ALU.add))
        m = p.done(p.after(m).tensor_tensor(root, mean, self.half[:, 0:n], ALU.pow))
        if scale != 1.0:
            m = p.done(p.after(m).tensor_scalar(root, root, scale, None, ALU.mult))
        return root, m

    def add_to_x(self, n, t, bank, m, scale=None):
        V, x = self.vec, self.X[:, t, n * CN:(n + 1) * CN]
        if scale is None:
            v = V.done(V.beside(m).tensor_tensor(x, x, bank.t[:, :], ALU.add))
        else:
            v = V.done(V.beside(m).scalar_tensor_tensor(x, bank.t[:, :], scale, x, ALU.mult, ALU.add))
        bank.free = (v,)
        self.next_norm.take(n, t, v)

    def copy_to(self, dst_of, func=ACT.Copy, scale_of=None):
        def evacuate(t, bank, m):
            dst = dst_of(t)
            scale = 1.0 if scale_of is None else scale_of(t)
            a = self.act.done(self.act.beside(m).activation(dst, bank.t[:, 0:dst.shape[-1]], func, scale=scale))
            bank.free = (a,)
            self.copied = a
        return evacuate

    def run(self, tasks, fill=(), limit=3):
        tasks, active, fill = list(tasks), [], iter(fill)
        while tasks or active:
            for task in list(active):
                if next(task, "end") == "end":
                    active.remove(task)
            if tasks and len(active) < limit:
                task = tasks.pop(0)
                if next(task, "end") != "end":
                    active.append(task)
            next(fill, None)
        for _ in fill:
            pass

    def softmax_rows(self, bank, m, nh, nk, bias, scale, floor=None):
        V, A = self.vec, self.act
        slot = self.rows_ring.take()
        s = slot.t[:, 0:nh * nk].rearrange("p (h n) -> p h n", n=nk)
        ps = bank.t[:, 0:nh * nk].rearrange("p (h n) -> p h n", n=nk)
        v = V.done(V.after(m, *slot.free).scalar_tensor_tensor(s, ps, scale, bias, ALU.mult, ALU.add))
        bank.free = (v,)
        top, neg, sums = self.stat(nh), self.stat(nh), self.stat(nh)
        v = V.done(V.after().tensor_reduce(top, s, AX.X, ALU.max))
        if floor is not None:
            v = V.done(V.after().tensor_tensor(top, top, floor, ALU.max))
        v = V.done(V.after().tensor_scalar(neg, top, -1.0, None, ALU.mult))
        A.wait(v)
        for h in range(nh):
            a = A.done(A.beside().activation(s[:, h, :], s[:, h, :], ACT.Exp, bias=neg[:, h:h + 1], accum_out=sums[:, h:h + 1]))
        return slot, s, sums, neg, a

    def turn(self, pieces, mark, done_with):
        bank, slot = self.small.take(), self.turned.take()
        self.pe.wait(mark, *bank.free)
        for i, p in enumerate(pieces):
            tr = self.nc.tensor.transpose(bank.t[:, i * P:(i + 1) * P], p, self.ident)
        m = self.pe.done(tr)
        done_with.free = (m,)
        n = P * len(pieces)
        a = self.act.done(self.act.after(m, *slot.free).activation(slot.t[:, 0:n], bank.t[:, 0:n], ACT.Copy))
        bank.free = (a,)
        return slot, a



def load_vectors(k, w):
    at, k.vcol = 0, {}
    for name, (source, n) in VECTORS.items():
        k.vectors_loaded = k.side.start("vectors", k.vector_rows[at:at + n, :], w[source][0].rearrange("(k p) -> k p", p=P))
        k.vcol[name] = k.vector_cols[:, at:at + n]
        at += n


def first_block(k, w):
    nc, V, A, T = k.nc, k.vec, k.act, k.nc.tensor
    with ExitStack() as phase:
        k.phase = phase
        gate = k.sb("gate", [P, D])
        with ExitStack() as inner:
            k.phase = inner
            bias, norm_g = k.sb("b_ada", [1, 3 * D]), k.sb("norm_g", [P, D])
            bias_loaded = k.side.start("b_ada", bias[:, :], w["b_ada"][0:1, :])
            g_loaded = k.row("norm_g", norm_g[:, :], w["norm_g"][0])
            k.x_loaded = k.side.start("x", k.X[:, :, :], w["x"][0].rearrange("(t p) n -> p t n", p=P))
            load_vectors(k, w)
            crow, c_silu = k.sb("c_row", [KT, P]), k.sb("c_silu", [P, KT])
            c_loaded = k.stream.start("c", crow[:, :], w["c"][0].rearrange("(k p) -> k p", p=P))
            k.weights.begin()
            bank = k.small.take()
            k.pe.wait(c_loaded)
            m = k.pe.done(T.transpose(bank.t[:, 0:KT], crow[:, :], k.ident[0:KT, 0:KT]))
            ch, cl = k.pair("cond", KT, P)
            a = A.done(A.after(m).activation(c_silu[:, :], bank.t[:, 0:KT], ACT.Silu))
            bank.free = (a,)
            wide = c_silu[:, :].unsqueeze(2).broadcast_to((P, KT, P))
            v = V.done(V.after(a).tensor_copy(ch, wide))
            v = V.done(V.after(v).tensor_tensor(cl, wide, ch.bitcast(F32), ALU.subtract))
            c_op = Operand(ch, cl, (v,))
            k.weights.begin_splits()
            def to_rows(base, n, dst):
                at = slice(n * CN, (n + 1) * CN)

                def evacuate(banks, m):
                    bank = banks[0]
                    k.pe.wait(bias_loaded)
                    at_b = ("shift", "scale", "gate").index(base) * D + n * CN
                    m = k.pe.done(T.matmul(bank.t[:, :], k.ones[0:1, :], bias[:, at_b:at_b + CN], start=False, stop=True, skip_group_check=True))
                    if base == "scale":
                        v = V.done(V.beside(m, g_loaded).scalar_tensor_tensor(dst[:, at], bank.t[:, :], 1.0, norm_g[:, at], ALU.add, ALU.mult))
                    else:
                        v = V.done(V.beside(m).tensor_copy(dst[:, at], bank.t[:, :]))
                    bank.free = (v,)
                    k.mod_mark = v
                    if base == "shift":
                        for t in range(NT):
                            hn = k.HN[:, t, at]
                            V.done(V.after(root_mark).scalar_tensor_tensor(hn, k.X[:, t, at], root[:, t:t + 1], k.G[0].t[:, at], ALU.mult, ALU.mult))
                            v = V.done(V.after().tensor_tensor(hn, hn, dst[:, at], ALU.add))

                        def turn():
                            for t in range(NT):
                                k.transposed(k.HN[:, t, :], [n * CN + P * i for i in range(CK)], k.H, n * CK, t, v)
                            k.hn_free = (k.pe.last,)
                        k.late.append(lambda: k.late.append(turn))
                drain(k.block(c_op, KT, [(0, 0, 0, 0, CN)], evacuate))
            for n in range(D // CN):
                to_rows("scale", n, k.G[0].t)
                if n == 0:
                    sums = k.stat(NT)
                    for t in range(NT):
                        a = A.done(A.after(k.x_loaded).activation(k.HN[:, t, :], k.X[:, t, :], ACT.Square, accum_out=sums[:, t:t + 1]))
                    root, root_mark = k.inverse_root(sums, D, RMS_EPS, a)
                to_rows("shift", n, k.G[1].t)
            for n in range(D // CN):
                to_rows("gate", n, gate)
            k.flush()
            gate_mark = k.mod_mark
            k.everyone()
        k.phase = phase
        tables_phase, table_marks = ExitStack(), {}
        c1 = tables_phase.enter_context(nc.sbuf_tensor("first_constants", [P, FIRST_W], F32, side="right"))

        def load_tables(names, *marks):
            at, end = FIRST[names[0]][0], sum(FIRST[names[-1]])
            mark = k.side.start("tables_" + names[0], c1[:, at:end], w["first_constants"][:, at:end], *marks)
            table_marks.update((n, mark) for n in names)
        load_tables(["decay"])

        def table(name, *dims):
            at, n = FIRST[name]
            v = c1[:, at:at + n]
            return v.rearrange("p (a b) -> p a b", a=dims[0]) if dims else v
        w1 = [k.G[i].t[:, :].rearrange("p (t m) -> p t m", m=HD) for i in range(2)]
        w2, span = k.sb("cmp_w2", [P, HD]), CMP // 2
        pos = k.sb("cmp_pos", [CMP, P])
        k.rows_ring = k.ring("rows", 2, [P, 512])
        k.turned = k.ring("turned", 2, [P, 512])
        two = [P, NT, BW]
        qk = k.sb("queries_keys", [P, 4, NH, S])
        q_c, k_c, q_d, k_d = (qk[0:HD, i, :, :] for i in range(4))
        k_b = k.sb("k_b", [HD, 2, S])
        q_b, q_a = q_d, k_d
        k_sel, k_win, cmp_t = k.sb("k_sel", [HD, S]), k.sb("k_win", [HD, S]), k.sb("cmp_t", [P, S])
        v_sel, v_win = k.sb("v_sel", [P, NT, HD]), k.sb("v_win", [P, NT, HD])
        v_c, v_d = k.sb("v_c", two), k.sb("v_d", two)
        v_b = v_d[:, :, 0:2 * HD]
        z = {b: k.sb("z_" + b, two) for b in "acd"}
        z["b"] = z["d"]
        gates = k.sb("gates", [P, NT, 3 * NH])
        merged = k.sb("merged", [P, NT, D])
        sig = Ring([k.HN[:, i, :].rearrange("p (t n) -> p t n", t=NT) for i in range(NT)])
        A.wait(*k.hn_free)
        y_ring = k.ring("y", 2, two)
        y_op = [Operand(*k.pair(f"y_op{i}", BW // P)) for i in range(2)]
        made = {}

        def heads(bank, off, dst, h0, m):
            for i in range(2):
                a = A.done(A.beside(m).activation(dst[:, h0 + i, :], bank.t[i * HD:(i + 1) * HD, off:off + S], ACT.Copy))
            return a

        def qk_block(q, kk, name):
            def evacuate(banks, m):
                for i in range(4):
                    a = heads(banks[i // 2], S * (i % 2), (q, kk)[i // 2], 2 * (i % 2), m)
                    banks[i // 2].free = (a,)
                made[name] = a
            return k.block(k.H, KT, [(i // 2, S * (i % 2), None, P * i, P) for i in range(4)], evacuate)

        def vz_block(vt, zt, name):
            w_v, w_z = vt.shape[-1], zt.shape[-1]

            def evacuate(t, bank, m):
                A.done(A.beside(m).activation(vt[:, t, :], bank.t[:, 0:w_v], ACT.Copy))
                a = A.done(A.beside(m).activation(zt[:, t, :], bank.t[:, w_v:w_v + w_z], ACT.Silu))
                bank.free = (a,)
                made[name] = a
            return evacuate

        def block_c3():
            inner = vz_block(v_b, z["b"], "b_v")

            def evacuate(banks, m):
                made["b_k"] = heads(banks[0], 0, k_b, 0, m)
                banks[0].free = (made["b_k"],)
                for t in range(NT):
                    inner(t, banks[1 + t], m)
            return k.block(k.H, KT, [(0, 0, None, 0, P)] + [(1 + t, 0, t, P, 384) for t in range(NT)], evacuate)

        def block_c2():
            def evacuate(banks, m):
                for i in range(2):
                    a = heads(banks[0], S * i, q_b, 2 * i, m)
                banks[0].free = (a,)
                for t in range(NT):
                    a = A.done(A.beside(m).activation(z["a"][:, t, :], banks[1 + t].t[:, 0:BW], ACT.Silu))
                    banks[1 + t].free = (a,)
                made["b_q"] = a
            return k.block(k.H, KT, [(0, S * i, None, BW + P * i, P) for i in range(2)]
                           + [(1 + t, 0, t, 0, BW) for t in range(NT)], evacuate)

        def block_c1():
            def evacuate(banks, m):
                for i, dst in enumerate((k_sel, k_win)):
                    a = A.done(A.beside(m).activation(dst[:, :], banks[0].t[0:HD, S * i:S * i + S], ACT.Copy))
                banks[0].free = (a,)
                for t in range(NT):
                    b = banks[1 + t]
                    A.done(A.beside(m).activation(v_sel[:, t, :], b.t[:, 0:HD], ACT.Copy))
                    A.done(A.beside(m).activation(v_win[:, t, :], b.t[:, HD:2 * HD], ACT.Copy))
                    a = A.done(A.beside(m).activation(gates[:, t, :], b.t[:, 2 * HD:2 * HD + 3 * NH], ACT.Sigmoid))
                    b.free = (a,)
                made["a_kv"] = a
            items = [(0, 0, None, 0, P), (0, S, None, P, P)]
            for t in range(NT):
                items += [(1 + t, 0, t, HD, HD), (1 + t, HD, t, P + HD, HD + 3 * NH)]
            return k.block(k.H, KT, items, evacuate)

        def block_c0():
            def evacuate(banks, m):
                for i in range(2):
                    a = heads(banks[0], S * i, q_a, 2 * i, m)
                banks[0].free = (a,)
                a = A.done(A.beside(m).activation(cmp_t[:, :], banks[1].t[:, 0:S], ACT.Copy))
                banks[1].free = (a,)
                made["a_q"] = a
            return k.block(k.H, KT, [(0, 0, None, 0, P), (0, S, None, P, P), (1, 0, None, 2 * P, P)], evacuate)

        def merge_gate(i, n):
            slot = sig.take()
            A.wait(*slot.free)
            yield from k.columns(k.H, KT, k.copy_to(lambda t: slot.t[:, t, :], ACT.Sigmoid))
            made["gate", n] = slot, k.copied

        def merge_branch(i, n, x):
            slot, mark = made["gate", n]

            def evacuate(t, bank, m):
                at = merged[:, t, n * CN:(n + 1) * CN]
                g = slot.t[:, t, :]
                if i == ORDER[0]:
                    v = V.done(V.after(m, mark).tensor_tensor(at, g, bank.t[:, :], ALU.mult))
                else:
                    v = V.done(V.after(m, mark).tensor_tensor(g, g, bank.t[:, :], ALU.mult))
                    v = V.done(V.after().tensor_tensor(at, at, g, ALU.add))
                bank.free = (v,)
                slot.free = (v,)
                made["merged"] = v
            yield from k.columns(x, BW // P, evacuate)

        def merge(i, x, blocks=range(D // CN)):
            for n in blocks:
                yield from merge_gate(i, n)
                yield from merge_branch(i, n, x)

        def turn_merged(n):
            for t in range(NT):
                k.transposed(merged[:, t, :], [n * CN + P * i for i in range(CK)], k.H, n * CK, t, made["merged"])

        def finish(branch, y, mark, op):
            V.wait(made[{"a": "b_q", "b": "b_v", "c": "c_v", "d": "d_v"}[branch]])
            for t in range(NT):
                v = V.done(V.after(mark).tensor_tensor(y.t[:, t, :], y.t[:, t, :], z[branch][:, t, :], ALU.mult))

            def turn():
                for t in range(NT):
                    k.transposed(y.t[:, t, :], [0, P], op, 0, t, v)
                y.free = (k.pe.last,)
            k.late.append(turn)

        def score_keys(q, kk, h, ready):
            bank = k.small.take()
            k.pe.wait(ready, *bank.free)
            T.matmul(bank.t[:, 0:S], kk[:, h, 0:P], q[:, h, :], start=True, stop=True, skip_group_check=True)
            m = k.pe.done(T.matmul(bank.t[:, S:S + P], kk[:, h, P:S], q[:, h, P:S], start=False, stop=True, skip_group_check=True))
            return bank, m

        def mix_keys(slot, mark, v, h, y):
            bank = k.small.take()
            k.pe.wait(mark, *bank.free)
            p, vh = slot.t, slice(h * HD, (h + 1) * HD)
            T.matmul(bank.t[:, 0:HD], p[:, 0:P], v[:, 0, vh], start=True, stop=True, skip_group_check=True)
            T.matmul(bank.t[:, HD:2 * HD], p[:, P:S], v[:, 0, vh], start=False, stop=True, skip_group_check=True)
            m = k.pe.done(T.matmul(bank.t[:, HD:2 * HD], p[:, S:S + P], v[:, 1, vh], start=False, stop=True, skip_group_check=True))
            slot.free = (m,)
            a = A.done(A.after(m).activation(y[:, :, vh], bank.t[:, 0:2 * HD].rearrange("p (t n) -> p t n", t=NT), ACT.Copy))
            bank.free = (a,)
            return a

        def retention(h, y):
            bank, m = score_keys(q_d, k_d, h, made["d_qk"])
            slot = k.rows_ring.take()
            decay = table("decay", NH)
            V.done(V.after(m, *slot.free).tensor_tensor(slot.t[:, 0:S], bank.t[:, 0:S], decay[:, h, :], ALU.mult))
            v = V.done(V.beside().tensor_tensor(slot.t[:, S:S + P], bank.t[:, S:S + P], decay[:, h, 0:P], ALU.mult))
            bank.free = (v,)
            yield
            made["y_d"] = mix_keys(slot, v, v_d, h, y)

        def retention_norm(y):
            g = NT * NH
            o = y[:, :, :].rearrange("p t (h d) -> p (t h) d", d=HD)
            sums, mean, sq_sums = k.stat(g), k.stat(g), k.stat(g)
            slot = k.rows_ring.take()
            sq = slot.t[:, :].rearrange("p (g d) -> p g d", d=HD)

            def wide(s):
                return s.unsqueeze(2).broadcast_to((P, g, HD))
            V.done(V.after(made["y_d"], *slot.free).tensor_reduce(sums, o, AX.X, ALU.add))
            V.done(V.after().tensor_scalar(mean, sums, 1.0 / HD, None, ALU.mult))
            V.done(V.after().tensor_tensor(o, o, wide(mean), ALU.subtract))
            V.done(V.after().tensor_tensor(sq, o, o, ALU.mult))
            v = V.done(V.after().tensor_reduce(sq_sums, sq, AX.X, ALU.add))
            slot.free = (v,)
            r, m = k.inverse_root(sq_sums, HD, LN_EPS, v)
            return V.done(V.after(m).tensor_tensor(o, o, wide(r), ALU.mult))

        def stick(h, y):
            n = S + P
            bank, m = score_keys(q_c, k_c, h, made["c_qk"])
            slot, soft = k.rows_ring.take(), k.turned.take()
            zt, sp, strict = slot.t[:, 0:n], soft.t[:, 0:n], table("strict")
            A.done(A.after(m, *slot.free).activation(zt, bank.t[:, 0:n], ACT.Copy, scale=HD ** -0.5))
            A.done(A.after(*soft.free).activation(sp, bank.t[:, 0:n], ACT.Abs, scale=HD ** -0.5))
            bank.free = (A.last,)
            A.done(A.after().activation(sp, sp, ACT.Exp, scale=-1.0))
            a = A.done(A.after().activation(sp, sp, ACT.Ln, bias=1.0))
            V.done(V.after(a).scalar_tensor_tensor(sp, zt, 0.0, sp, ALU.max, ALU.add))
            V.done(V.after().tensor_tensor(zt, zt, sp, ALU.subtract))
            v = V.done(V.after().tensor_tensor(sp, sp, strict, ALU.mult))
            yield
            yield
            bank = k.small.take()
            k.pe.wait(v, *bank.free)
            after, ones = table("after"), k.ones
            T.matmul(bank.t[:, 0:S], after, sp[:, 0:S], start=True, stop=True, skip_group_check=True)
            T.matmul(bank.t[:, P:S], ones, sp[:, S:n], start=False, stop=True, skip_group_check=True)
            m = k.pe.done(T.matmul(bank.t[:, S:n], after, sp[:, S:n], start=False, stop=True, skip_group_check=True))
            soft.free = (m,)
            v = V.done(V.after(m).tensor_tensor(zt, zt, bank.t[:, 0:n], ALU.subtract))
            bank.free = (v,)
            a = A.done(A.after(v).activation(zt, zt, ACT.Exp))
            v = V.done(V.after(a).tensor_tensor(zt, zt, strict, ALU.mult))
            yield
            yield
            made["y_c"] = mix_keys(slot, v, v_c, h, y)

        def softmax_group(q, kk_of, v_of, bias, heads_, t, ready, out):
            nh, nk = len(heads_), P * (t + 1)
            bank = k.small.take()
            k.pe.wait(ready, *bank.free)
            for i, h in enumerate(heads_):
                mm = T.matmul(bank.t[:, i * nk:(i + 1) * nk], q[:, h, t * P:(t + 1) * P], kk_of(h)[:, 0:nk],
                              start=i == 0, stop=True, skip_group_check=True)
            m = k.pe.done(mm)
            h0 = heads_[0]
            floor = sink[:, h0:h0 + nh] if out.sink else None
            slot, s, sums, neg, a = k.softmax_rows(bank, m, nh, nk, table(bias, NH)[:, h0:h0 + nh, 2 * P - nk:2 * P], HD ** -0.5, floor)
            yield
            turned, tm = k.turn([s[:, i, j * P:(j + 1) * P] for i in range(nh) for j in range(t + 1)], a, slot)
            yield
            bank = k.small.take()
            k.pe.wait(tm, *bank.free)
            for i, h in enumerate(heads_):
                for j in range(t + 1):
                    b = i * (t + 1) + j
                    mm = T.matmul(bank.t[:, i * HD:(i + 1) * HD], turned.t[:, b * P:(b + 1) * P], v_of(h, j),
                                  start=b == 0, stop=True, skip_group_check=True)
            m = k.pe.done(mm)
            turned.free = (m,)
            out(bank, m, sums, neg, heads_, t)

        class Out:
            def __init__(self, y, first, gate_index=None, use_sink=False):
                self.y, self.first, self.gate, self.sink = y, first, gate_index, use_sink

            def __call__(self, bank, m, sums, neg, heads_, t):
                nh, h0 = len(heads_), heads_[0]
                inv = k.stat(nh)
                if self.sink:
                    tail = k.stat(nh)
                    V.done(V.after(m).tensor_tensor(tail, sink[:, h0:h0 + nh], neg, ALU.add))
                    a = A.done(A.after(V.last).activation(tail, tail, ACT.Exp))
                    V.done(V.after(a).tensor_tensor(sums, sums, tail, ALU.add))
                V.done(V.after(m).reciprocal(inv, sums))
                if self.gate is not None:
                    g = gates[:, t, :].rearrange("p (h c) -> p c h", c=3)[:, self.gate, h0:h0 + nh]
                    V.done(V.after().tensor_tensor(inv, inv, g, ALU.mult))
                wide = inv.unsqueeze(2).broadcast_to((P, nh, HD))
                o = bank.t[:, 0:nh * HD].rearrange("p (h d) -> p h d", d=HD)
                y = self.y[:, t, h0 * HD:(h0 + nh) * HD].rearrange("p (h d) -> p h d", d=HD)
                if self.first:
                    bank.free = (V.done(V.after().tensor_tensor(y, o, wide, ALU.mult)),)
                else:
                    slot = k.part_ring.take()
                    part = slot.t[:, 0:nh * HD].rearrange("p (h d) -> p h d", d=HD)
                    bank.free = (V.done(V.after().tensor_tensor(part, o, wide, ALU.mult)),)
                    slot.free = (V.done(V.after().tensor_tensor(y, y, part, ALU.add)),)

        groups = [([0, 1], 1), ([2, 3], 1), ([0, 1, 2, 3], 0)]
        k.part_ring = k.ring("part", 1, [P, BW])
        sink = k.sb("sink_row", [P, NH])
        V.wait(k.row("sink", sink[:, :], w["sink"][0]))

        def compressed(y):
            bank = k.small.take()
            k.pe.wait(l3, *bank.free)
            m = k.pe.done(T.transpose(bank.t[:, 0:CMP], pos[:, :], k.ident[0:CMP, 0:CMP]))
            pos_t = k.stat(CMP)
            v = V.done(V.after(m).tensor_copy(pos_t, bank.t[:, 0:CMP]))
            bank.free = (v,)
            blocks = cmp_t[:, :].rearrange("p (c t) -> p c t", t=CMP)
            v = V.done(V.after(made["a_q"]).tensor_tensor(blocks, blocks, pos_t.unsqueeze(1).broadcast_to((P, NC, CMP)), ALU.add))
            yield
            hid, hid4 = k.stat(NC), k.stat(NH * NC)
            for j in range(2):
                bank = k.small.take()
                r = slice(j * HD, (j + 1) * HD)
                k.pe.wait(v, l1, *bank.free)
                for t in range(CMP):
                    mm = T.matmul(bank.t[r, 0:NC], w1[t // span][r, t % span, :], blocks[r, :, t], start=t == 0, stop=t == CMP - 1)
                m = k.pe.done(mm)
                a = A.done(A.after(m).activation(hid[r, :], bank.t[r, 0:NC], ACT.Silu))
                bank.free = (a,)
            v = V.done(V.after(a).tensor_copy(hid4[HD:P, :].rearrange("p (h c) -> p h c", h=NH),
                                              hid[HD:P, :].unsqueeze(1).broadcast_to((HD, NH, NC))))
            yield
            kc, vc = k.stat(NC), k_c[0:NH * NC, 0, :]
            b0, b1 = k.small.take(), k.small.take()
            k.pe.wait(a, v, l2, *b0.free, *b1.free)
            m = k.pe.done(T.matmul(b0.t[0:HD, 0:NC], w2[0:HD, :], hid[0:HD, :], start=True, stop=True))
            v0 = V.done(V.after(m).tensor_copy(kc[0:HD, :], b0.t[0:HD, 0:NC]))
            b0.free = (v0,)
            m = k.pe.done(T.matmul(b1.t[0:NH * NC, 0:HD], hid4[HD:P, :], w2[HD:P, :], start=True, stop=True))
            v1 = V.done(V.after(m).tensor_tensor(
                vc.rearrange("p (h d) -> p h d", d=HD),
                b1.t[0:NH * NC, 0:HD].unsqueeze(1).broadcast_to((NH * NC, NH, HD)),
                table("block")[0:NH * NC, :].rearrange("p (h d) -> p h d", d=HD), ALU.mult))
            b1.free = (v1,)
            yield
            bank = k.small.take()
            k.pe.wait(v0, *bank.free)
            for t in range(NT):
                for h in range(NH):
                    c = (t * NH + h) * NC
                    mm = T.matmul(bank.t[:, c:c + NC], q_a[:, h, t * P:(t + 1) * P], kc[0:HD, :],
                                  start=c == 0, stop=True, skip_group_check=True)
            m = k.pe.done(mm)
            g, n = NT * NH, NT * NH * NC
            slot = k.rows_ring.take()
            s = slot.t[:, 0:n]
            s3 = s.rearrange("p (g c) -> p g c", c=NC)
            top, sums, inv = k.stat(g), k.stat(g), k.stat(g)

            def wide(x):
                return x.unsqueeze(2).broadcast_to((P, g, NC))
            v = V.done(V.after(m, *slot.free).scalar_tensor_tensor(s, bank.t[:, 0:n], HD ** -0.5, table("cmp_bias"), ALU.mult, ALU.add))
            bank.free = (v,)
            V.done(V.after().tensor_reduce(top, s3, AX.X, ALU.max))
            v = V.done(V.after().tensor_tensor(s3, s3, wide(top), ALU.subtract))
            a = A.done(A.after(v).activation(s, s, ACT.Exp))
            V.done(V.after(a).tensor_tensor(s, s, table("cmp_mask"), ALU.mult))
            V.done(V.after().tensor_reduce(sums, s3, AX.X, ALU.add))
            V.done(V.after().tensor_scalar(sums, sums, TINY, None, ALU.max))
            V.done(V.after().reciprocal(inv, sums))
            gg = gates[:, :, :].rearrange("p t (h c) -> p (t h) c", c=3)[:, :, 0]
            V.done(V.after().tensor_tensor(inv, inv, gg, ALU.mult))
            v = V.done(V.after().tensor_tensor(s3, s3, wide(inv), ALU.mult))
            yield
            bank, turned = k.small.take(), k.turned.take()
            k.pe.wait(v, *bank.free)
            half = NH * NC
            for t in range(NT):
                tr = T.transpose(bank.t[0:half, t * P:(t + 1) * P], s[:, t * half:(t + 1) * half], k.ident)
            m = k.pe.done(tr)
            slot.free = (m,)
            a = A.done(A.after(m, *turned.free).activation(turned.t[0:half, 0:S], bank.t[0:half, 0:S], ACT.Copy))
            bank.free = (a,)
            yield
            bank = k.small.take()
            k.pe.wait(a, v1, *bank.free)
            for t in range(NT):
                mm = T.matmul(bank.t[:, t * BW:(t + 1) * BW], turned.t[0:half, t * P:(t + 1) * P], vc,
                              start=t == 0, stop=True, skip_group_check=True)
            m = k.pe.done(mm)
            turned.free = (m,)
            v = V.done(V.after(m).tensor_tensor(y[:, :, :], y[:, :, :], bank.t[:, :].rearrange("p (t n) -> p t n", t=NT), ALU.add))
            bank.free = (v,)

        def chain(*gens):
            for g in gens:
                yield from g

        def all_of(gen):
            for _ in gen:
                pass

        all_of(qk_block(q_d, k_d, "d_qk"))
        all_of(k.columns(k.H, KT, vz_block(v_d, z["d"], "d_v")))
        k.pe.wait(made["d_v"])
        V.wait(table_marks["decay"])
        load_tables(["strict", "after"], made["d_v"])
        load_tables(["window"])
        for j in range(2):
            for i in range(2):
                l1 = k.side.start("cmp_w1", w1[i][j * HD:(j + 1) * HD, :, :],
                                  w["cmp_w1"][0, j].rearrange("(t d) m -> d t m", d=HD)[:, i * span:(i + 1) * span, :], made["d_v"])
        l2 = k.side.start("cmp_w2", w2[:, :], w["cmp_w2"][0].rearrange("j d m -> (j d) m"))
        l3 = k.side.start("cmp_pos", pos[:, 0:HD], w["cmp_pos"][0, 0])
        l3 = k.side.start("cmp_pos", pos[:, HD:P], w["cmp_pos"][0, 1])
        y = y_ring.take()
        A.wait(*y.free)
        k.run([retention(h, y.t) for h in range(NH)],
              chain(qk_block(q_c, k_c, "c_qk"), k.columns(k.H, KT, vz_block(v_c, z["c"], "c_v"))))
        finish("d", y, retention_norm(y.t), y_op[0])

        for l in (V, k.pe):
            l.wait(made["c_v"], table_marks["strict"])
        A.wait(k.pe.last, V.last)
        load_tables(["alibi"], made["c_v"])
        load_tables(["cmp_bias", "cmp_mask", "block"])
        y = y_ring.take()
        A.wait(*y.free)
        k.run([stick(h, y.t) for h in range(NH)], chain(block_c3(), block_c2(), merge(3, y_op[0])), 2)
        finish("c", y, made["y_c"], y_op[1])

        k.pe.wait(made["b_v"], made["b_q"])
        V.wait(table_marks["window"])
        y = y_ring.take()
        V.wait(*y.free)
        k.run([softmax_group(q_b, lambda h: k_b[:, h // 2, :], lambda h, j: v_b[:, j, (h // 2) * HD:(h // 2 + 1) * HD],
                             "window", hs, t, made["b_q"], Out(y.t, True, use_sink=True)) for hs, t in groups],
              chain(block_c1(), block_c0()))
        finish("b", y, V.last, y_op[0])

        k.pe.wait(made["a_kv"], made["a_q"])
        V.wait(table_marks["alibi"], table_marks["block"])
        V.wait(made["a_kv"], k.pe.last)
        y = y_ring.take()
        V.wait(*y.free)
        selected = [softmax_group(q_a, lambda h: k_sel[:, :], lambda h, j: v_sel[:, j, :], "alibi", hs, t, made["a_q"], Out(y.t, True, 1))
                    for hs, t in groups]
        k.run(selected[:1] + [compressed(y.t)] + selected[1:]
              + [softmax_group(q_a, lambda h: k_win[:, :], lambda h, j: v_win[:, j, :], "alibi", hs, t, made["a_q"], Out(y.t, False, 2))
                 for hs, t in groups],
              chain(merge(2, y_op[1]), merge(1, y_op[0])))
        finish("a", y, V.last, y_op[1])
        mem_rows = qk[:, 0:NT, :, :].rearrange("p t h n -> p t (h n)")
        mem_loaded = k.side.start("mem", mem_rows, w["mem_2"][0].rearrange("(t p) n -> p t n", p=P), V.last, k.pe.last, A.last)
        A.wait(V.last, k.pe.last)
        V.wait(k.pe.last)
        tables_phase.close()
        mem = Operand(*(k.ctx.enter_context(nc.sbuf_tensor(f"mem_{part}", [P, KT, S], F32R, side="right"))[:, :, :]
                        for part in ("high", "low")))
        all_of(merge(0, y_op[1], [0]))
        for t in range(NT):
            k.transposed(mem_rows[:, t, :], [P * i for i in range(KT)], mem, 0, t, mem_loaded)
        all_of(merge_gate(0, 1))
        turn_merged(0)
        all_of(merge_branch(0, 1, y_op[1]))

        k.late.append(lambda: turn_merged(1))
        g1, g2 = (k.load_gain(n, i, j) for n, i, j in (("final_g", None, 0), ("norm_mix_2", 0, 1)))
        squares = k.stat(2 * 2 * NT)
        junk = qk[:, 2, 0:CN // S, :]

        done = []

        def to_x(banks, m):
            n = len(done)
            done.append(n)
            at = slice(n * CN, (n + 1) * CN)
            x, hn = ([b[:, t, at] for t in range(NT)] for b in (k.X, k.HN))
            for t in range(NT):
                v = V.done(V.beside(m, gate_mark).tensor_tensor(hn[t], banks[t].t[:, :], gate[:, at], ALU.mult))
                banks[t].free = (v,)
                v = V.done(V.after().tensor_tensor(x[t], x[t], hn[t], ALU.add))
                i = n * NT + t
                sq = A.done(A.after(v).activation(junk.rearrange("p a n -> p (a n)"), x[t], ACT.Square, accum_out=squares[:, i:i + 1]))
            for t in range(NT):
                v = V.done(V.beside(g1, sq).tensor_tensor(x[t], x[t], k.G[0].t[:, at], ALU.mult))
                i = 2 * NT + n * NT + t
                A.done(A.after(v).activation(junk.rearrange("p a n -> p (a n)"), x[t], ACT.Square, accum_out=squares[:, i:i + 1]))
        all_of(k.square(k.H, both=to_x))
        for t in range(NT):
            for n in range(D // CN):
                at = slice(n * CN, (n + 1) * CN)
                V.done(V.after(g2).tensor_tensor(k.HN[:, t, at], k.X[:, t, at], k.G[1].t[:, at], ALU.mult))
        p, means, k.two_roots = k.pool, k.stat(2 * NT), k.stat(2 * NT)
        s4 = squares.rearrange("p (s n t) -> p s n t", s=2, n=2)
        p.done(p.after(A.last).tensor_tensor(means.rearrange("p (s t) -> p s t", s=2), s4[:, :, 0, :], s4[:, :, 1, :], ALU.add))
        p.done(p.after().tensor_scalar(means[:, 0:NT], means[:, 0:NT], 1.0 / D, RMS_EPS, ALU.mult, ALU.add))
        r1, r2 = k.two_roots[:, 0:NT], k.two_roots[:, NT:2 * NT]
        p.done(p.after().tensor_tensor(r1, means[:, 0:NT], k.half[:, 0:NT], ALU.pow))
        p.done(p.after().tensor_tensor(means[:, NT:2 * NT], means[:, NT:2 * NT], r1, ALU.mult))
        p.done(p.after().tensor_tensor(means[:, NT:2 * NT], means[:, NT:2 * NT], r1, ALU.mult))
        p.done(p.after().tensor_scalar(means[:, NT:2 * NT], means[:, NT:2 * NT], 1.0 / D, RMS_EPS, ALU.mult, ALU.add))
        p.done(p.after().tensor_tensor(r2, means[:, NT:2 * NT], k.half[:, 0:NT], ALU.pow))
        k.roots_mark = p.done(p.after().tensor_tensor(r2, r1, r2, ALU.mult))
        k.everyone()
    k.phase = k.ctx
    return mem


ORDER = (3, 2, 1, 0)



def drain(gen):
    for _ in gen:
        pass


def memory_keys(k, layer, mem, keys, values, made):
    for n in range(D // CN):
        def to_keys(banks, m):
            for b in range(2):
                a = k.act.done(k.act.after(m).activation(keys[:, 4 * n + 2 * b:4 * n + 2 * b + 2, :],
                                                         banks[b].t[:, :].rearrange("p (k n) -> p k n", n=S), ACT.Copy))
                banks[b].free = (a,)
            made["keys", layer] = a
        yield from k.block(mem, KT, [(i // 2, S * (i % 2), None, P * i, P) for i in range(4)], to_keys)
    for n in range(D // CN):
        yield from k.columns(mem, KT, k.copy_to(lambda t: values[:, t, n * CN:(n + 1) * CN]))
    made["values", layer] = k.copied


def memory_attention(k, layer, keys, values, made):
    V, A, T = k.vec, k.act, k.nc.tensor
    norm = k.next_norm
    k.rows_ring, k.turned = k.ring(f"mrows{layer}_", 3, [P, 512]), k.ring(f"mturned{layer}_", 2, [P, 512])
    q = k.sb(f"q_mem{layer}", [P, KT, S])
    o = Operand(*k.pair(f"o_mem{layer}", KT))

    def q_block(n):
        def to_q(banks, m):
            for b in range(2):
                a = A.done(A.beside(m).activation(q[:, 4 * n + 2 * b:4 * n + 2 * b + 2, :],
                                                  banks[b].t[:, :].rearrange("p (k n) -> p k n", n=S), ACT.Copy))
                banks[b].free = (a,)
            made["q", n] = a
        return k.block(k.H, KT, [(i // 2, S * (i % 2), None, P * i, P) for i in range(4)], to_q)
    drain(q_block(0))
    scale = (D // MH) ** -0.5
    norm.root(0)
    scales, neg_scales = k.stat(NT), k.stat(NT)
    V.done(V.after().tensor_scalar(scales, norm.roots, scale, None, ALU.mult))
    scale_mark = V.done(V.after().tensor_scalar(neg_scales, norm.roots, -scale, None, ALU.mult))

    def head(h):
        bank, slot = k.small.take(), k.rows_ring.take()
        k.pe.wait(made["q", h // 2], made["keys", layer], *bank.free)
        for t in range(NT):
            for j in range(MHT):
                kt = h * MHT + j
                mm = T.matmul(bank.t[:, t * S:(t + 1) * S], q[:, kt, t * P:(t + 1) * P], keys[:, kt, :],
                              start=t == 0 and j == 0, stop=True, skip_group_check=True)
        m = k.pe.done(mm)
        s = slot.t[:, :].rearrange("p (t n) -> p t n", t=NT)
        ps = bank.t[:, :].rearrange("p (t n) -> p t n", t=NT)
        top, neg, sums, inv = k.stat(NT), k.stat(NT), k.stat(NT), k.stat(NT)
        v = V.done(V.beside(m).tensor_reduce(top, ps, AX.X, ALU.max))
        v = V.done(V.after().tensor_tensor(neg, top, neg_scales, ALU.mult))
        A.wait(v, scale_mark, *slot.free)
        for t in range(NT):
            a = A.done(A.beside().activation(s[:, t, :], ps[:, t, :], ACT.Exp, bias=neg[:, t:t + 1], scale=scales[:, t:t + 1],
                                             accum_out=sums[:, t:t + 1]))
        bank.free = (a,)
        V.done(V.beside(a).reciprocal(inv, sums))
        v = V.done(V.after().tensor_tensor(s, s, inv.unsqueeze(2).broadcast_to((P, NT, S)), ALU.mult))
        yield
        turned, tm = k.turn([s[:, t, j * P:(j + 1) * P] for j in range(2) for t in range(NT)], v, slot)
        yield
        bank = k.small.take()
        k.pe.wait(tm, made["values", layer], *bank.free)
        for f in range(MHT):
            c = (h * MHT + f) * P
            for j in range(2):
                mm = T.matmul(bank.t[:, f * S:(f + 1) * S], values[:, j, c:c + P], turned.t[:, j * S:(j + 1) * S],
                              start=f == 0 and j == 0, stop=True, skip_group_check=True)
        m = k.pe.done(mm)
        turned.free = (m,)
        at = slice(h * MHT, (h + 1) * MHT)
        v = k.split_operand(bank.t[:, :].rearrange("p (k n) -> p k n", n=S), m, o.high[:, at, :], o.low[:, at, :])
        bank.free = (v,)
        o.ready[h // 2] = (v,)
        made["attended"] = k.so_far()

    def fill():
        yield from q_block(1)
        yield
        yield from k.square(o, k.add_to_x)
    k.next_norm = Norm(k, "norm_ffn_2", layer, 1)
    k.run([head(h) for h in range(MH)], fill())


def feed_forward(k, layer, beside, following):
    V, A, T = k.vec, k.act, k.nc.tensor
    with ExitStack() as phase:
        k.phase = phase
        norm = k.next_norm
        hidden = Operand(*k.pair(f"hidden{layer}", FT))
        mids = k.ring(f"mid{layer}_", 2, [P, CK, S])
        diagonal, roots = k.sb(f"ffn_diagonal{layer}", [P, NT, P]), k.sb(f"ffn_roots{layer}", [P, S])
        made = {}
        for t in range(NT):
            v = V.done(V.beside(norm.mark).tensor_scalar(diagonal[:, t, :], k.ident, norm.roots[:, t:t + 1], None, ALU.mult))

        def spread():
            bank = k.small.take()
            k.pe.wait(v, *bank.free)
            m = k.pe.done(T.matmul(bank.t[:, 0:S], k.ones, diagonal[:, :, :].rearrange("p t n -> p (t n)"), start=True, stop=True))
            made["roots"] = V.done(V.beside(m).tensor_copy(roots[:, :], bank.t[:, 0:S]))
            bank.free = (made["roots"],)
        k.late.append(spread)
        two_roots = roots[:, :].unsqueeze(1).broadcast_to((P, 2, S))

        def gate_to(slot, b, bank, m):
            at, ps = slot.t[:, 2 * b:2 * b + 2, :], bank.t[:, :].rearrange("p (k n) -> p k n", n=S)
            v = V.done(V.after(m, *slot.free).tensor_tensor(at, ps, two_roots, ALU.mult))
            bank.free = (v,)
            slot.gated = A.done(A.beside(v).activation(at, at, ACT.Silu))

        def up_to(slot, b, f, bank, m):
            at, ps = slot.t[:, 2 * b:2 * b + 2, :], bank.t[:, :].rearrange("p (k n) -> p k n", n=S)
            v = V.done(V.beside(m, slot.gated).tensor_tensor(at, at, ps, ALU.mult))
            bank.free = (v,)
            v = k.split_operand(at, v, hidden.high[:, f:f + 2, :], hidden.low[:, f:f + 2, :])
            slot.free = (v,)
            hidden.ready[f // CK] = (v,)
        wide = [(i // 2, S * (i % 2), None, P * i, P) for i in range(CK)]
        full = FF // CN
        for n in range(full):
            slot = mids.take()

            def gates(banks, m):
                for b in range(2):
                    gate_to(slot, b, banks[b], m)

            def ups(banks, m):
                for b in range(2):
                    up_to(slot, b, CK * n + 2 * b, banks[b], m)
            if n == 0:
                seen = []

                def gates_then_ups(banks, m):
                    (ups if seen else gates)(banks, m)
                    seen.append(m)
                drain(k.block(k.H, KT, wide + [(b + 2, *item) for b, *item in wide], gates_then_ups,
                              [(first, banks, first > 0) for first in range(0, KT, CK) for banks in ((0, 1), (2, 3))]))
            else:
                drain(k.block(k.H, KT, wide, gates))
                drain(k.block(k.H, KT, wide, ups))
            next(beside, None)
        slot = mids.take()

        def last(banks, m):
            gate_to(slot, 0, banks[0], m)
            up_to(slot, 0, CK * full, banks[1], m)
        drain(k.block(k.H, KT, wide, last))
        k.next_norm = following()
        for n in range(D // CN):
            drain(k.columns(hidden, FT, lambda t, bank, m: k.add_to_x(n, t, bank, m, norm.root(t))))
            if n == 0:
                ended = k.so_far()
        k.hand_over(ended + [k.pe.last])
    k.phase = k.ctx


def conv_layer(k, w, mem, kv, made):
    V, A, T = k.vec, k.act, k.nc.tensor
    with ExitStack() as phase:
        k.phase = phase
        pad = TAPS - 1
        u, y = k.sb("conv_in", [P, KT, pad + S]), k.sb("conv_out", [P, KT, S])
        taps = k.sb("taps", [P, KT, TAPS])
        tap_rows = k.sb("tap_rows", [TAPS, D])
        sig = k.ring("glu", 2, [P, 2, S])
        diagonals = k.ring("diagonal", 4, [P, 4, P])
        mean_of, diag_root = k.sb("mean_of", [P, P]), k.sb("diag_root", [P, NT, P])
        variance = k.sb("ln_variance", [P, S])
        taps_mark = k.side.start("taps", tap_rows[:, :], w["conv_w_dw_2"][0])
        scaled = []
        for t in range(NT):
            root = k.two_roots[:, NT + t:NT + t + 1]
            a = A.done(A.beside(k.roots_mark).activation(k.HN[:, t, 0:CN], k.HN[:, t, 0:CN], ACT.Copy, scale=root))
            v = V.done(V.beside(k.roots_mark).tensor_scalar(k.HN[:, t, CN:D], k.HN[:, t, CN:D], root, None, ALU.mult))
            scaled.append((a, v))
        fill = memory_keys(k, 0, mem, *kv, made)
        for _ in range(2):
            next(fill)
        for t, (a, v) in enumerate(scaled):
            k.transposed(k.HN[:, t, :], [P * i for i in range(CK)], k.H, 0, t, a)
            k.transposed(k.HN[:, t, :], [CN + P * i for i in range(CK)], k.H, CK, t, v)
        k.hn_free = (k.pe.last,)
        for t in range(NT):
            V.done(V.beside().tensor_scalar(k.X[:, t, :], k.X[:, t, :], k.two_roots[:, t:t + 1], None, ALU.mult))
        b2_mark = k.load_gain("conv_b_pw2_2", 0, 1)
        k.next_norm = Norm(k, "norm_mem_2", 0)
        V.done(V.after().memset(u[:, :, 0:pad], 0.0))
        mean_mark = V.done(V.after().memset(mean_of[:, :], 1.0 / D))
        for t in range(NT):
            V.done(V.after(b2_mark).tensor_tensor(k.X[:, t, :], k.X[:, t, :], k.G[1].t[:, :], ALU.add))

        ready, marks = {}, {}

        def tap_steps(tiles):
            for tap in range(TAPS):
                for i, f in enumerate(tiles):
                    if tap > 0 and i % 2 == 0:
                        V.wait(marks[tiles[min(i + 1, len(tiles) - 1)]])
                    src, wt = u[:, f, tap:tap + S], taps[:, f, tap:tap + 1]
                    if tap == 0:
                        marks[f] = V.done(V.beside(ready[f]).tensor_scalar(y[:, f, :], src, wt, k.vcol["b_dw"][:, f:f + 1], ALU.mult, ALU.add))
                    else:
                        marks[f] = V.done(V.beside(marks[f]).scalar_tensor_tensor(y[:, f, :], src, wt, y[:, f, :], ALU.mult, ALU.add))
                    yield

        def tap_products(tiles):
            groups = [(f, range(g, min(g + 4, TAPS))) for f in tiles for g in range(0, TAPS, 4)]
            made_d = {}

            def diagonal(n):
                if n < len(groups):
                    f, group = groups[n]
                    slot = diagonals.take()
                    A.wait(*slot.free)
                    for i, tap in enumerate(group):
                        a = A.done(A.beside().activation(slot.t[:, i, :], k.ident, ACT.Copy, scale=taps[:, f, tap:tap + 1]))
                    made_d[n] = slot, a
            for n in range(3):
                diagonal(n)
            yield
            for n, (f, group) in enumerate(groups):
                slot, a = made_d[n]
                if group[0] == 0:
                    bank = k.small.take()
                    k.pe.wait(ready[f], *bank.free)
                k.pe.wait(a)
                for i, tap in enumerate(group):
                    mm = T.matmul(bank.t[:, 0:S], slot.t[:, i, :], u[:, f, tap:tap + S], start=tap == 0, stop=tap == TAPS - 1)
                m = k.pe.done(mm)
                slot.free = (m,)
                diagonal(n + 3)
                if group[-1] == TAPS - 1:
                    marks[f] = V.done(V.beside(m).tensor_scalar(y[:, f, :], bank.t[:, 0:S], k.vcol["b_dw"][:, f:f + 1], None, ALU.add))
                    bank.free = (marks[f],)
                if n % 2:
                    yield

        def chain(*gens):
            for g in gens:
                yield from g

        def steps(gen, n):
            for _ in range(n):
                next(gen, None)
        on_pe = 3
        vec_taps = chain(tap_steps([0, 1]), tap_steps(list(range(2, KT - on_pe))))
        pe_taps = tap_products(list(range(KT - on_pe, KT)))
        for n in range(KT // 2):
            def evacuate(banks, m):
                slot = sig.take()
                for i in range(2):
                    f = 2 * n + i
                    a = A.done(A.after(m, *slot.free).activation(slot.t[:, i, :], banks[1].t[:, i * S:(i + 1) * S], ACT.Sigmoid,
                                                                bias=k.vcol["b_pw1"][:, KT + f:KT + f + 1]))
                for i in range(2):
                    f = 2 * n + i
                    v = V.done(V.beside(m, a).scalar_tensor_tensor(u[:, f, pad:pad + S], banks[0].t[:, i * S:(i + 1) * S],
                                                                   k.vcol["b_pw1"][:, f:f + 1], slot.t[:, i, :], ALU.add, ALU.mult))
                    ready[f] = v
                banks[1].free, banks[0].free, slot.free = (a,), (v,), (v,)
            for _ in k.block(k.H, KT, [(0, 0, None, 0, P), (0, S, None, P, P), (1, 0, None, 2 * P, P), (1, S, None, 3 * P, P)], evacuate):
                if n:
                    steps(vec_taps, 8)
            if n == 0:
                for g in range(0, KT, 4):
                    bank = k.small.take()
                    k.pe.wait(taps_mark, *bank.free)
                    for i in range(4):
                        tr = T.transpose(bank.t[:, i * P:i * P + TAPS], tap_rows[:, (g + i) * P:(g + i + 1) * P], k.ident[0:TAPS, 0:TAPS])
                    m = k.pe.done(tr)
                    v = V.done(V.after(m).tensor_copy(taps[:, g:g + 4, :], bank.t[:, :].rearrange("p (k n) -> p k n", n=P)[:, :, 0:TAPS]))
                    bank.free = (v,)
                    taps_ready = v
                A.wait(taps_ready)
            if n == KT // 2 - 2:
                next(pe_taps)
        rounds = on_pe * (1 + TAPS // 8)
        for i in range(rounds):
            next(pe_taps, None)
            if i % 6 == 1:
                next(fill, None)
            steps(vec_taps, 10)
        drain(pe_taps)
        drain(vec_taps)
        next(fill, None)

        halves = [slice(h * CK, (h + 1) * CK) for h in range(2)]
        order = [*range(KT - on_pe, KT), *range(KT - on_pe)]
        bank = k.small.take()
        k.pe.wait(mean_mark, *bank.free)
        for f in order:
            k.pe.wait(marks[f])
            mm = T.matmul(bank.t[:, 0:S], mean_of[:, :], y[:, f, :], start=f == order[0], stop=f == order[-1])
        m = k.pe.done(mm)
        sq, sq_marks = k.HN[:, :, :].rearrange("p t (k n) -> p (t k) n", n=S), []
        A.wait(*k.hn_free)
        for at in halves:
            v = V.done(V.beside(m).tensor_tensor(y[:, at, :], y[:, at, :], bank.t[:, 0:S].unsqueeze(1).broadcast_to((P, CK, S)), ALU.subtract))
            sq_marks.append(A.done(A.beside(v).activation(sq[:, at, :], y[:, at, :], ACT.Square)))
        bank.free = (v,)
        next(fill, None)
        bank = k.small.take()
        k.pe.wait(*bank.free)
        for f in range(KT):
            k.pe.wait(sq_marks[f // CK])
            mm = T.matmul(bank.t[:, 0:S], mean_of[:, :], sq[:, f, :], start=f == 0, stop=f == KT - 1)
        m = k.pe.done(mm)
        k.hn_free = (m,)
        v = V.done(V.beside(m).tensor_scalar(variance[:, :], bank.t[:, 0:S], LN_EPS, None, ALU.add))
        bank.free = (v,)
        bank, root = k.small.take(), k.stat(NT)
        k.pe.wait(v, *bank.free)
        for t in range(NT):
            mm = T.matmul(bank.t[:, t:t + 1], variance[:, t * P:(t + 1) * P], k.ident[:, 0:1], start=t == 0, stop=True, skip_group_check=True)
        m = k.pe.done(mm)
        next(fill, None)
        v = V.done(V.beside(m).tensor_copy(root, bank.t[:, 0:NT]))
        bank.free = (v,)
        p = k.pool.done(k.pool.after(v).tensor_tensor(root, root, k.half[:, 0:NT], ALU.pow))
        for t in range(NT):
            v = V.done(V.beside(p).tensor_scalar(diag_root[:, t, :], k.ident, root[:, t:t + 1], None, ALU.mult))
        bank = k.small.take()
        k.pe.wait(v, *bank.free)
        m = k.pe.done(T.matmul(bank.t[:, 0:S], k.ones, diag_root[:, :, :].rearrange("p t n -> p (t n)"), start=True, stop=True))
        wide_root = bank.t[:, 0:S].unsqueeze(1).broadcast_to((P, CK, S))
        o = k.H
        for h, at in enumerate(halves):
            v = V.done(V.beside(m).tensor_tensor(y[:, at, :], y[:, at, :], wide_root, ALU.mult))
            A.wait(v)
            for f in range(h * CK, (h + 1) * CK):
                a = A.done(A.beside().activation(y[:, f, :], y[:, f, :], ACT.Silu, scale=k.vcol["ln_g"][:, f:f + 1], bias=k.vcol["ln_b"][:, f:f + 1]))
            halves[h] = (at, a)
        bank.free = (v,)
        for h, (at, a) in enumerate(halves):
            v = V.done(V.beside(a, *o.free[h]).tensor_copy(o.high[:, at, :], y[:, at, :]))
            o.ready[h] = (V.done(V.after(v).tensor_tensor(o.low[:, at, :], y[:, at, :], o.high[:, at, :].bitcast(F32), ALU.subtract)),)
        drain(fill)
        ended = k.so_far()
        drain(k.square(o, k.add_to_x))
        k.hand_over(ended)
    k.phase = k.ctx


def lambda_and_rope(k, w, made):
    V, A, n = k.vec, k.act, ROT // 2
    cos, sin = k.stat(NT * n), k.stat(NT * n)
    raw, pos = k.sb("positions", [P, NT], I32), k.stat(NT)
    lrow = k.sb("lambda_rows", [P, 4, HD])
    with k.nc.allow_non_contiguous_dma(reason="256 numbers, a row of partitions each"):
        positions_loaded = k.side.start("positions", raw[:, :], w["positions_2"][0].rearrange("(t p) -> p t", p=P))
    for i, name in enumerate(("q1", "k1", "q2", "k2")):
        rows_loaded = k.row("lambda", lrow[:, i, :], w[f"diff_lambda_{name}_2"][0])
    yield
    V.done(V.after(positions_loaded).tensor_copy(pos, raw[:, :]))
    step = 1.5 * 2.0 ** 23
    ang, turns = k.stat(NT * n), k.stat(NT * n)
    for t in range(NT):
        V.done(V.after().tensor_scalar(ang[:, t * n:(t + 1) * n], k.invfreq, pos[:, t:t + 1], None, ALU.mult))
    c1 = 6.28125
    c2 = round((TWO_PI - c1) * 2.0 ** 20) / 2.0 ** 20
    c3 = TWO_PI - c1 - c2
    for dst, quarter in ((cos, 0.25), (sin, 0.0)):
        r = k.stat(NT * n)
        V.done(V.after().tensor_scalar(turns, ang, 1.0 / TWO_PI, quarter, ALU.mult, ALU.add))
        V.done(V.after().tensor_scalar(turns, turns, step, None, ALU.add))
        V.done(V.after().tensor_scalar(turns, turns, step, None, ALU.subtract))
        V.done(V.after().scalar_tensor_tensor(r, turns, -c1, ang, ALU.mult, ALU.add))
        V.done(V.after().scalar_tensor_tensor(r, turns, -c2, r, ALU.mult, ALU.add))
        V.done(V.after().scalar_tensor_tensor(r, turns, -c3, r, ALU.mult, ALU.add))
        V.done(V.after().tensor_scalar(r, r, quarter * TWO_PI, 3.1415925, ALU.add, ALU.min))
        v = V.done(V.after().tensor_scalar(r, r, -3.1415925, None, ALU.max))
        made["rope_mark"] = A.done(A.beside(v).activation(dst, r, ACT.Sin))
    yield
    e, neg_lam = k.stat(2), k.stat(1)
    V.done(V.after(rows_loaded).tensor_tensor(lrow[:, 0, :], lrow[:, 0, :], lrow[:, 1, :], ALU.mult))
    V.done(V.after().tensor_tensor(lrow[:, 1, :], lrow[:, 2, :], lrow[:, 3, :], ALU.mult))
    v = V.done(V.after().tensor_reduce(e, lrow[:, 0:2, :], AX.X, ALU.add))
    a = A.done(A.beside(v).activation(e, e, ACT.Exp))
    yield
    V.done(V.beside(a).tensor_tensor(neg_lam, e[:, 1:2], e[:, 0:1], ALU.subtract))
    V.done(V.after(made["rope_mark"]).tensor_scalar(neg_lam, neg_lam, LAMBDA_INIT, None, ALU.subtract))
    made["rope"] = cos, sin, neg_lam


def differential_layer(k, w, mem, kv, made):
    V, A, T = k.vec, k.act, k.nc.tensor
    with ExitStack() as phase:
        k.phase = phase
        norm = k.next_norm
        vals, out = k.sb("vals", [P, NT, D]), k.sb("attended", [P, NT, D])
        tok = out
        qt, kt_ = k.sb("q_t", [P, DH, S]), k.sb("k_t", [P, DH, S])
        k.rows_ring = k.ring("drows", 4, [P, 512])
        k.turned = k.ring("dturned", 2, [P, 512])
        cos, sin, neg_lam = made["rope"]
        tok_free = [()]
        parts_ring = k.ring("rotated", 2, [P, 4 * DH * ROT // 2])

        def rotate(t, n, mark):
            r, nh = ROT // 2, DH
            heads = tok[:, t, n * CN:(n + 1) * CN].rearrange("p (h d) -> p h d", d=HD)
            r1, r2 = heads[:, :, 0:r], heads[:, :, r:2 * r]
            c = cos[:, t * r:(t + 1) * r].unsqueeze(1).broadcast_to((P, nh, r))
            s = sin[:, t * r:(t + 1) * r].unsqueeze(1).broadcast_to((P, nh, r))
            slot = parts_ring.take()
            q4 = slot.t[:, :].rearrange("p (f h d) -> p f h d", f=4, d=r)
            V.done(V.after(mark, *slot.free).tensor_tensor(q4[:, 0], r1, c, ALU.mult))
            V.done(V.beside().tensor_tensor(q4[:, 1], r2, s, ALU.mult))
            V.done(V.beside().tensor_tensor(q4[:, 2], r1, s, ALU.mult))
            V.done(V.beside().tensor_tensor(q4[:, 3], r2, c, ALU.mult))
            V.done(V.after().tensor_tensor(r1, q4[:, 0], q4[:, 1], ALU.subtract))
            v = V.done(V.beside().tensor_tensor(r2, q4[:, 2], q4[:, 3], ALU.add))
            slot.free = (v,)
            return v

        def to_heads(dst, name):
            def evacuate(n, t, bank, m):
                A.wait(*tok_free[0])
                k.copy_to(lambda t: tok[:, t, n * CN:(n + 1) * CN], scale_of=norm.root)(t, bank, m)
                v = rotate(t, n, k.copied)

                def turn():
                    g, bank = n * CK, k.small.take()
                    k.pe.wait(v, *bank.free)
                    for i in range(4):
                        tr = T.transpose(bank.t[:, i * P:(i + 1) * P], tok[:, t, (g + i) * P:(g + i + 1) * P], k.ident)
                    m = k.pe.done(tr)
                    a = A.done(A.beside(m).activation(dst[:, g:g + 4, t * P:(t + 1) * P],
                                                      bank.t[:, :].rearrange("p (k n) -> p k n", n=P), ACT.Copy))
                    bank.free = (a,)
                    made[name] = a
                    if n == 1 and t == 1:
                        tok_free[0] = (m,)
                k.late.append(turn)
            return evacuate
        drain(k.square(k.H, to_heads(kt_, "k")))
        q_norm = Norm(k, "norm_mix_2", 1, 1)

        def to_vals(n, t, bank, m):
            k.copy_to(lambda t: vals[:, t, n * CN:(n + 1) * CN], scale_of=norm.root)(t, bank, m)
            made["v"] = k.copied
            if t == 1:
                for tt in range(NT):
                    q_norm.take(n, tt, None, squares=False)
        drain(k.square(k.H, to_vals))
        to_q = to_heads(qt, "q")

        def queries(n):
            return k.columns(k.H, KT, lambda t, bank, m: to_q(n, t, bank, m))

        def fill():
            yield from queries(1)
            yield from memory_keys(k, 1, mem, *kv, made)
            project = k.square(k.H, k.add_to_x)
            for half in range(2):
                while ("half", half) not in made:
                    yield
                next(project)
                yield
                next(project)
                yield
            drain(project)
        filling = fill()
        drain(queries(0))
        next(filling)
        k.pe.wait(made["k"], made["v"])
        scale = HD ** -0.5
        causal = k.causal

        def group(heads, t):
            nh, nk = len(heads), P * (t + 1)
            parts = []
            for c in range(2):
                r = slice(c * HD, (c + 1) * HD)
                bank, slot = k.small.take(), k.rows_ring.take()
                k.pe.wait(made["q"], *bank.free)
                for i, h in enumerate(heads):
                    mm = T.matmul(bank.t[:, i * nk:(i + 1) * nk], qt[r, h, t * P:(t + 1) * P], kt_[r, h, 0:nk],
                                  start=i == 0, stop=True, skip_group_check=True)
                m = k.pe.done(mm)
                s = slot.t[:, :].rearrange("p (h n) -> p h n", n=nk)
                mask = causal[:, 2 * P - nk:2 * P].unsqueeze(1).broadcast_to((P, nh, nk))
                top, neg, sums = k.stat(nh), k.stat(nh), k.stat(nh)
                v = V.done(V.after(m, *slot.free).tensor_tensor(s, bank.t[:, :].rearrange("p (h n) -> p h n", n=nk), mask, ALU.add))
                bank.free = (v,)
                V.done(V.after().tensor_reduce(top, s, AX.X, ALU.max))
                v = V.done(V.after().tensor_scalar(neg, top, -scale, None, ALU.mult))
                A.wait(v)
                for i in range(nh):
                    a = A.done(A.beside().activation(s[:, i, :], s[:, i, :], ACT.Exp, bias=neg[:, i:i + 1], scale=scale, accum_out=sums[:, i:i + 1]))
                parts.append((slot, s, sums, a))
            yield
            (slot0, s0, sum0, _), (slot1, s1, sum1, a) = parts
            V.done(V.after(a).reciprocal(sum1, sum1))
            V.done(V.after().scalar_tensor_tensor(sum1, sum0, neg_lam, sum1, ALU.mult, ALU.mult))
            V.done(V.after().reciprocal(sum0, sum0))
            for i in range(nh):
                v = V.done(V.beside().scalar_tensor_tensor(s0[:, i, :], s1[:, i, :], sum1[:, i:i + 1], s0[:, i, :], ALU.mult, ALU.add))
            slot1.free = (v,)
            yield
            turned, tm = k.turn([s0[:, i, j * P:(j + 1) * P] for i in range(nh) for j in range(t + 1)], v, slot0)
            yield
            bank = k.small.take()
            k.pe.wait(tm, *bank.free)
            for i, h in enumerate(heads):
                for j in range(t + 1):
                    b = i * (t + 1) + j
                    mm = T.matmul(bank.t[:, i * P:(i + 1) * P], turned.t[:, b * P:(b + 1) * P], vals[:, j, h * P:(h + 1) * P],
                                  start=b == 0, stop=True, skip_group_check=True)
            m = k.pe.done(mm)
            turned.free = (m,)
            A.wait(m)
            for i, h in enumerate(heads):
                a = A.done(A.beside().activation(out[:, t, h * P:(h + 1) * P], bank.t[:, i * P:(i + 1) * P], ACT.Copy, scale=sum0[:, i:i + 1]))
            bank.free = (a,)
            made["out"] = a
            made["groups"] += 1

        def finish_half(half):
            hs, at = DH // 2, slice(half * CN, (half + 1) * CN)
            roots, turns = [], []
            while made["groups"] < 3 * (half + 1):
                yield
            for t in range(NT):
                sums, slot = k.stat(hs), k.rows_ring.take()
                V.done(V.after(made["out"], *slot.free).tensor_tensor(slot.t[:, :], out[:, t, at], out[:, t, at], ALU.mult))
                v = V.done(V.after().tensor_reduce(sums, slot.t[:, :].rearrange("p (h d) -> p h d", d=P), AX.X, ALU.add))
                slot.free = (v,)
                roots.append(k.inverse_root(sums, P, 1e-5, v, 1.0 - LAMBDA_INIT))
            yield
            for t, (r, m) in enumerate(roots):
                o_t = out[:, t, at].rearrange("p (h d) -> p h d", d=P)
                turns.append(V.done(V.beside(m).tensor_tensor(o_t, o_t, r.unsqueeze(2).broadcast_to((P, hs, P)), ALU.mult)))
            yield
            for t, v in enumerate(turns):
                k.transposed(out[:, t, :], [half * CN + P * i for i in range(CK)], k.H, half * CK, t, v, scale=k.vcol["subln_g"])
            made["half", half], made["turned"] = True, k.so_far()

        def half_groups(h0):
            return [group([h0, h0 + 1], 1), group([h0 + 2, h0 + 3], 1), group([h0, h0 + 1, h0 + 2, h0 + 3], 0)]

        made["groups"] = 0
        k.next_norm = Norm(k, "norm_mem_2", 1)
        k.run(half_groups(0) + half_groups(4) + [finish_half(0), finish_half(1)], filling, 4)
        k.hand_over(made["turned"] + [k.pe.last])
    k.phase = k.ctx


def chunks(w, tiles, cols):
    view = w.rearrange("(k p) n -> p k n", p=P)
    return [([(view[:, f:min(f + CK, tiles), c:c + n], n) for c, n in cols], min(CK, tiles - f)) for f in range(0, tiles, CK)]


def weight_plan(w):
    plan = []

    def add(m, *blocks, tiles=KT):
        for cols in blocks:
            plan.extend(chunks(m, tiles, cols))

    def square(m):
        for f in range(0, KT, CK):
            for c in range(0, D, CN):
                plan.append(chunks(m, KT, [(c, CN)])[f // CK])

    def even(m, tiles=KT):
        add(m, *[[(c, CN)] for c in range(0, D, CN)], tiles=tiles)

    ada, w_in = w["w_ada"][0], w["w_in"][0]
    add(ada, *[[(c, CN)] for c in (D, 0, D + CN, CN, 2 * D, 2 * D + CN)])
    add(w_in, [(W_D_Q, 512)], [(W_D_V, 512)], [(W_C_Q, 512)], [(W_C_V, 512)])
    add(w_in, [(W_B_K, 512)], [(W_A_Z, 512)])

    def merge(i):
        for c in range(0, D, CN):
            add(w["w_merge"][0, i], [(c, CN)])
            add(w["w_br"][0, i], [(c, CN)], tiles=BW // P)
    merge(3)
    add(w_in, [(W_A_KV + 2 * HD, 268)], [(W_A_Q, 384)])
    merge(2)
    merge(1)
    merge(0)
    square(w["w_out"][0])
    add(w["mem_w_k_2"][0], [(0, CN)])

    pw1 = w["conv_w_pw1_2"][0]
    add(pw1, *[[(c, S), (D + c, S)] for c in range(0, D, S)])

    def memory(layer, done=0):
        for c in range(done, D, CN):
            add(w["mem_w_k_2"][layer], [(c, CN)])
        even(w["mem_w_v_2"][layer])

    def memory_use(layer):
        even(w["mem_w_q_2"][layer])
        square(w["mem_w_o_2"][layer])

    def feed(layer):
        g, u, d = w["ffn_w_gate_2"][layer], w["ffn_w_up_2"][layer], w["ffn_w_down_2"][layer]
        for f in range(2):
            plan.extend(chunks(m, KT, [(0, CN)])[f] for m in (g, u))
        for c in range(CN, FF - CN + 1, CN):
            add(g, [(c, CN)])
            add(u, [(c, CN)])
        c = FF // CN * CN
        gv, uv = (m.rearrange("(k p) n -> p k n", p=P) for m in (g, u))
        for f in range(0, KT, CK):
            plan.append(([(gv[:, f:f + CK, c:FF], FF - c), (uv[:, f:f + CK, c:FF], FF - c)], CK))
        even(d, tiles=FT)
    memory(0, CN)
    square(w["conv_w_pw2_2"][0])
    memory_use(0)
    feed(0)
    square(w["w_k_shared_2"])
    square(w["w_v_shared_2"])
    even(w["diff_w_q_2"][0])
    memory(1)
    square(w["diff_w_o_2"][0])
    memory_use(1)
    feed(1)
    return plan


def build(nc, w, out):
    with ExitStack() as ctx:
        k = Kernel(nc, ctx, w)
        common = k.sb("common", [P, COMMON_W])
        common_mark = k.stream.start("common", common[:, :], w["common_constants"])

        def const(name):
            at, n = COMMON[name]
            return common[:, at:at + n]
        k.ident, k.ones, k.causal, k.invfreq, k.half = (const(n) for n in ("ident", "ones", "causal", "invfreq", "half"))
        k.X, k.HN = k.sb("X", [P, NT, D]), k.sb("HN", [P, NT, D])
        k.G = [Slot(k.sb(f"gain{i}", [P, D])) for i in range(2)]
        k.H = Operand(*k.pair("H", KT))
        k.weights = Weights(k, weight_plan(w))
        k.next_norm = None
        k.hn_free, made = (), {}
        k.vector_rows, k.vector_cols = k.sb("vector_rows", [N_VECTOR_ROWS, P]), k.sb("vector_cols", [P, N_VECTOR_ROWS])
        for l in (k.pe, k.pool, k.vec):
            l.wait(common_mark)

        mem = first_block(k, w)
        bank = k.small.take()
        k.pe.wait(k.vectors_loaded)
        m = k.pe.done(nc.tensor.transpose(bank.t[:, 0:N_VECTOR_ROWS], k.vector_rows[:, :], k.ident[0:N_VECTOR_ROWS, 0:N_VECTOR_ROWS]))
        columns = k.vec.done(k.vec.after(m).tensor_copy(k.vector_cols[:, :], bank.t[:, 0:N_VECTOR_ROWS]))
        bank.free = (columns,)
        k.act.wait(columns)
        with ExitStack() as phase:
            k.phase = phase
            k.junk = k.sb("junk", [P, CN])
            for layer in range(2):
                with ExitStack() as kv_phase:
                    k.phase = kv_phase
                    kv = k.sb(f"mem_keys{layer}", [P, KT, S]), k.sb(f"mem_values{layer}", [P, NT, D])
                    (conv_layer, differential_layer)[layer](k, w, mem, kv, made)
                    with ExitStack() as inner:
                        k.phase = inner
                        memory_attention(k, layer, *kv, made)
                        k.hand_over(made["attended"] + [k.pe.last])
                if layer == 0:
                    feed_forward(k, 0, lambda_and_rope(k, w, made), lambda: Norm(k, "kv_norm_2", None))
                else:
                    feed_forward(k, 1, iter(()), lambda: Norm(k, "norm_final_2", None, transposed=False))
                    last = k.next_norm
        for t in range(NT):
            root, hn = last.root(t), k.HN[:, t, :]
            v = k.vec.done(k.vec.beside().tensor_scalar(hn[:, 0:CN], hn[:, 0:CN], root, None, ALU.mult))
            a = k.act.done(k.act.after(k.vec.last).activation(hn[:, CN:D], hn[:, CN:D], ACT.Copy, scale=root))
            stored = k.stream.start("result", out[0, t * P:(t + 1) * P, :], hn, v, a)
        k.stream.lane.wait(stored)


_INS = ["x", "c", "w_ada", "b_ada", "norm_g", "w_in", "cmp_pos", "cmp_w1", "cmp_w2", "sink", "w_merge", "w_br", "w_out",
        "final_g", "mem_2", "positions_2", "norm_mix_2", "norm_mem_2", "norm_ffn_2", "norm_final_2", "conv_w_pw1_2",
        "conv_b_pw1_2", "conv_w_dw_2", "conv_b_dw_2", "conv_ln_g_2", "conv_ln_b_2", "conv_w_pw2_2", "conv_b_pw2_2",
        "kv_norm_2", "w_k_shared_2", "w_v_shared_2", "diff_w_q_2", "diff_lambda_q1_2", "diff_lambda_k1_2",
        "diff_lambda_q2_2", "diff_lambda_k2_2", "diff_subln_g_2", "diff_w_o_2", "mem_w_q_2", "mem_w_k_2", "mem_w_v_2",
        "mem_w_o_2", "ffn_w_gate_2", "ffn_w_up_2", "ffn_w_down_2"]


def kernel(**inputs):
    import concourse.bacc as bacc
    from concourse.bass_utils import run_bass_kernel_spmd

    nc = bacc.Bacc("TRN2", target_bir_lowering=False, num_devices=1)
    common, first = constants()
    arrays = {name: np.ascontiguousarray(inputs[name]) for name in _INS}
    arrays.update(common_constants=common, first_constants=first)
    arrays = {f"in_{name}": a for name, a in arrays.items()}
    w = {name[3:]: nc.dram_tensor(name, a.shape, mybir.dt.from_np(a.dtype), kind="ExternalInput").ap()
         for name, a in arrays.items()}
    out = nc.dram_tensor("result", (1, S, D), F32, kind="ExternalOutput").ap()
    build(nc, w, out)
    r = run_bass_kernel_spmd(nc, [arrays], core_ids=[0])
    return r.results[0]["result"]
```
